# Optimizing a Trainium2 kernel written in Bass

```python
import math
import jax
import jax.numpy as jnp
from jax import lax
import numpy as np

D_MODEL = 1024
BATCH = 1
SEQ = 256
DEPTH = 2

A_HEADS = 8
A_HEAD_DIM = 64
A_WIDTH = A_HEADS * A_HEAD_DIM
MOBA_BLOCK = 256
MOBA_TOPK = 3
MOBA_Q_CHUNK = 64
REL_BUCKETS = 32
REL_MAX_DIST = 128
S5_WIDTH = D_MODEL - A_WIDTH
S5_GROUP = 16
S5_GROUPS = S5_WIDTH // S5_GROUP
S5_STATE = 64
C_HEADS = 8
C_HEAD_DIM = D_MODEL // C_HEADS
C_WIDTH = C_HEADS * C_HEAD_DIM
C_CONV = 4
C_CHUNK = 64
D_FF = 4 * D_MODEL
N_EVEN = (DEPTH + 1) // 2
N_ODD = DEPTH // 2
DN_ALPHA = (2 * DEPTH) ** 0.25
DN_BETA = (8 * DEPTH) ** -0.25
LN_EPS = 1e-5
RMS_EPS = 1e-6
L2_EPS = 1e-6
NEG_INF = -1e30

kernel_name = 'moba_s5_gated_deltanet_deepnorm_hybrid'

def _layer_norm(x, g, b):
    xf = x.astype(jnp.float32)
    mu = jnp.mean(xf, axis=-1, keepdims=True)
    var = jnp.mean(jnp.square(xf - mu), axis=-1, keepdims=True)
    y = (xf - mu) * lax.rsqrt(var + LN_EPS) * g.astype(jnp.float32) + b.astype(jnp.float32)
    return y.astype(x.dtype)

def _t5_bucket(dist):
    max_exact = REL_BUCKETS // 2
    n = jnp.maximum(dist, 0)
    nf = jnp.maximum(n, 1).astype(jnp.float32)
    large = max_exact + (jnp.log(nf / max_exact) / math.log(REL_MAX_DIST / max_exact)
                         * (REL_BUCKETS - max_exact)).astype(jnp.int32)
    large = jnp.minimum(large, REL_BUCKETS - 1)
    return jnp.where(n < max_exact, n, large)

def _moba_attention(q, k, v, rel_table):
    b, s, h, d = q.shape
    nb = -(-s // MOBA_BLOCK)
    s_pad = nb * MOBA_BLOCK
    pad = ((0, 0), (0, 0), (0, s_pad - s), (0, 0))
    q = q.transpose(0, 2, 1, 3) * (d ** -0.5)
    k_blocks = jnp.pad(k.transpose(0, 2, 1, 3), pad).reshape(b, h, nb, MOBA_BLOCK, d)
    v_blocks = jnp.pad(v.transpose(0, 2, 1, 3), pad).reshape(b, h, nb, MOBA_BLOCK, d)
    k_mean = jnp.mean(k_blocks, axis=3)
    gate = jnp.einsum('bhsd,bhnd->bhsn', q, k_mean).astype(jnp.float32)
    q_blk = jnp.arange(s) // MOBA_BLOCK
    past = jnp.arange(nb)[None, :] < q_blk[:, None]
    gate = jnp.where(past, gate, NEG_INF)
    n_sel = min(MOBA_TOPK, nb)
    _, sel = lax.top_k(gate, n_sel)

    qc = MOBA_Q_CHUNK
    nc = s // qc
    q_ch = q.reshape(b, h, nc, qc, d).transpose(2, 0, 1, 3, 4)
    sel_ch = sel.reshape(b, h, nc, qc, n_sel).transpose(2, 0, 1, 3, 4)
    b_idx = jnp.arange(b)[:, None, None, None]
    h_idx = jnp.arange(h)[None, :, None, None]
    h_idx5 = jnp.arange(h)[None, :, None, None, None]
    table_t = rel_table.T
    offs = jnp.arange(MOBA_BLOCK)

    def chunk_attn(args):
        c, q_c, sel_c = args
        q_pos = c * qc + jnp.arange(qc)
        blk = (c * qc) // MOBA_BLOCK
        k_own = lax.dynamic_index_in_dim(k_blocks, blk, axis=2, keepdims=False)
        v_own = lax.dynamic_index_in_dim(v_blocks, blk, axis=2, keepdims=False)
        dist_own = q_pos[:, None] - (blk * MOBA_BLOCK + offs)[None, :]
        logit_own = (jnp.einsum('bhqd,bhkd->bhqk', q_c, k_own).astype(jnp.float32)
                     + table_t[:, _t5_bucket(dist_own)][None].astype(jnp.float32))
        logit_own = jnp.where(dist_own >= 0, logit_own, NEG_INF)
        k_sel = k_blocks[b_idx, h_idx, sel_c]
        v_sel = v_blocks[b_idx, h_idx, sel_c]
        dist_sel = q_pos[None, None, :, None, None] - (sel_c[..., None] * MOBA_BLOCK + offs)
        logit_sel = (jnp.einsum('bhqd,bhqnkd->bhqnk', q_c, k_sel).astype(jnp.float32)
                     + table_t[h_idx5, _t5_bucket(dist_sel)].astype(jnp.float32))
        valid = (sel_c < blk)[..., None]
        logit_sel = jnp.where(valid, logit_sel, NEG_INF)
        logits = jnp.concatenate([logit_own, logit_sel.reshape(b, h, qc, n_sel * MOBA_BLOCK)], axis=-1)
        p = jax.nn.softmax(logits, axis=-1).astype(v_blocks.dtype)
        p_own = p[..., :MOBA_BLOCK]
        p_sel = p[..., MOBA_BLOCK:].reshape(b, h, qc, n_sel, MOBA_BLOCK)
        return (jnp.einsum('bhqk,bhkd->bhqd', p_own, v_own)
                + jnp.einsum('bhqnk,bhqnkd->bhqd', p_sel, v_sel))

    out = lax.map(chunk_attn, (jnp.arange(nc), q_ch, sel_ch))
    return out.transpose(1, 0, 3, 2, 4).reshape(b, s, h * d)

def _complex_linear_combine(e1, e2):
    a1r, a1i, b1r, b1i = e1
    a2r, a2i, b2r, b2i = e2
    ar = a2r * a1r - a2i * a1i
    ai = a2r * a1i + a2i * a1r
    br = a2r * b1r - a2i * b1i + b2r
    bi = a2r * b1i + a2i * b1r + b2i
    return (ar, ai, br, bi)

def _s5_mixer(u, lam_re, lam_im, b_re, b_im, c_re, c_im, d_skip, log_dt, w_glu, b_glu):
    f32 = jnp.float32
    bsz, s, _ = u.shape
    uf = u.astype(f32)
    ug = uf.reshape(bsz, s, S5_GROUPS, S5_GROUP)
    lr = jnp.minimum(lam_re.astype(f32), -1e-4)
    li = lam_im.astype(f32)
    dt = jnp.exp(log_dt.astype(f32))[:, None]
    mag = jnp.exp(lr * dt)
    a_re = mag * jnp.cos(li * dt)
    a_im = mag * jnp.sin(li * dt)
    den = lr * lr + li * li
    coef_re = ((a_re - 1.0) * lr + a_im * li) / den
    coef_im = (a_im * lr - (a_re - 1.0) * li) / den
    br = b_re.astype(f32)
    bi = b_im.astype(f32)
    bb_re = coef_re[..., None] * br - coef_im[..., None] * bi
    bb_im = coef_re[..., None] * bi + coef_im[..., None] * br
    x_re = jnp.einsum('gph,bsgh->sbgp', bb_re, ug)
    x_im = jnp.einsum('gph,bsgh->sbgp', bb_im, ug)
    a_re_t = jnp.broadcast_to(a_re[None, None], (s, 1) + a_re.shape)
    a_im_t = jnp.broadcast_to(a_im[None, None], (s, 1) + a_im.shape)
    _, _, h_re, h_im = lax.associative_scan(_complex_linear_combine,
                                            (a_re_t, a_im_t, x_re, x_im), axis=0)
    y = (jnp.einsum('ghp,sbgp->bsgh', c_re.astype(f32), h_re)
         - jnp.einsum('ghp,sbgp->bsgh', c_im.astype(f32), h_im))
    y = y.reshape(bsz, s, S5_WIDTH) + d_skip.astype(f32) * uf
    g = jax.nn.gelu(y)
    out = g * jax.nn.sigmoid(g @ w_glu.astype(f32) + b_glu.astype(f32))
    return out.astype(u.dtype)

def _causal_depthwise_conv(x, w):
    kw = w.shape[0]
    return lax.conv_general_dilated(x, w[:, None, :].astype(x.dtype), window_strides=(1,),
                                    padding=[(kw - 1, 0)],
                                    dimension_numbers=('NWC', 'WIO', 'NWC'),
                                    feature_group_count=x.shape[-1])

def _l2norm(t):
    return t * lax.rsqrt(jnp.sum(t * t, axis=-1, keepdims=True) + L2_EPS)

def _gated_delta_rule(q, k, v, g, beta):
    b, s, h, dk = q.shape
    dv = v.shape[-1]
    c = C_CHUNK
    n = s // c

    def chunks(t):
        return t.reshape(b, n, c, h, -1).transpose(0, 3, 1, 2, 4)

    q = chunks(q) * (dk ** -0.5)
    k = chunks(k)
    v = chunks(v)
    beta = beta.reshape(b, n, c, h).transpose(0, 3, 1, 2)
    g = jnp.cumsum(g.reshape(b, n, c, h).transpose(0, 3, 1, 2), axis=-1)
    tril_incl = jnp.tril(jnp.ones((c, c), bool))
    tril_strict = jnp.tril(jnp.ones((c, c), bool), -1)
    diff = g[..., :, None] - g[..., None, :]
    decay = jnp.where(tril_incl, jnp.exp(jnp.where(tril_incl, diff, 0.0)), 0.0)
    k_beta = k * beta[..., None]
    v_beta = v * beta[..., None]
    lower = jnp.where(tril_strict, jnp.einsum('bhnid,bhnjd->bhnij', k_beta, k) * decay, 0.0)
    a_mat = lower + jnp.eye(c, dtype=jnp.float32)
    u = lax.linalg.triangular_solve(a_mat, v_beta, left_side=True, lower=True, unit_diagonal=True)
    w = lax.linalg.triangular_solve(a_mat, k_beta * jnp.exp(g)[..., None], left_side=True,
                                    lower=True, unit_diagonal=True)
    intra = jnp.einsum('bhnid,bhnjd->bhnij', q, k) * decay
    g_last = g[..., -1]
    q_dec = q * jnp.exp(g)[..., None]
    k_dec = k * jnp.exp(g_last[..., None] - g)[..., None]

    def step(state, xs):
        q_i, k_i, u_i, w_i, a_i, gl_i = xs
        v_new = u_i - jnp.einsum('bhcd,bhde->bhce', w_i, state)
        o = jnp.einsum('bhcd,bhde->bhce', q_i, state) + jnp.einsum('bhij,bhje->bhie', a_i, v_new)
        state = state * jnp.exp(gl_i)[..., None, None] + jnp.einsum('bhcd,bhce->bhde', k_i, v_new)
        return state, o

    xs = (jnp.moveaxis(q_dec, 2, 0), jnp.moveaxis(k_dec, 2, 0), jnp.moveaxis(u, 2, 0),
          jnp.moveaxis(w, 2, 0), jnp.moveaxis(intra, 2, 0), jnp.moveaxis(g_last, 2, 0))
    state0 = jnp.zeros((b, h, dk, dv), jnp.float32)
    _, o = lax.scan(step, state0, xs)
    return o.transpose(1, 0, 3, 2, 4).reshape(b, s, h, dv)

def _gdn_mixer(hp, conv_w, a_log, dt_bias, norm_w):
    f32 = jnp.float32
    bsz, s, _ = hp.shape
    qkv = jax.nn.silu(_causal_depthwise_conv(hp[..., :3 * C_WIDTH], conv_w)).astype(f32)
    gate = hp[..., 3 * C_WIDTH:4 * C_WIDTH].astype(f32)
    beta_raw = hp[..., 4 * C_WIDTH:4 * C_WIDTH + C_HEADS].astype(f32)
    a_raw = hp[..., 4 * C_WIDTH + C_HEADS:].astype(f32)
    q = _l2norm(qkv[..., :C_WIDTH].reshape(bsz, s, C_HEADS, C_HEAD_DIM))
    k = _l2norm(qkv[..., C_WIDTH:2 * C_WIDTH].reshape(bsz, s, C_HEADS, C_HEAD_DIM))
    v = qkv[..., 2 * C_WIDTH:].reshape(bsz, s, C_HEADS, C_HEAD_DIM)
    beta = jax.nn.sigmoid(beta_raw)
    g = -jnp.exp(a_log.astype(f32)) * jax.nn.softplus(a_raw + dt_bias.astype(f32))
    o = _gated_delta_rule(q, k, v, g, beta)
    o = o * lax.rsqrt(jnp.mean(o * o, axis=-1, keepdims=True) + RMS_EPS) * norm_w.astype(f32)
    o = o.reshape(bsz, s, C_WIDTH) * jax.nn.silu(gate)
    return o.astype(hp.dtype)

def setup_inputs(seed: int = 0) -> dict:
    key = jax.random.key(seed)
    ks = jax.random.split(key, 32)
    f32 = jnp.float32

    def nrm(k, shape, scale):
        return jax.random.normal(k, shape, f32) * scale

    ev_in = 3 * A_WIDTH + S5_WIDTH
    od_in = 4 * C_WIDTH + 2 * C_HEADS
    dt_c = jnp.exp(jax.random.uniform(ks[20], (N_ODD, C_HEADS), f32, math.log(1e-3), math.log(1e-1)))
    return {
        'x': nrm(ks[0], (BATCH, SEQ, D_MODEL), 1.0),
        'rel_table': nrm(ks[1], (REL_BUCKETS, A_HEADS), 0.5),
        'ev_w_in': nrm(ks[2], (N_EVEN, D_MODEL, ev_in), D_MODEL ** -0.5),
        'ev_w_out': nrm(ks[3], (N_EVEN, A_WIDTH + S5_WIDTH, D_MODEL), (A_WIDTH + S5_WIDTH) ** -0.5 * DN_BETA),
        's5_lambda_re': -0.5 + nrm(ks[4], (N_EVEN, S5_GROUPS, S5_STATE), 0.01),
        's5_lambda_im': jnp.broadcast_to(jnp.pi * jnp.arange(S5_STATE, dtype=f32), (N_EVEN, S5_GROUPS, S5_STATE)),
        's5_b_re': nrm(ks[5], (N_EVEN, S5_GROUPS, S5_STATE, S5_GROUP), (2 * S5_GROUP) ** -0.5),
        's5_b_im': nrm(ks[6], (N_EVEN, S5_GROUPS, S5_STATE, S5_GROUP), (2 * S5_GROUP) ** -0.5),
        's5_c_re': nrm(ks[7], (N_EVEN, S5_GROUPS, S5_GROUP, S5_STATE), S5_STATE ** -0.5),
        's5_c_im': nrm(ks[8], (N_EVEN, S5_GROUPS, S5_GROUP, S5_STATE), S5_STATE ** -0.5),
        's5_d': nrm(ks[9], (N_EVEN, S5_WIDTH), 1.0),
        's5_log_dt': jax.random.uniform(ks[10], (N_EVEN, S5_GROUPS), f32, math.log(1e-3), math.log(1e-1)),
        's5_w_glu': nrm(ks[11], (N_EVEN, S5_WIDTH, S5_WIDTH), S5_WIDTH ** -0.5),
        's5_b_glu': nrm(ks[12], (N_EVEN, S5_WIDTH), 0.01),
        'od_w_in': nrm(ks[13], (N_ODD, D_MODEL, od_in), D_MODEL ** -0.5),
        'od_conv_w': nrm(ks[14], (N_ODD, C_CONV, 3 * C_WIDTH), C_CONV ** -0.5),
        'od_a_log': jnp.log(jax.random.uniform(ks[15], (N_ODD, C_HEADS), f32, 1.0, 16.0)),
        'od_dt_bias': dt_c + jnp.log(-jnp.expm1(-dt_c)),
        'od_norm_w': 1.0 + nrm(ks[16], (N_ODD, C_HEAD_DIM), 0.01),
        'od_w_out': nrm(ks[17], (N_ODD, C_WIDTH, D_MODEL), C_WIDTH ** -0.5 * DN_BETA),
        'ln_mix_g': 1.0 + nrm(ks[18], (DEPTH, D_MODEL), 0.01),
        'ln_mix_b': nrm(ks[19], (DEPTH, D_MODEL), 0.01),
        'mlp_w1': nrm(ks[21], (DEPTH, D_MODEL, D_FF), D_MODEL ** -0.5),
        'mlp_w2': nrm(ks[22], (DEPTH, D_FF, D_MODEL), D_FF ** -0.5 * DN_BETA),
        'ln_ffn_g': 1.0 + nrm(ks[23], (DEPTH, D_MODEL), 0.01),
        'ln_ffn_b': nrm(ks[24], (DEPTH, D_MODEL), 0.01),
    }

def reference(x, rel_table, ev_w_in, ev_w_out, s5_lambda_re, s5_lambda_im, s5_b_re, s5_b_im,
              s5_c_re, s5_c_im, s5_d, s5_log_dt, s5_w_glu, s5_b_glu, od_w_in, od_conv_w,
              od_a_log, od_dt_bias, od_norm_w, od_w_out, ln_mix_g, ln_mix_b, mlp_w1, mlp_w2,
              ln_ffn_g, ln_ffn_b):
    bsz, s, _ = x.shape
    for layer in range(DEPTH):
        i = layer // 2
        if layer % 2 == 0:
            hp = x @ ev_w_in[i]
            q = hp[..., :A_WIDTH].reshape(bsz, s, A_HEADS, A_HEAD_DIM)
            k = hp[..., A_WIDTH:2 * A_WIDTH].reshape(bsz, s, A_HEADS, A_HEAD_DIM)
            v = hp[..., 2 * A_WIDTH:3 * A_WIDTH].reshape(bsz, s, A_HEADS, A_HEAD_DIM)
            u = hp[..., 3 * A_WIDTH:]
            attn = _moba_attention(q, k, v, rel_table)
            ssm = _s5_mixer(u, s5_lambda_re[i], s5_lambda_im[i], s5_b_re[i], s5_b_im[i],
                            s5_c_re[i], s5_c_im[i], s5_d[i], s5_log_dt[i], s5_w_glu[i], s5_b_glu[i])
            mix = jnp.concatenate([attn, ssm.astype(attn.dtype)], axis=-1) @ ev_w_out[i]
        else:
            hp = x @ od_w_in[i]
            mix = _gdn_mixer(hp, od_conv_w[i], od_a_log[i], od_dt_bias[i], od_norm_w[i]) @ od_w_out[i]
        x = _layer_norm(DN_ALPHA * x + mix.astype(x.dtype), ln_mix_g[layer], ln_mix_b[layer])
        hid = jnp.square(jax.nn.relu(x @ mlp_w1[layer]))
        x = _layer_norm(DN_ALPHA * x + (hid @ mlp_w2[layer]).astype(x.dtype), ln_ffn_g[layer], ln_ffn_b[layer])
    return x


_drawn_inputs = setup_inputs


def setup_inputs(seed=0):
    import zlib

    import numpy as np

    out = dict(_drawn_inputs(seed))
    spreads = {}
    factors = {'s5_lambda_re': 64.0,
     's5_lambda_im': 64.0,
     's5_b_re': 64.0,
     's5_b_im': 64.0,
     's5_c_re': 64.0,
     's5_c_im': 64.0,
     's5_log_dt': 64.0,
     's5_b_glu': 64.0,
     'od_a_log': 2.843,
     'od_norm_w': 45.788,
     'ln_mix_g': 3.87,
     'ln_mix_b': 3.783,
     'ln_ffn_g': 10.854,
     'ln_ffn_b': 10.953}
    for name, (base, spread) in spreads.items():
        noise = np.random.default_rng([zlib.crc32(name.encode()), seed]).standard_normal(out[name].shape)
        drawn = base * np.exp(spread * noise) if base else spread * noise
        out[name] = jnp.asarray(drawn.astype(out[name].dtype))
    for name, factor in factors.items():
        out[name] = (out[name] * factor).astype(out[name].dtype)
    return out
```

```python
import math
from contextlib import ExitStack

import concourse.bass as bass
from concourse import mybir

P = 128
SEQ = 256
DM = 1024
TM = SEQ // P
KC = DM // P
NW = 512
AH, AD = 8, 64
AW = AH * AD
SG, SH, SN = 32, 16, 64
SW = SG * SH
NJ = SG // 2
CH, CD, CONV, CK = 8, 128, 4, 64
FF = 4 * DM
FB = FF // NW
ALPHA = 4.0 ** 0.25
LN_EPS, RMS_EPS, L2_EPS = 1e-5, 1e-6, 1e-6
NEG = -1e30
BUCKETS = 32
GW = 384
ROUND = 1.5 * 2.0 ** 23
ROUND16 = 1.5 * 2.0 ** 9
TWO_PI = 2 * math.pi
PI_A, PI_B = 6.28125, 1.9350051879882812e-3
PI_C = TWO_PI - PI_A - PI_B

RAW, SPL = 8, 4
EV_IN, GLU, EV_OUT = 0, 16, 18
MLP_A = 26
OD_IN = MLP_A + 8 * FB
OD_OUT = OD_IN + 32
MLP_B = OD_OUT + 8
SLABS = MLP_B + 8 * FB

C_ID, C_UP, C_SAME, C_NEG, C_LVL = 0, 128, 256, 384, 512
LEVELS = 6
C_CH = C_LVL + LEVELS * P
C_T = C_CH + 2 * P
C_ONE = C_T + 32
C_FLIP = C_ONE + 2
C_W = C_FLIP + P


def build(nc, x, rel_table, ev_w_in, ev_w_out, lam_re, lam_im, b_re, b_im, c_re, c_im, s5_d,
          log_dt, w_glu, b_glu, od_w_in, conv_w, a_log, dt_bias, norm_w, od_w_out,
          ln_mix_g, ln_mix_b, mlp_w1, mlp_w2, ln_ffn_g, ln_ffn_b, consts, onehot, out):
    f32, f32r = mybir.dt.float32, mybir.dt.float32r
    ALU, ACT, AX = mybir.AluOpType, mybir.ActivationFunctionType, mybir.AxisListType
    MUL, ADD, SUB, MAX = ALU.mult, ALU.add, ALU.subtract, ALU.max

    ctx = ExitStack()
    with ctx:
        def sb(name, shape, dt=f32):
            return ctx.enter_context(nc.sbuf_tensor(name, shape, dt))

        def sem(name):
            return ctx.enter_context(nc.semaphore(name))

        raw = sb("raw", [P, RAW, 2, NW])
        whi = sb("whi", [P, SPL, 2, NW], f32r)
        wlo = sb("wlo", [P, SPL, 2, NW], f32r)
        xrow = sb("xrow", [P, TM, DM])
        xh = sb("xh", [P, KC, SEQ], f32r)
        xl = sb("xl", [P, KC, SEQ], f32r)
        fh = sb("fh", [P, 4, SEQ], f32r)
        fl = sb("fl", [P, 4, SEQ], f32r)
        stage = sb("stage", [P, 2, TM, NW])
        cst = sb("cst", [P, C_W])
        lnp = sb("lnp", [P, 2, DM])
        lns = sb("lns", [P, TM, 2, 6])
        lnm = sb("lnm", [P, TM, 2])
        lnr = sb("lnr", [P, TM])
        arena = sb("arena", [P, 22000])
        ps = ctx.enter_context(nc.psum_tensor("ps", [P, 8, NW], f32))

        ident = cst[:, C_ID:C_ID + P]

        class Carve:
            def __init__(self):
                self.at = 0

            def __call__(self, *shape, rows=P):
                n = int(math.prod(shape))
                v = arena[0:rows, self.at:self.at + n]
                self.at += n
                if len(shape) == 1:
                    return v
                names = "abcd"[:len(shape)]
                return v.rearrange(f"p ({' '.join(names)}) -> p {' '.join(names)}",
                                   **dict(zip(names, shape)))

        A = Carve()
        uT, qT, kT = A(4, SEQ), A(4, SEQ), A(4, SEQ)
        vrow = A(TM, AW)
        bias = A(AH, GW)
        tab33 = A(AH, rows=BUCKETS + 1)
        att_s, att_p, att_pt = A(GW), A(GW), A(GW)
        hot, biasrow = att_s[0:BUCKETS + 1], att_p[0:AH]
        att_nm, att_sum, att_rs = A(2 * AH), A(TM, AH), A(TM, AH)
        prow = A(P, rows=104)
        yT, zs = A(4, SEQ), A(4, SEQ)
        early1 = stage[:, 1].rearrange("p a b -> p (a b)")
        lamr, lami, lrd, th, nn, rr, den, s1 = (early1[0:NJ, P * k:P * k + P] for k in range(8))
        s2, aim, ar1, t16 = (yT.rearrange("p a b -> p (a b)")[0:NJ, P * k:P * k + P] for k in range(4))
        par16 = zs.rearrange("p a b -> p (a b)")[0:NJ, 0:5 * P].rearrange("p (a b) -> p a b", a=5)
        ldt = A(2, rows=NJ)
        par = A(5, NJ)
        ph, pr = A(NJ, 32), A(NJ, 32)
        sint, cost = A(NJ, 32), A(NJ, 32)
        bre, bim, btmp, btm2 = A(NJ, SH), A(NJ, SH), A(NJ, SH), A(NJ, SH)
        bpad = lnp[:, 0, :].rearrange("p (a b c) -> p a b c", a=2, b=NJ)
        bT = A(2, 4, P)
        cpad = lnp[:, 1, :].rearrange("p (a b c) -> p a b c", a=2, b=4)
        cT = A(2, 4, P)
        tcos, tsin, ttmp = A(2, 2, SEQ), A(2, 2, SEQ), A(2, SEQ)
        pa, pb, pc, pd = A(2, SEQ), A(2, SEQ), A(2, SEQ), A(2, SEQ)
        gre, gim = A(2, SEQ), A(2, SEQ)
        params = sb("params", [P, 104])
        half_pi = sb("half_pi", [P, 1])

        A = Carve()
        convT = A(24, SEQ)
        kTd, qTd, vTd = convT[:, 0:8, :], convT[:, 8:16, :], convT[:, 16:24, :]
        gate = A(TM, DM)
        dv, kw, kdec = A(TM, CH, CD), A(TM, CH, CD), A(TM, CH, CD)
        NT, intraT = A(TM, CH, P), A(TM, CH, P)
        TT = A(TM, CH, P)
        T = vTd.rearrange("p a (b c) -> p (a b) c", b=2).rearrange("p (m h) c -> p m h c", m=TM)
        XX = lnp[:, 0, :].rearrange("p (a b c) -> p a b c", a=2, b=4)
        dec = A(4, P)
        SM = A(24, TM, CH)
        sm = [SM[:, i] for i in range(24)]
        (BETA, XG, AXX, E1, W1, LW, DD, EQ, GR, EG, NEGEG, EKD, GC, IK, RK, DINV, SSK, SSQ, RQ, BRK2,
         BRK, CC, BB) = range(23)
        ba_b = sm[BB]
        WT = T
        vnew = kw
        S = [None, NT[:, 0], NT[:, 1], lnp[:, 1, :].rearrange("p (a b) -> p a b", a=CH)]
        obuf = XX.rearrange("p a b c -> p (a b c)")
        sqT = kdec[:, 0].rearrange("p a b -> p (a b)").rearrange("p (a b) -> p a b", a=4)

        def osq(m):
            return intraT[:, m].rearrange("p a b -> p (a b)")

        wba = sb("wba", [P, KC, 16])
        nw = sb("nw", [P, CD])
        wbh = sb("wbh", [P, KC, 16], f32r)
        wbl = sb("wbl", [P, KC, 16], f32r)
        alog = sb("alog", [P, CH])
        dtb = sb("dtb", [P, CH])
        egl = sb("egl", [P, 4, CH])
        scratch = nc.dram_tensor("bias_rows", [AH, GW], f32, kind="Internal").ap()

        loaded = [sem(f"slab_loaded{i}") for i in range(RAW)]
        hi_ready = sem("hi_ready")
        lo_ready = sem("lo_ready")
        slab_used = sem("slab_used")
        s_x, s_cst, s_small, s_lnp = sem("x_loaded"), sem("consts_loaded"), sem("small_loaded"), sem("lnp_loaded")
        s_bias_in, s_bias_out = sem("bias_rows_stored"), sem("bias_loaded")
        s_out = sem("out_stored")
        s_l1 = sem("layer1_small_loaded")
        s_zero, s_cp = sem("pads_cleared"), sem("c_padded")
        dve_ch, act_ch, pool_ch = sem("dve_chain"), sem("act_chain"), sem("pool_chain")
        xt_ps, xt_hi, xt_lo = sem("xt_in_psum"), sem("xt_hi"), sem("xt_lo")
        ln_var, ln_rstd, ln_done = sem("ln_var"), sem("ln_rstd"), sem("ln_done")
        h_row, ht_ps, ht_hi, ht_lo = sem("h_rows"), sem("ht_in_psum"), sem("ht_hi"), sem("ht_lo")
        g_row, t_ps, t_sb = sem("proj_rows"), sem("projT_in_psum"), sem("projT")

        s_tab, s_prow, s_b, s_wba, wb_split = (
            sem("s_tab"), sem("s_prow"), sem("s_b"), sem("s_wba"), sem("wb_split"))
        tab_ready, phases_ready, rot_ready, rot_done, scan_done = (
            sem("tab_ready"), sem("phases_ready"), sem("rot_ready"), sem("rot_done"), sem("scan_done"))
        unrot_half, unrot_dve, him_ready, hre_ready, h_relu = (
            sem("unrot_half"), sem("unrot_dve"), sem("him_ready"), sem("hre_ready"), sem("h_relu"))
        t_init, gate_w, s5_dt, s5_ang, s5_mag = (
            sem("t_init"), sem("gate_w"), sem("s5_dt"), sem("s5_ang"), sem("s5_mag"))
        s5_par, par_ps, prow_ps, bias_ps, bias_row_sb = (
            sem("s5_par"), sem("par_ps"), sem("prow_ps"), sem("bias_ps"), sem("bias_row_sb"))
        params_sb, ph_done, b_padded, b_ps, bT_sb = (
            sem("params_sb"), sem("ph_done"), sem("b_padded"), sem("b_ps"), sem("bT_sb"))
        c_ps, cT_sb, x_ps, y_done, y_sum = (
            sem("c_ps"), sem("cT_sb"), sem("x_ps"), sem("y_done"), sem("y_sum"))
        gelu_hi, gelu_lo, z_ps, z_sig, ssm_rows = (
            sem("gelu_hi"), sem("gelu_lo"), sem("z_ps"), sem("z_sig"), sem("ssm_rows"))
        ssm_hi, ssm_lo, att_sc, att_max, att_exp = (
            sem("ssm_hi"), sem("ssm_lo"), sem("att_sc"), sem("att_max"), sem("att_exp"))
        att_pt_ps, att_pt_sb, att_o, att_rows, conv_done = (
            sem("att_pt_ps"), sem("att_pt_sb"), sem("att_o"), sem("att_rows"), sem("conv_done"))
        sq_done, ss_ps, v_silu, t1_ps, g1_row = (
            sem("sq_done"), sem("ss_ps"), sem("v_silu"), sem("t1_ps"), sem("g1_row"))
        ba_ps, ba_sb, gate_exp, cum_ps, cum_exp = (
            sem("ba_ps"), sem("ba_sb"), sem("gate_exp"), sem("cum_ps"), sem("cum_exp"))
        g_ready, dec_in, dec_ready, norm_in, norm_out = (
            sem("g_ready"), sem("dec_in"), sem("dec_ready"), sem("norm_in"), sem("norm_out"))
        kk_ps, nt_ready, rows_ps, rows_sb, nt_ps = (
            sem("kk_ps"), sem("nt_ready"), sem("rows_ps"), sem("rows_sb"), sem("nt_ps"))
        xx_ready, tx_ps, t_done, wt_ps, wt_sb = (
            sem("xx_ready"), sem("tx_ps"), sem("t_done"), sem("wt_ps"), sem("wt_sb"))
        v_ps, vnew_done, kv_ps, s_ready, o2_ps = (
            sem("v_ps"), sem("vnew_done"), sem("kv_ps"), sem("s_ready"), sem("o2_ps"))
        o2_sb, o_sum, o_sq, rms_in, rms_out = (
            sem("o2_sb"), sem("o_sum"), sem("o_sq"), sem("rms_in"), sem("rms_out"))
        o_rows = sem("o_rows")

        block = ctx.enter_context(nc.Block())

        def bc(ap, shape):
            return ap.to_broadcast(shape)

        def psq(b, n=1):
            return ps[:, b:b + n, :].rearrange("p a b -> p (a b)")

        def in_slab(w, col, k):
            return w[256 * k:256 * k + 256, col:col + NW].rearrange("(a p) n -> p a n", p=P)

        EV_COLS = [3 * AW, 0, AW, 2 * AW]
        OD_COLS = [DM, DM + NW, 0, NW, 2 * DM, 2 * DM + NW, 3 * DM, 3 * DM + NW]

        def hi(act, s, i=0):
            act.wait_ge(loaded[s % RAW], 16 * (s // RAW + 1) + 16 * i)
            if s >= SPL:
                act.wait_ge(slab_used, s - SPL + 1 + 8 * i)
            act.activation(whi[:, s % SPL], raw[:, s % RAW], ACT.Copy).then_inc(hi_ready, 1)

        def lo(dve, s, i=0):
            dve.wait_ge(hi_ready, s + 1 + 8 * i)
            dve.tensor_tensor(wlo[:, s % SPL], raw[:, s % RAW], whi[:, s % SPL].bitcast(f32),
                              SUB).then_inc(lo_ready, 1)

        def slab_product(pe, s, banks, left, k0, first, last, i=0):
            lh, ll = left
            pe.wait_ge(lo_ready, s + 1 + 8 * i)
            q = s % SPL
            for m in range(TM):
                for kk in range(2):
                    rows = slice(m * P, m * P + P)
                    o = ps[:, banks[m], :]
                    a, b = first and kk == 0, last and kk == 1
                    pe.matmul(o, lh[:, k0 + kk, rows], whi[:, q, kk, :], start=a, stop=False)
                    pe.matmul(o, lh[:, k0 + kk, rows], wlo[:, q, kk, :], start=False, stop=False)
                    ins = pe.matmul(o, ll[:, k0 + kk, rows], whi[:, q, kk, :], start=False, stop=b)
            ins.then_inc(slab_used, 1)
            return ins

        NT_PAIR = KC // 2

        def xt_transposes(pe, r, banks, srcs=KC // 2, src=None, wait=None):
            for q in range(srcs):
                for j in range(2):
                    for m in range(TM):
                        c = 2 * q + j
                        ins = pe.transpose(ps[:, banks[q], j * SEQ + m * P:j * SEQ + m * P + P],
                                           src[:, m, c * P:c * P + P], ident)
                ins.then_inc(xt_ps, 1)

        XT = {"x": 0, "att": 4, "ln0": 6, "ln1": 10, "gdn": 14, "ln2": 18}

        def xt_upper(act, r, banks, n=4, dst=0):
            for q in range(n):
                act.wait_ge(xt_ps, XT[r] + q + 1)
                act.activation(xh[:, dst + 2 * q:dst + 2 * q + 2, :],
                               ps[:, banks[q], :].rearrange("p (a b) -> p a b", a=2),
                               ACT.Copy).then_inc(xt_hi, 1)

        def xt_lower(dve, r, banks, n=4, dst=0):
            for q in range(n):
                dve.wait_ge(xt_hi, XT[r] + q + 1)
                dve.tensor_tensor(xl[:, dst + 2 * q:dst + 2 * q + 2, :],
                                  ps[:, banks[q], :].rearrange("p (a b) -> p a b", a=2),
                                  xh[:, dst + 2 * q:dst + 2 * q + 2, :].bitcast(f32),
                                  SUB).then_inc(xt_lo, 1)

        def ln_stats(dve, r, chain):
            for m in range(TM):
                dve.wait_ge(slab_used, (EV_OUT + 8, MLP_A + 8 * FB, OD_OUT + 8, MLP_B + 8 * FB)[r])
                chain(dve.scalar_tensor_tensor(xrow[:, m, :], xrow[:, m, :], ALPHA, psq(2 * m, 2),
                                               MUL, ADD))
                for j in range(2):
                    ins = dve.bn_stats(lns[:, m, j, :], xrow[:, m, j * NW:j * NW + NW])
                chain(ins)
                chain(dve.bn_aggr(lnm[:, m, :], lns[:, m, :, :]))
                chain(dve.tensor_scalar(lnr[:, m:m + 1], lnm[:, m, 1:2], LN_EPS, None, ADD))
                dve.reciprocal(lnr[:, m:m + 1], lnr[:, m:m + 1]).then_inc(ln_var, 1)

        def ln_sqrt(act, r):
            for m in range(TM):
                act.wait_ge(ln_var, 2 * r + m + 1)
                act.activation(lnr[:, m:m + 1], lnr[:, m:m + 1], ACT.Sqrt).then_inc(ln_rstd, 1)

        def ln_apply(dve, r, chain):
            dve.wait_ge(s_lnp, 32 * (r + 1))
            for m in range(TM):
                dve.wait_ge(ln_rstd, 2 * r + m + 1)
                chain(dve.tensor_scalar(xrow[:, m, :], xrow[:, m, :], lnm[:, m, 0:1],
                                        lnr[:, m:m + 1], SUB, MUL))
                chain(dve.tensor_tensor(xrow[:, m, :], xrow[:, m, :], lnp[:, 0, :], MUL))
                dve.tensor_tensor(xrow[:, m, :], xrow[:, m, :], lnp[:, 1, :], ADD).then_inc(ln_done, 1)

        @block.sync
        def _(sp):
            def load(s, src, i=0):
                if s >= RAW:
                    sp.wait_ge(lo_ready, s - RAW + 1 + 8 * i)
                sp.dma_start(raw[:, s % RAW], src).then_inc(loaded[s % RAW], 16)

            def load_row(s, w, row, col, i=0):
                load(s, w[bass.ds(row, 256), bass.ds(col, NW)].rearrange("(a p) n -> p a n", p=P), i)

            for m in range(TM):
                sp.dma_start(xrow[:, m, :], x[0, m * P:m * P + P, :]).then_inc(s_x, 16)
            for g in range(4):
                for k in range(4):
                    load(EV_IN + 4 * g + k, in_slab(ev_w_in[0], EV_COLS[g], k))
            for k in range(2):
                load(GLU + k, in_slab(w_glu[0], 0, k))
            for n in range(2):
                for k in range(4):
                    load(EV_OUT + 4 * n + k, in_slab(ev_w_out[0], n * NW, k))

            def mlp_loads(base, layer):
                w1, w2 = mlp_w1[layer], mlp_w2[layer]
                for k in range(4):
                    load(base + k, in_slab(w1, 0, k))
                with sp.Fori(0, FB - 1) as j:
                    for k in range(4):
                        load_row(base + 4 + k, w1, 256 * k, NW * j + NW, j)
                    for n in range(2):
                        for k in range(2):
                            load_row(base + 8 + 2 * n + k, w2, NW * j + 256 * k, NW * n, j)
                for n in range(2):
                    for k in range(2):
                        load(base + 8 * FB - 4 + 2 * n + k, in_slab(w2, NW * n, 2 * (FB - 1) + k))

            mlp_loads(MLP_A, 0)
            for g in range(8):
                for k in range(4):
                    load(OD_IN + 4 * g + k, in_slab(od_w_in[0], OD_COLS[g], k))
            for n in range(2):
                for k in range(4):
                    load(OD_OUT + 4 * n + k, in_slab(od_w_out[0], n * NW, k))
            mlp_loads(MLP_B, 1)
            for m in range(TM):
                sp.wait_ge(ln_done, 6 + m + 1)
                sp.dma_start(out[0, m * P:m * P + P, :], xrow[:, m, :]).then_inc(s_out, 16)
            sp.wait_ge(s_out, 16 * TM)


        def chained(eng, s):
            n = [0]

            def chain(ins):
                n[0] += 1
                ins.then_inc(s, 1)
                eng.wait_ge(s, n[0])
            return chain

        def inverse_step(dve, lev, b, chain):
            m, h0, n = b // 2, 4 * (b % 2), 4 * lev + b
            dve.wait_ge(tx_ps, n + 1)
            t, tt = T[:, m, h0:h0 + 4, :], TT[:, m, h0:h0 + 4, :]
            dve.tensor_tensor(t, t, ps[:, 2, :].rearrange("p (a b) -> p a b", a=4), SUB)
            dve.tensor_tensor(tt, tt, ps[:, 3, :].rearrange("p (a b) -> p a b", a=4), SUB).then_inc(t_done, 1)

        @block.gpsimd
        def _(pool):
            chain = chained(pool, pool_ch)
            chain(pool.memset(tab33[BUCKETS:BUCKETS + 1, :], NEG))
            chain(pool.memset(cpad.rearrange("p a b c -> p (a b c)"), 0.0))
            pool.sem_inc(s_zero, 1)
            chain(pool.memset(bpad.rearrange("p a b c -> p (a b c)"), 0.0))
            chain(pool.memset(half_pi[:, :], math.pi / 2))
            pool.sem_inc(s_zero, 1)

            def tables(q):
                j, t = 2 * q, q % 2
                fine = [v[:, j:j + 2, 0:16].unsqueeze(2).to_broadcast([P, 2, 16, 16]) for v in (cost, sint)]
                rough = [v[:, j:j + 2, 16:32].unsqueeze(3).to_broadcast([P, 2, 16, 16]) for v in (cost, sint)]
                tc, ts_, tt = [v.rearrange("p j (a b) -> p j a b", a=16) for v in (tcos[:, t], tsin[:, t], ttmp)]
                if q >= 2:
                    pool.wait_ge(hre_ready, q - 1)
                pool.tensor_tensor(tc, rough[0], fine[0], MUL)
                chain(pool.tensor_tensor(tt, rough[1], fine[1], MUL))
                chain(pool.tensor_tensor(tc, tc, tt, SUB))
                pool.tensor_tensor(ts_, rough[1], fine[0], MUL)
                chain(pool.tensor_tensor(tt, rough[0], fine[1], MUL))
                pool.tensor_tensor(ts_, ts_, tt, ADD).then_inc(tab_ready, 1)

            pool.wait_ge(phases_ready, 2)
            tables(0)
            for q in range(NJ // 2):
                pool.wait_ge(rot_ready, q + 1)
                pool.tensor_tensor(pa, pa, pb, ADD)
                pool.tensor_tensor(pc, pc, pd, SUB).then_inc(rot_done, 1)
                if q + 1 < NJ // 2:
                    tables(q + 1)
                pool.wait_ge(scan_done, q + 1)
                pool.tensor_tensor(pb, tsin[:, q % 2], gim, MUL).then_inc(unrot_half, 1)
                chain(pool.tensor_tensor(pc, tsin[:, q % 2], gre, MUL))
                pool.wait_ge(unrot_dve, 2 * q + 1)
                pool.tensor_tensor(pd, pd, pc, ADD).then_inc(him_ready, 1)

            def squares(layer, i=0, j0=0):
                for m in range(TM):
                    pool.wait_ge(h_relu, TM * (FB * layer + j0) + m + 1 + TM * i)
                    pool.tensor_tensor(stage[:, 0, m, :], stage[:, 0, m, :], stage[:, 0, m, :],
                                       MUL).then_inc(h_row, 1)

            with pool.Fori(0, FB) as j:
                squares(0, j)
            pool.wait_ge(g1_row, TM * 8)
            for m in range(TM):
                g3 = gate[:, m, :].rearrange("p (h d) -> p h d", h=CH)
                ins = pool.tensor_tensor(g3, g3, nw[:, :].unsqueeze(1).to_broadcast([P, CH, CD]), MUL)
            ins.then_inc(gate_w, 1)
            pool.wait_ge(rows_ps, 4)
            for m in range(TM):
                for h in range(CH):
                    pool.tensor_copy(T[:, m, h, :], ident)
                    ins = pool.tensor_copy(TT[:, m, h, :], ident)
            ins.then_inc(t_init, 1)
            with pool.Fori(0, FB) as j:
                squares(1, j)

        @block.scalar
        def _(act):
            chain = chained(act, act_ch)
            act.dma_start(cst[:, :], consts).then_inc(s_cst, 16)
            act.dma_start(tab33[0:BUCKETS, :], rel_table).then_inc(s_tab, 16)
            act.dma_start(hot, onehot).then_inc(s_tab, 16)
            act.dma_start(ldt, log_dt[0].rearrange("(j g) -> j g", g=2)).then_inc(s_small, 16)
            act.dma_start(lamr, lam_re[0].rearrange("(j g) n -> j (g n)", g=2)).then_inc(s_small, 16)
            act.dma_start(lami, lam_im[0].rearrange("(j g) n -> j (g n)", g=2)).then_inc(s_small, 16)
            act.dma_start(prow[0:96, :], conv_w[0].rearrange("k (c p) -> (k c) p", p=P)).then_inc(s_prow, 16)
            act.dma_start(prow[96:100, :], s5_d[0].rearrange("(c p) -> c p", p=P)).then_inc(s_prow, 16)
            act.dma_start(prow[100:104, :], b_glu[0].rearrange("(c p) -> c p", p=P)).then_inc(s_prow, 16)
            act.dma_start(wba[:, :, :], od_w_in[0][:, 4 * DM:4 * DM + 16].rearrange("(a p) n -> p a n", p=P)).then_inc(s_wba, 16)
            act.dma_start(alog[:, :], a_log.to_broadcast([P, CH])).then_inc(s_l1, 16)
            act.dma_start(dtb[:, :], dt_bias.to_broadcast([P, CH])).then_inc(s_l1, 16)
            act.dma_start(nw[:, :], norm_w.to_broadcast([P, CD])).then_inc(s_l1, 16)
            act.dma_start(bre, b_re[0].rearrange("(j g) n h -> (g n) j h", g=2)).then_inc(s_b, 16)
            act.dma_start(bim, b_im[0].rearrange("(j g) n h -> (g n) j h", g=2)).then_inc(s_b, 16)
            act.wait_ge(s_zero, 1)
            for r, src in enumerate((c_re, c_im)):
                for g in range(8):
                    act.dma_start(cpad[16 * g:16 * g + 16, r, :, SN * (g % 2):SN * (g % 2) + SN],
                                  src[0].rearrange("(c g) h n -> g h c n", g=8)[g]).then_inc(s_cp, 16)
            act.wait_ge(s_small, 48)
            act.activation(ldt, ldt, ACT.Exp).then_inc(s5_dt, 1)
            hi(act, 0)
            act.wait_ge(s5_ang, 1)
            act.activation(par16[:, 0, :], lrd, ACT.Exp).then_inc(s5_mag, 1)
            act.activation(s1, rr, ACT.Sin).then_inc(s5_mag, 1)
            act.activation(s2, t16, ACT.Sin).then_inc(s5_mag, 1)
            xt_upper(act, "x", (4, 5, 6, 7))
            for s in range(1, 4):
                hi(act, s)
            act.wait_ge(bias_row_sb, 1)
            act.dma_start(scratch, biasrow).then_inc(s_bias_in, 16)
            act.wait_ge(s_bias_in, 16)
            for off, c0, n in ((P, 0, P), (0, P, SEQ)):
                act.dma_start(bias[:, :, c0:c0 + n],
                              bass.AP(tensor=scratch.tensor, offset=off,
                                      ap=[[1, P], [GW, AH], [1, n]])).then_inc(s_bias_out, 16)
            act.wait_ge(ph_done, 1)
            act.wait_ge(s_zero, 2)
            act.activation(sint, ph, ACT.Sin, scale=6.283185).then_inc(phases_ready, 1)
            chain(act.activation(pr, ph, ACT.Abs))
            act.activation(cost, pr, ACT.Sin, scale=-6.283185, bias=half_pi[:, 0:1]).then_inc(phases_ready, 1)

            def rows_out(g, dst):
                for m in range(TM):
                    act.wait_ge(slab_used, EV_IN + 4 * g + 4)
                    act.activation(dst[:, m, :], ps[:, 4 + m, :], ACT.Copy).then_inc(g_row, 1)

            def transposed_out(g, dst, scale):
                act.wait_ge(t_ps, g + 1)
                act.activation(dst.rearrange("p a b -> p (a b)"), psq(2, 2), ACT.Copy,
                               scale=scale).then_inc(t_sb, 1)

            act.wait_ge(s_wba, 16)
            act.activation(wbh[:, :, :], wba[:, :, :], ACT.Copy).then_inc(wb_split, 1)
            rows_out(0, stage[:, 0])
            for s in range(4, 8):
                hi(act, s)
            rows_out(1, stage[:, 1])
            transposed_out(0, uT, 1.0)
            for s in range(8, 12):
                hi(act, s)
            transposed_out(1, qT, AD ** -0.5)
            rows_out(2, stage[:, 0])
            for s in range(12, 16):
                hi(act, s)
            transposed_out(2, kT, 1.0)
            rows_out(3, vrow)
            for s in range(GLU, GLU + 4):
                hi(act, s)

            for h in range(AH):
                act.wait_ge(att_max, h + 1)
                if h >= 1:
                    act.wait_ge(att_pt_ps, h)
                for m in range(TM):
                    c0, n = (0, P) if m == 0 else (P, SEQ)
                    ins = act.activation(att_p[:, c0:c0 + n], ps[:, 4, c0:c0 + n], ACT.Exp,
                                         bias=att_nm[:, 2 * h + m:2 * h + m + 1],
                                         accum_out=att_sum[:, m, h:h + 1])
                ins.then_inc(att_exp, 1)
                act.wait_ge(att_pt_ps, h + 1)
                if h >= 1:
                    act.wait_ge(att_o, h)
                act.activation(att_pt, ps[:, 5, 0:GW], ACT.Copy).then_inc(att_pt_sb, 1)
            xt_upper(act, "att", (4, 5), n=2)

            for c in range(4):
                act.wait_ge(y_sum, c + 1)
                chain(act.activation(yT[:, c, :], yT[:, c, :], ACT.Gelu_apprx_tanh))
                act.activation(fh[:, c, :], yT[:, c, :], ACT.Copy).then_inc(gelu_hi, 1)
            for c in range(4):
                act.wait_ge(z_ps, 1)
                act.activation(zs[:, c, :], ps[:, c // 2, (c % 2) * SEQ:(c % 2) * SEQ + SEQ], ACT.Sigmoid,
                               bias=params[:, 100 + c:101 + c]).then_inc(z_sig, 1)
            for c in range(4):
                act.wait_ge(ssm_rows, c + 1)
                act.activation(xh[:, 4 + c, :], yT[:, c, :], ACT.Copy).then_inc(ssm_hi, 1)
            for s in range(EV_OUT + 2, EV_OUT + 8):
                hi(act, s)

            def lnp_load(g, b):
                for k, w in enumerate((g, b)):
                    act.dma_start(lnp[:, k, :], w.unsqueeze(0).to_broadcast([P, DM])).then_inc(s_lnp, 16)

            lnp_load(ln_mix_g[0], ln_mix_b[0])
            ln_sqrt(act, 0)
            for s in range(MLP_A, MLP_A + 4):
                hi(act, s)
            xt_upper(act, "ln0", (4, 5, 6, 7))
            act.wait_ge(ln_done, TM * 1)
            lnp_load(ln_ffn_g[0], ln_ffn_b[0])

            def relu(layer, i=0, j0=0):
                base = (MLP_A, MLP_B)[layer] + 8 * j0 + (0 if j0 else 4)
                for m in range(TM):
                    act.wait_ge(slab_used, base + 8 * i)
                    act.activation(stage[:, 0, m, :], ps[:, 4 + m, :], ACT.Relu).then_inc(h_relu, 1)

            def ht_upper(layer, i=0, j0=0):
                for q in range(2):
                    act.wait_ge(ht_ps, 2 * (FB * layer + j0) + q + 1 + 2 * i)
                    act.activation(fh[:, 2 * q:2 * q + 2, :],
                                   ps[:, 6 + q, :].rearrange("p (a b) -> p a b", a=2),
                                   ACT.Copy).then_inc(ht_hi, 1)

            def mlp(base, layer):
                relu(layer)
                for k in range(4, 8):
                    hi(act, base + k)

                with act.Fori(0, FB - 1) as j:
                    hi(act, base + 8, j)
                    hi(act, base + 9, j)
                    ht_upper(layer, j)
                    hi(act, base + 10, j)
                    hi(act, base + 11, j)
                    relu(layer, j, 1)
                    for k in range(12, 16):
                        hi(act, base + k, j)
                ht_upper(layer, 0, FB - 1)

            mlp(MLP_A, 0)
            ln_sqrt(act, 1)

            for s in range(OD_IN, OD_IN + 4):
                hi(act, s)
            xt_upper(act, "ln1", (4, 5, 6, 7))

            def conv_silu(g):
                act.wait_ge(conv_done, g + 1)
                v = convT[:, 4 * g:4 * g + 4, :]
                ins = act.activation(v, v, ACT.Silu)
                if g < 4:
                    chain(ins)
                    if g:
                        act.wait_ge(ss_ps, g)
                    act.activation(sqT, v, ACT.Square).then_inc(sq_done, 1)
                else:
                    ins.then_inc(v_silu, 1)

            def od_rows_out(g):
                b = 4 + 2 * (g % 2)
                if g >= 2:
                    act.wait_ge(t1_ps, min(g - 1, 6))
                for m in range(TM):
                    act.wait_ge(slab_used, OD_IN + 4 * g + 4)
                    if g < 6:
                        act.activation(stage[:, g % 2, m, :], ps[:, b + m, :], ACT.Copy).then_inc(g1_row, 1)
                    else:
                        act.activation(gate[:, m, (g - 6) * NW:(g - 5) * NW], ps[:, b + m, :],
                                       ACT.Silu).then_inc(g1_row, 1)

            for g in range(8):
                for k in range(4):
                    hi(act, OD_IN + 4 * (g + 1) + k)
                od_rows_out(g)
                if g >= 2:
                    conv_silu(g - 2)

            act.wait_ge(ba_sb, 1)
            act.activation(sm[BETA], ba_b, ACT.Exp, scale=-1.0).then_inc(gate_exp, 1)
            act.activation(alog[:, :], alog[:, :], ACT.Exp).then_inc(gate_exp, 1)
            act.wait_ge(ba_sb, 2)
            act.activation(sm[E1], sm[AXX], ACT.Exp, scale=-1.0).then_inc(gate_exp, 1)
            act.wait_ge(ba_sb, 3)
            act.activation(sm[LW], sm[W1], ACT.Ln).then_inc(gate_exp, 1)
            act.wait_ge(norm_in, 1)
            act.activation(sm[RK], sm[IK], ACT.Sqrt).then_inc(norm_out, 1)
            act.activation(sm[DINV], sm[SSK], ACT.Sqrt).then_inc(norm_out, 1)
            act.activation(sm[RQ], sm[SSQ], ACT.Sqrt).then_inc(norm_out, 1)
            act.wait_ge(ba_sb, 4)
            act.activation(sm[EG], sm[GC], ACT.Exp).then_inc(cum_exp, 1)
            act.activation(egl[:, :, :].rearrange("p a b -> p (a b)"), ps[:, 1, 64:96], ACT.Exp).then_inc(cum_exp, 1)
            act.activation(sm[EKD], sm[EKD], ACT.Exp).then_inc(cum_exp, 1)
            for b in range(4):
                act.wait_ge(dec_in, b + 1)
                act.activation(dec, dec, ACT.Exp).then_inc(dec_ready, 1)
            for b in range(4):
                act.wait_ge(wt_ps, b + 1)
                act.activation(WT[:, b // 2, 4 * (b % 2):4 * (b % 2) + 4, :],
                               ps[:, 4 + b, :].rearrange("p (a b) -> p a b", a=4), ACT.Copy).then_inc(wt_sb, 1)
            for m in range(TM):
                act.wait_ge(o2_ps, m + 1)
                if m:
                    act.wait_ge(o_rows, m)
                act.activation(obuf, psq(6, 2), ACT.Copy).then_inc(o2_sb, 1)
                act.wait_ge(o_sum, m + 1)
                act.activation(osq(m), obuf, ACT.Square).then_inc(o_sq, 1)
                act.wait_ge(rms_in, m + 1)
                act.activation(sm[CC][:, m, :], sm[CC][:, m, :], ACT.Sqrt).then_inc(rms_out, 1)
            act.wait_ge(o_rows, TM)
            lnp_load(ln_mix_g[1], ln_mix_b[1])
            xt_upper(act, "gdn", (4, 5, 6, 7))
            for s in range(OD_OUT + 4, OD_OUT + 8):
                hi(act, s)
            ln_sqrt(act, 2)
            for s in range(MLP_B, MLP_B + 4):
                hi(act, s)
            xt_upper(act, "ln2", (4, 5, 6, 7))
            act.wait_ge(ln_done, TM * 3)
            lnp_load(ln_ffn_g[1], ln_ffn_b[1])
            mlp(MLP_B, 1)
            ln_sqrt(act, 3)

        @block.vector
        def _(dve):
            chain = chained(dve, dve_ch)
            dve.wait_ge(s5_dt, 1)
            dtb3 = ldt.unsqueeze(2).to_broadcast([NJ, 2, SN])

            def v3(a):
                return a.rearrange("p (g n) -> p g n", g=2)

            chain(dve.tensor_scalar(lamr, lamr, -1e-4, None, ALU.min))
            dve.tensor_tensor(v3(lrd), v3(lamr), dtb3, MUL)
            chain(dve.tensor_tensor(v3(th), v3(lami), dtb3, MUL))
            chain(dve.tensor_scalar(nn, th, 1 / TWO_PI, ROUND, MUL, ADD))
            chain(dve.tensor_scalar(nn, nn, ROUND, None, SUB))
            chain(dve.scalar_tensor_tensor(rr, nn, -PI_A, th, MUL, ADD))
            chain(dve.scalar_tensor_tensor(rr, nn, -PI_B, rr, MUL, ADD))
            chain(dve.scalar_tensor_tensor(rr, nn, -PI_C, rr, MUL, ADD))
            chain(dve.tensor_scalar(rr, rr, 3.1415925, -3.1415925, ALU.min, MAX))
            dve.tensor_scalar(t16, rr, 0.5, None, MUL).then_inc(s5_ang, 1)
            dve.tensor_tensor(den, lamr, lamr, MUL)
            chain(dve.tensor_tensor(th, lami, lami, MUL))
            chain(dve.tensor_tensor(den, den, th, ADD))
            chain(dve.reciprocal(den, den))
            dve.wait_ge(s5_mag, 3)
            mag = par16[:, 0, :]
            chain(dve.tensor_tensor(s2, s2, s2, MUL))
            chain(dve.tensor_scalar(ar1, s2, -2.0, 1.0, MUL, ADD))
            dve.tensor_tensor(aim, mag, s1, MUL)
            chain(dve.tensor_tensor(ar1, ar1, mag, MUL))
            chain(dve.tensor_scalar(ar1, ar1, 1.0, None, SUB))
            dve.tensor_tensor(th, ar1, lamr, MUL)
            chain(dve.tensor_tensor(s1, aim, lami, MUL))
            chain(dve.tensor_tensor(th, th, s1, ADD))
            dve.tensor_tensor(par16[:, 1, :], th, den, MUL)
            chain(dve.tensor_tensor(s1, aim, lamr, MUL))
            chain(dve.tensor_tensor(s2, ar1, lami, MUL))
            chain(dve.tensor_tensor(s1, s1, s2, SUB))
            dve.tensor_tensor(par16[:, 2, :], s1, den, MUL)
            chain(dve.tensor_scalar(rr, rr, 1 / TWO_PI, None, MUL))
            chain(dve.tensor_scalar(par16[:, 3, :], rr, ROUND16, ROUND16, ADD, SUB))
            dve.tensor_tensor(par16[:, 4, :], rr, par16[:, 3, :], SUB).then_inc(s5_par, 1)
            dve.wait_ge(par_ps, 1)
            chain(dve.tensor_copy(par.rearrange("p a b -> p (a b)"), ps[:, 0, 0:5 * NJ]))
            dve.wait_ge(prow_ps, 1)
            dve.tensor_copy(params[:, :], ps[:, 0, 128:232]).then_inc(params_sb, 1)
            dve.wait_ge(bias_ps, 1)
            dve.tensor_copy(biasrow, ps[0:AH, 1, 0:GW]).then_inc(bias_row_sb, 1)
            def perp(k):
                return par[:, k, :].unsqueeze(2).to_broadcast([P, NJ, 32])
            tv = cst[:, C_T:C_T + 32].unsqueeze(1).to_broadcast([P, NJ, 32])
            chain(dve.tensor_tensor(ph, perp(3), tv, MUL))
            for step in range(2):
                chain(dve.tensor_scalar(pr, ph, ROUND, ROUND, ADD, SUB))
                chain(dve.tensor_tensor(ph, ph, pr, SUB))
                if step == 0:
                    chain(dve.tensor_tensor(pr, perp(4), tv, MUL))
                    chain(dve.tensor_tensor(ph, ph, pr, ADD))
            dve.sem_inc(ph_done, 1)
            xt_lower(dve, "x", (4, 5, 6, 7))
            for s in range(0, 4):
                lo(dve, s)
            dve.wait_ge(wb_split, 1)
            dve.tensor_tensor(wbl[:, :, :], wba[:, :, :], wbh[:, :, :].bitcast(f32), SUB).then_inc(wb_split, 1)
            dve.wait_ge(s_b, 32)
            dve.wait_ge(s_zero, 2)

            def coef(k):
                return par[:, k, :].unsqueeze(2).to_broadcast([P, NJ, SH])
            for r, (b1, b2, op) in enumerate(((bre, bim, SUB), (bim, bre, ADD))):
                dve.tensor_tensor(btmp, coef(1), b1, MUL)
                chain(dve.tensor_tensor(btm2, coef(2), b2, MUL))
                for g in range(2):
                    rows = slice(SN * g, SN * g + SN)
                    ins = dve.tensor_tensor(bpad[rows, r, :, SH * g:SH * g + SH], btmp[rows], btm2[rows], op)
                chain(ins)
            dve.sem_inc(b_padded, 1)
            dve.wait_ge(b_ps, 1)
            dve.tensor_copy(bT.rearrange("p a b c -> p (a b c)"), psq(2, 2)).then_inc(bT_sb, 1)
            dve.wait_ge(c_ps, 1)
            dve.tensor_copy(cT[:, 0].rearrange("p b c -> p (b c)"), psq(0))
            dve.tensor_scalar(cT[:, 1].rearrange("p b c -> p (b c)"), psq(1), -1.0, None, MUL).then_inc(cT_sb, 1)

            def rotate(q):
                tc, ts_ = tcos[:, q % 2], tsin[:, q % 2]
                xre, xim = ps[:, 0:2, 0:SEQ], ps[:, 0:2, SEQ:2 * SEQ]
                dve.wait_ge(x_ps, q + 1)
                dve.wait_ge(tab_ready, q + 1)
                if q >= 1:
                    dve.wait_ge(y_done, q)
                dve.tensor_tensor(pa, xre, tc, MUL)
                dve.tensor_tensor(pb, xim, ts_, MUL)
                dve.tensor_tensor(pc, xim, tc, MUL)
                dve.tensor_tensor(pd, xre, ts_, MUL).then_inc(rot_ready, 1)

            def scans(q):
                dve.wait_ge(rot_done, q + 1)
                if q >= 1:
                    dve.wait_ge(him_ready, q)
                for jj in range(2):
                    decay = par[:, 0, 2 * q + jj:2 * q + jj + 1].to_broadcast([P, SEQ])
                    dve.tensor_tensor_scan(gre[:, jj, :], decay, pa[:, jj, :], 0.0, MUL, ADD)
                    ins = dve.tensor_tensor_scan(gim[:, jj, :], decay, pc[:, jj, :], 0.0, MUL, ADD)
                ins.then_inc(scan_done, 1)
                dve.wait_ge(scan_done, q + 1)

            def unrotate(q):
                tc = tcos[:, q % 2]
                dve.tensor_tensor(pd, tc, gim, MUL).then_inc(unrot_dve, 1)
                dve.tensor_tensor(pa, tc, gre, MUL).then_inc(unrot_dve, 1)
                dve.wait_ge(unrot_dve, 2 * q + 2)
                dve.wait_ge(unrot_half, q + 1)
                dve.tensor_tensor(pa, pa, pb, SUB).then_inc(hre_ready, 1)

            def pair(q):
                rotate(q)
                scans(q)
                unrotate(q)

            def skip_sum(c):
                dve.wait_ge(y_done, 2 * c + 2)
                dve.scalar_tensor_tensor(yT[:, c, :], uT[:, c, :], params[:, 96 + c:97 + c],
                                         ps[:, 6 + c % 2, 0:SEQ], MUL, ADD).then_inc(y_sum, 1)

            for s in range(4, 10):
                lo(dve, s)
            pair(0)
            lo(dve, 10)
            lo(dve, 11)
            pair(1)
            for s in range(12, 16):
                lo(dve, s)
            pair(2)
            skip_sum(0)
            pair(3)
            for s in range(GLU, GLU + 4):
                lo(dve, s)

            def head(h):
                dve.wait_ge(att_sc, h + 1)
                dve.reduce_max(att_nm[:, 2 * h:2 * h + 1], ps[:, 4, 0:P], AX.X)
                chain(dve.reduce_max(att_nm[:, 2 * h + 1:2 * h + 2], ps[:, 4, P:GW], AX.X))
                dve.tensor_scalar(att_nm[:, 2 * h:2 * h + 2], att_nm[:, 2 * h:2 * h + 2], -1.0, None,
                                  MUL).then_inc(att_max, 1)

            for q in range(4, 8):
                head(2 * (q - 4))
                pair(q)
                head(2 * (q - 4) + 1)
                if q % 2 == 0:
                    skip_sum(q // 2 - 1)
            skip_sum(3)

            dve.wait_ge(att_exp, AH)
            chain(dve.reciprocal(att_rs.rearrange("p a b -> p (a b)"), att_sum.rearrange("p a b -> p (a b)")))
            dve.wait_ge(att_o, AH)
            for m in range(TM):
                dve.tensor_tensor(stage[:, 1, m, :].rearrange("p (h d) -> p h d", h=AH),
                                  ps[:, 2 + m, :].rearrange("p (h d) -> p h d", h=AH),
                                  att_rs[:, m, :].unsqueeze(2).to_broadcast([P, AH, AD]),
                                  MUL).then_inc(att_rows, 1)
            xt_lower(dve, "att", (4, 5), n=2)
            for c in range(4):
                dve.wait_ge(gelu_hi, c + 1)
                dve.tensor_tensor(fl[:, c, :], yT[:, c, :], fh[:, c, :].bitcast(f32), SUB).then_inc(gelu_lo, 1)
            for c in range(4):
                dve.wait_ge(z_sig, c + 1)
                dve.tensor_tensor(yT[:, c, :], yT[:, c, :], zs[:, c, :], MUL).then_inc(ssm_rows, 1)
            for c in range(4):
                dve.wait_ge(ssm_hi, c + 1)
                dve.tensor_tensor(xl[:, 4 + c, :], yT[:, c, :], xh[:, 4 + c, :].bitcast(f32), SUB).then_inc(ssm_lo, 1)
            for s in range(EV_OUT + 2, EV_OUT + 8):
                lo(dve, s)
            ln_stats(dve, 0, chain)
            ln_apply(dve, 0, chain)
            for s in range(MLP_A, MLP_A + 4):
                lo(dve, s)
            xt_lower(dve, "ln0", (4, 5, 6, 7))

            def ht_lower(layer, i=0, j0=0):
                for q in range(2):
                    dve.wait_ge(ht_hi, 2 * (FB * layer + j0) + q + 1 + 2 * i)
                    dve.tensor_tensor(fl[:, 2 * q:2 * q + 2, :],
                                      ps[:, 6 + q, :].rearrange("p (a b) -> p a b", a=2),
                                      fh[:, 2 * q:2 * q + 2, :].bitcast(f32), SUB).then_inc(ht_lo, 1)

            def mlp(base, layer):
                for k in range(4, 8):
                    lo(dve, base + k)
                with dve.Fori(0, FB - 1) as j:
                    lo(dve, base + 8, j)
                    lo(dve, base + 9, j)
                    ht_lower(layer, j)
                    lo(dve, base + 10, j)
                    lo(dve, base + 11, j)
                    for k in range(12, 16):
                        lo(dve, base + k, j)
                ht_lower(layer, 0, FB - 1)

            mlp(MLP_A, 0)
            ln_stats(dve, 1, chain)
            ln_apply(dve, 1, chain)

            for s in range(OD_IN, OD_IN + 4):
                lo(dve, s)
            xt_lower(dve, "ln1", (4, 5, 6, 7))
            dve.wait_ge(ba_ps, 1)
            dve.wait_ge(s_l1, 48)
            ba = ps[:, 1, 0:32].rearrange("p (m c) -> p m c", m=TM)
            dve.tensor_copy(ba_b, ba[:, :, 0:CH]).then_inc(ba_sb, 1)
            chain(dve.tensor_tensor(sm[XG], ba[:, :, CH:2 * CH],
                                    dtb[:, :].unsqueeze(1).to_broadcast([P, TM, CH]), ADD))
            chain(dve.tensor_scalar(sm[AXX], sm[XG], -1.0, None, MUL))
            dve.tensor_tensor(sm[AXX], sm[AXX], sm[XG], MAX).then_inc(ba_sb, 1)

            def conv(g):
                dve.wait_ge(t1_ps, g + 1)
                c0 = OD_COLS[g] // P
                for tap in range(CONV - 1, -1, -1):
                    d = CONV - 1 - tap
                    for c in range(4):
                        w = params[:, 24 * tap + c0 + c:24 * tap + c0 + c + 1]
                        src = ps[:, 2 + c // 2, (c % 2) * SEQ:(c % 2) * SEQ + SEQ - d]
                        o = convT[:, 4 * g + c, d:SEQ]
                        if d == 0:
                            ins = dve.tensor_scalar(o, src, w, None, MUL)
                        else:
                            ins = dve.scalar_tensor_tensor(o, src, w, o, MUL, ADD)
                    if tap:
                        chain(ins)
                ins.then_inc(conv_done, 1)

            for g in range(8):
                for k in range(4):
                    lo(dve, OD_IN + 4 * (g + 1) + k)
                if 1 <= g <= 6:
                    conv(g - 1)

            dve.wait_ge(gate_exp, 3)
            chain(dve.tensor_scalar(sm[BETA], sm[BETA], 1.0, None, ADD))
            dve.reciprocal(sm[BETA], sm[BETA])
            dve.tensor_scalar(sm[W1], sm[E1], 1.0, None, ADD).then_inc(ba_sb, 1)
            dve.wait_ge(ba_sb, 3)
            chain(dve.tensor_scalar(sm[DD], sm[W1], 1.0, None, SUB))
            chain(dve.tensor_scalar(sm[EQ], sm[DD], 0.0, None, ALU.is_equal))
            chain(dve.tensor_tensor(sm[DD], sm[DD], sm[EQ], ADD))
            chain(dve.reciprocal(sm[DD], sm[DD]))
            chain(dve.tensor_tensor(sm[E1], sm[E1], sm[DD], MUL))
            dve.wait_ge(gate_exp, 4)
            chain(dve.tensor_tensor(sm[LW], sm[LW], sm[EQ], ADD))
            chain(dve.tensor_tensor(sm[E1], sm[E1], sm[LW], MUL))
            chain(dve.scalar_tensor_tensor(sm[GR], sm[XG], 0.0, sm[E1], MAX, ADD))
            dve.scalar_tensor_tensor(sm[GR], sm[GR], -1.0, alog[:, :].unsqueeze(1).to_broadcast([P, TM, CH]),
                                     MUL, MUL).then_inc(g_ready, 1)
            dve.wait_ge(ss_ps, 4)
            ss = ps[:, 0, 0:32].rearrange("p (c m) -> p m c", m=TM)
            chain(dve.tensor_scalar(sm[SSK], ss[:, :, 0:CH], L2_EPS, None, ADD))
            chain(dve.reciprocal(sm[IK], sm[SSK]))
            chain(dve.tensor_scalar(sm[SSQ], ss[:, :, CH:2 * CH], L2_EPS, None, ADD))
            chain(dve.reciprocal(sm[SSQ], sm[SSQ]))
            chain(dve.tensor_tensor(sm[BRK2], sm[BETA], sm[IK], MUL))
            dve.sem_inc(norm_in, 1)
            dve.wait_ge(cum_ps, 1)
            chain(dve.tensor_copy(sm[GC], ps[:, 1, 32:48].rearrange("p (a b) -> p a b", a=2)))
            dve.tensor_tensor(sm[EKD], ps[:, 1, 48:64].rearrange("p (a b) -> p a b", a=2), sm[GC],
                              SUB).then_inc(ba_sb, 1)
            negm = cst[:, C_NEG:C_NEG + P]
            dve.wait_ge(norm_out, 3)
            for b in range(4):
                m, h0, base = b // 2, 4 * (b % 2), 2 + 3 * (b % 2)
                dve.wait_ge(kk_ps, b + 1)
                for h in range(4):
                    ins = dve.scalar_tensor_tensor(dec[:, h, :], ps[:, base, h * P:h * P + P],
                                                   sm[GC][:, m, h0 + h:h0 + h + 1], negm, SUB, ADD)
                ins.then_inc(dec_in, 1)
                dve.wait_ge(dec_ready, b + 1)
                for h in range(4):
                    dve.scalar_tensor_tensor(intraT[:, m, h0 + h, :], ps[:, base + 2, h * P:h * P + P],
                                             sm[RK][:, m, h0 + h:h0 + h + 1], dec[:, h, :], MUL, MUL)
                for h in range(4):
                    ins = dve.scalar_tensor_tensor(NT[:, m, h0 + h, :], ps[:, base + 1, h * P:h * P + P],
                                                   sm[BRK2][:, m, h0 + h:h0 + h + 1], dec[:, h, :], MUL, MUL)
                chain(ins)
                dve.sem_inc(nt_ready, 1)

            dve.wait_ge(cum_exp, 3)

            def rowb(v, m):
                return v[:, m, :].unsqueeze(2).to_broadcast([P, CH, CD])
            chain(dve.tensor_tensor(sm[BRK], sm[BETA], sm[RK], MUL))
            chain(dve.tensor_tensor(sm[EKD], sm[EKD], sm[RK], MUL))
            chain(dve.tensor_scalar(sm[NEGEG], sm[EG], -1.0, None, MUL))
            chain(dve.tensor_scalar(sm[RQ], sm[RQ], CD ** -0.5, None, MUL))
            for m in range(TM):
                dve.wait_ge(rows_ps, 2 * m + 1)
                dve.tensor_tensor(dv[:, m], psq(4, 2).rearrange("p (a b) -> p a b", a=CH),
                                  rowb(sm[DINV], m), MUL).then_inc(rows_sb, 1)
                dve.wait_ge(rows_ps, 2 * m + 2)
                kr = psq(6, 2).rearrange("p (a b) -> p a b", a=CH)
                dve.tensor_tensor(kw[:, m], kr, rowb(sm[NEGEG], m), MUL)
                dve.tensor_tensor(kdec[:, m], kr, rowb(sm[EKD], m), MUL).then_inc(rows_sb, 1)

            dve.wait_ge(t_init, 1)
            for lev in range(LEVELS):
                mask = cst[:, C_LVL + lev * P:C_LVL + lev * P + P].unsqueeze(1).to_broadcast([P, 4, P])
                for b in range(4):
                    m, h0, n = b // 2, 4 * (b % 2), 4 * lev + b
                    dve.wait_ge(nt_ps, n + 1)
                    if n >= 2:
                        dve.wait_ge(tx_ps, n - 1)
                    dve.tensor_tensor(XX[:, b % 2], ps[:, b % 2, :].rearrange("p (a b) -> p a b", a=4), mask,
                                      MUL).then_inc(xx_ready, 1)
                    if b >= 1:
                        inverse_step(dve, lev, b - 1, chain)
                inverse_step(dve, lev, 3, chain)

            for n in range(4):
                m, rows = n // 2, slice(CK * (n % 2), CK * (n % 2) + CK)
                dve.wait_ge(v_ps, n + 1)
                dve.tensor_tensor(vnew[rows, m], psq(0, 2)[rows].rearrange("p (a b) -> p a b", a=CH),
                                  sm[BRK][rows, m, :].unsqueeze(2).to_broadcast([CK, CH, CD]),
                                  MUL).then_inc(vnew_done, 1)
                if n < 3:
                    s4 = S[n + 1]
                    if n:
                        chain(dve.tensor_tensor(s4, S[n], egl[:, n, :].unsqueeze(2).to_broadcast([P, CH, CD]), MUL))
                    dve.wait_ge(kv_ps, n + 1)
                    kv = psq(2, 2).rearrange("p (a b) -> p a b", a=CH)
                    if n:
                        dve.tensor_tensor(s4, s4, kv, ADD).then_inc(s_ready, 1)
                    else:
                        dve.tensor_copy(s4, kv).then_inc(s_ready, 1)
                if n % 2:
                    rr_ = slice(0, P) if m else slice(CK, P)
                    nr = P if m else CK
                    dve.wait_ge(o2_sb, m + 1)
                    chain(dve.tensor_tensor(osq(m)[rr_].rearrange("p (a b) -> p a b", a=CH),
                                            psq(4, 2)[rr_].rearrange("p (a b) -> p a b", a=CH),
                                            sm[EG][rr_, m, :].unsqueeze(2).to_broadcast([nr, CH, CD]), MUL))
                    chain(dve.tensor_tensor(obuf[rr_], obuf[rr_], osq(m)[rr_], ADD))
                    dve.sem_inc(o_sum, 1)
                    dve.wait_ge(o_sq, m + 1)
                    cc, rq = sm[CC][:, m, :], sm[RQ][:, m, :]
                    chain(dve.reduce_sum(cc, osq(m).rearrange("p (a b) -> p a b", a=CH), AX.X))
                    chain(dve.tensor_tensor(cc, cc, rq, MUL))
                    chain(dve.tensor_tensor(cc, cc, rq, MUL))
                    chain(dve.tensor_scalar(cc, cc, 1.0 / CD, RMS_EPS, MUL, ADD))
                    dve.reciprocal(cc, cc).then_inc(rms_in, 1)
                    dve.wait_ge(rms_out, m + 1)
                    chain(dve.tensor_tensor(cc, cc, rq, MUL))
                    ob3 = obuf.rearrange("p (a b) -> p a b", a=CH)
                    chain(dve.tensor_tensor(ob3, ob3, cc.unsqueeze(2).to_broadcast([P, CH, CD]), MUL))
                    dve.wait_ge(gate_w, 1)
                    dve.tensor_tensor(gate[:, m, :], gate[:, m, :], obuf, MUL).then_inc(o_rows, 1)
            xt_lower(dve, "gdn", (4, 5, 6, 7))
            for s in range(OD_OUT + 4, OD_OUT + 8):
                lo(dve, s)
            ln_stats(dve, 2, chain)
            ln_apply(dve, 2, chain)
            for s in range(MLP_B, MLP_B + 4):
                lo(dve, s)
            xt_lower(dve, "ln2", (4, 5, 6, 7))
            mlp(MLP_B, 1)
            ln_stats(dve, 3, chain)
            ln_apply(dve, 3, chain)

        @block.tensor
        def _(pe):
            left_x, left_f = (xh, xl), (fh, fl)

            def project(g):
                if g >= 1:
                    pe.wait_ge(g_row, TM * g)
                for k in range(4):
                    slab_product(pe, EV_IN + 4 * g + k, (4, 5), left_x, 2 * k, k == 0, k == 3)

            def transpose_rows(g):
                pe.wait_ge(g_row, TM * (g + 1))
                if g >= 1:
                    pe.wait_ge(t_sb, g)
                for c in range(4):
                    for m in range(TM):
                        ins = pe.transpose(ps[:, 2 + c // 2, (c % 2) * SEQ + m * P:(c % 2) * SEQ + m * P + P],
                                           stage[:, g % 2, m, c * P:c * P + P], ident)
                ins.then_inc(t_ps, 1)

            pe.wait_ge(s_cst, 16)
            pe.wait_ge(s_x, 16 * TM)
            xt_transposes(pe, "x", (4, 5, 6, 7), src=xrow)
            pe.wait_ge(s_prow, 48)
            pe.transpose(ps[:, 0, 128:232], prow, ident[0:104, 0:104]).then_inc(prow_ps, 1)
            pe.wait_ge(s_tab, 32)
            pe.wait_ge(pool_ch, 1)
            pe.matmul(ps[0:AH, 1, 0:GW], tab33, hot, start=True, stop=True).then_inc(bias_ps, 1)
            pe.wait_ge(s5_par, 1)
            for k in range(5):
                ins = pe.transpose(ps[:, 0, NJ * k:NJ * k + NJ], par16[:, k, :], ident[0:NJ, 0:NJ])
            ins.then_inc(par_ps, 1)
            pe.wait_ge(xt_lo, 4)
            project(0)
            pe.wait_ge(b_padded, 1)
            for r in range(2):
                for c in range(4):
                    ins = pe.transpose(ps[:, 2 + r, c * P:c * P + P],
                                       bpad[:, r, 4 * c:4 * c + 4, :].rearrange("p a b -> p (a b)"), ident)
            ins.then_inc(b_ps, 1)
            pe.wait_ge(s_cp, 256)
            pe.wait_ge(bias_row_sb, 1)
            pe.wait_ge(params_sb, 1)
            for r in range(2):
                for c in range(4):
                    ins = pe.transpose(ps[:, r, c * P:c * P + P], cpad[:, r, c, :], ident)
            ins.then_inc(c_ps, 1)
            project(1)
            pe.wait_ge(bT_sb, 1)
            transpose_rows(0)

            def inputs(q):
                if q == 0:
                    pe.wait_ge(t_sb, 1)
                    pe.wait_ge(cT_sb, 1)
                else:
                    pe.wait_ge(rot_ready, q)
                c = q // 2
                for jj in range(2):
                    i = 2 * (q % 2) + jj
                    rows = slice(32 * i, 32 * i + 32)
                    for r in range(2):
                        ins = pe.matmul(ps[:, jj, r * SEQ:r * SEQ + SEQ], bT[rows, r, c, :], uT[rows, c, :],
                                        start=True, stop=True)
                ins.then_inc(x_ps, 1)

            def outputs(q):
                c = q // 2
                pe.wait_ge(hre_ready, q + 1)
                pe.wait_ge(him_ready, q + 1)
                if c >= 2:
                    pe.wait_ge(y_sum, c - 1)
                for jj in range(2):
                    i = 2 * (q % 2) + jj
                    o = ps[32 * i:32 * i + 32, 6 + c % 2, 0:SEQ]
                    pe.matmul(o, cT[:, 0, c, 32 * i:32 * i + 32], pa[:, jj, :], start=True, stop=False)
                    ins = pe.matmul(o, cT[:, 1, c, 32 * i:32 * i + 32], pd[:, jj, :], start=False, stop=True)
                ins.then_inc(y_done, 1)

            inputs(0)
            project(2)
            transpose_rows(1)
            inputs(1)
            outputs(0)
            project(3)
            transpose_rows(2)
            outputs(1)
            inputs(2)
            outputs(2)
            inputs(3)
            outputs(3)
            pe.wait_ge(g_row, TM * 4)
            pe.wait_ge(t_sb, 3)
            pe.wait_ge(s_bias_out, 32)

            def scores(h):
                if h >= 1:
                    pe.wait_ge(att_exp, h)
                c, r = h // 2, slice(AD * (h % 2), AD * (h % 2) + AD)
                flip = cst[:, C_FLIP:C_FLIP + P]
                pe.matmul(ps[:, 4, 0:P], flip, bias[:, h, 0:P], start=True, stop=False)
                pe.matmul(ps[:, 4, 0:P], qT[r, c, 0:P], kT[r, c, 0:P], start=False, stop=True)
                pe.matmul(ps[:, 4, P:GW], flip, bias[:, h, P:GW], start=True, stop=False)
                pe.matmul(ps[:, 4, P:GW], qT[r, c, P:SEQ], kT[r, c, :], start=False, stop=True).then_inc(att_sc, 1)

            def weighted(h):
                pe.wait_ge(att_exp, h + 1)
                if h >= 1:
                    pe.wait_ge(att_pt_sb, h)
                for b in range(3):
                    ins = pe.transpose(ps[:, 5, b * P:b * P + P], att_p[:, b * P:b * P + P], ident)
                ins.then_inc(att_pt_ps, 1)
                pe.wait_ge(att_pt_sb, h + 1)
                v = slice(h * AD, h * AD + AD)
                pe.matmul(ps[:, 2, v], att_pt[:, 0:P], vrow[:, 0, v], start=True, stop=True)
                pe.matmul(ps[:, 3, v], att_pt[:, P:2 * P], vrow[:, 0, v], start=True, stop=False)
                pe.matmul(ps[:, 3, v], att_pt[:, 2 * P:GW], vrow[:, 1, v], start=False, stop=True).then_inc(att_o, 1)

            for q in range(4, 8):
                h = 2 * (q - 4)
                scores(h)
                inputs(q)
                weighted(h)
                scores(h + 1)
                outputs(q)
                weighted(h + 1)
            pe.wait_ge(att_rows, TM)
            xt_transposes(pe, "att", (4, 5), srcs=2, src=stage[:, 1])
            pe.wait_ge(gelu_lo, 4)
            pe.wait_ge(lo_ready, GLU + 2)
            for c in range(4):
                o = ps[:, c // 2, (c % 2) * SEQ:(c % 2) * SEQ + SEQ]
                cols = slice(c * P, c * P + P)
                for k in range(4):
                    q, kk = (GLU + k // 2) % SPL, k % 2
                    pe.matmul(o, whi[:, q, kk, cols], fh[:, k, :], start=k == 0, stop=False)
                    pe.matmul(o, whi[:, q, kk, cols], fl[:, k, :], start=False, stop=False)
                    ins = pe.matmul(o, wlo[:, q, kk, cols], fh[:, k, :], start=False, stop=k == 3)
            ins.then_inc(z_ps, 1)
            pe.sem_inc(slab_used, 2)

            def out_product(base, r):
                for n in range(2):
                    for k in range(4):
                        slab_product(pe, base + 4 * n + k, (n, 2 + n), left_x, 2 * k, k == 0, k == 3)

            pe.wait_ge(xt_lo, XT["ln0"])
            pe.wait_ge(ssm_lo, 4)
            out_product(EV_OUT, 0)

            def norm_transposes(r, name):
                pe.wait_ge(ln_done, TM * (r + 1))
                xt_transposes(pe, name, (4, 5, 6, 7), src=xrow)
                pe.wait_ge(xt_lo, XT[name] + 4)

            norm_transposes(0, "ln0")

            def hidden_slabs(base, ks, i=0):
                for k in ks:
                    slab_product(pe, base + k, (4, 5), left_x, 2 * (k % 4), k % 4 == 0, k % 4 == 3, i)

            def hidden_transposes(layer, i=0, j0=0):
                b = FB * layer + j0
                pe.wait_ge(h_row, TM * (b + 1) + TM * i)
                if layer or j0:
                    pe.wait_ge(ht_lo, 2 * b + 2 * i)
                for c in range(4):
                    for m in range(TM):
                        ins = pe.transpose(ps[:, 6 + c // 2, (c % 2) * SEQ + m * P:(c % 2) * SEQ + m * P + P],
                                           stage[:, 0, m, c * P:c * P + P], ident)
                    if c % 2:
                        ins.then_inc(ht_ps, 1)

            def down(base, layer, i=0, j0=0, first=False, last=False):
                pe.wait_ge(ht_lo, 2 * (FB * layer + j0 + 1) + 2 * i)
                for n in range(2):
                    for k in range(2):
                        s = base + 8 * FB - 4 if last else base + 8 * j0 + 8
                        slab_product(pe, s + 2 * n + k,
                                     (n, 2 + n), left_f, 2 * k, first and k == 0, last and k == 1, i)

            def mlp(base, layer):
                r = 2 * layer + 1
                hidden_slabs(base, range(4))

                def step(i, j0, first):
                    pe.wait_ge(h_relu, TM * (FB * layer + j0 + 1) + TM * i)
                    hidden_slabs(base + 8 * j0 + 4, (0, 1), i)
                    hidden_transposes(layer, i, j0)
                    hidden_slabs(base + 8 * j0 + 4, (2, 3), i)
                    down(base, layer, i, j0, first=first)

                step(0, 0, True)
                with pe.Fori(0, FB - 2) as j:
                    step(j, 1, False)
                hidden_transposes(layer, 0, FB - 1)
                down(base, layer, 0, FB - 1, last=True)

            mlp(MLP_A, 0)

            norm_transposes(1, "ln1")
            pe.wait_ge(wb_split, 2)
            for m in range(TM):
                rows = slice(m * P, m * P + P)
                for k in range(KC):
                    o = ps[:, 1, 16 * m:16 * m + 16]
                    pe.matmul(o, xh[:, k, rows], wbh[:, k, :], start=k == 0, stop=False)
                    pe.matmul(o, xh[:, k, rows], wbl[:, k, :], start=False, stop=False)
                    ins = pe.matmul(o, xl[:, k, rows], wbh[:, k, :], start=False, stop=k == KC - 1)
            ins.then_inc(ba_ps, 1)

            def od_project(g):
                b = 4 + 2 * (g % 2)
                if g >= 2:
                    pe.wait_ge(g1_row, TM * (g - 1))
                for k in range(4):
                    slab_product(pe, OD_IN + 4 * g + k, (b, b + 1), left_x, 2 * k, k == 0, k == 3)

            def od_transposes(g):
                pe.wait_ge(g1_row, TM * (g + 1))
                if g:
                    pe.wait_ge(conv_done, g)
                for c in range(4):
                    for m in range(TM):
                        ins = pe.transpose(ps[:, 2 + c // 2, (c % 2) * SEQ + m * P:(c % 2) * SEQ + m * P + P],
                                           stage[:, g % 2, m, c * P:c * P + P], ident)
                ins.then_inc(t1_ps, 1)

            one = cst[:, C_ONE:C_ONE + 1]

            def lengths(g):
                pe.wait_ge(sq_done, g + 1)
                for c in range(4):
                    for m in range(TM):
                        i = 2 * (4 * g + c) + m
                        ins = pe.matmul(ps[:, 0, i:i + 1], sqT[:, c, m * P:m * P + P], one, start=True, stop=True)
                ins.then_inc(ss_ps, 1)

            for g in range(8):
                od_project(g)
                if 1 <= g <= 6:
                    od_transposes(g - 1)
                if 3 <= g <= 6:
                    lengths(g - 3)

            up, same = cst[:, C_UP:C_UP + P], cst[:, C_SAME:C_SAME + P]
            pe.wait_ge(g_ready, 1)
            for m in range(TM):
                gr = sm[GR][:, m, :]
                pe.matmul(ps[:, 1, 32 + 8 * m:40 + 8 * m], up, gr, start=True, stop=True)
                pe.matmul(ps[:, 1, 48 + 8 * m:56 + 8 * m], same, gr, start=True, stop=True)
                for c in range(2):
                    n = 2 * m + c
                    ins = pe.matmul(ps[:, 1, 64 + 8 * n:72 + 8 * n], cst[:, C_CH + c * P:C_CH + c * P + P], gr,
                                    start=True, stop=True)
            ins.then_inc(cum_ps, 1)
            pe.wait_ge(g1_row, TM * 8)
            for b in range(4):
                m, h0, base = b // 2, 4 * (b % 2), 2 + 3 * (b % 2)
                rows = slice(m * P, m * P + P)
                if b >= 2:
                    pe.wait_ge(nt_ready, b - 1)
                for h in range(4):
                    c = slice(h * P, h * P + P)
                    pe.matmul(ps[:, base, c], sm[GR][:, m, h0 + h:h0 + h + 1].to_broadcast([P, P]), up,
                              start=True, stop=True)
                    pe.matmul(ps[:, base + 1, c], kTd[:, h0 + h, rows], kTd[:, h0 + h, rows], start=True, stop=True)
                    ins = pe.matmul(ps[:, base + 2, c], kTd[:, h0 + h, rows], qTd[:, h0 + h, rows],
                                    start=True, stop=True)
                ins.then_inc(kk_ps, 1)
            pe.wait_ge(nt_ready, 4)
            pe.wait_ge(v_silu, 2)
            for m in range(TM):
                for v, src in ((0, vTd), (1, kTd)):
                    if m:
                        pe.wait_ge(rows_sb, 2 * m - 1 + v)
                    for h in range(CH):
                        ins = pe.transpose(ps[:, 4 + 2 * v + h // 4, (h % 4) * P:(h % 4) * P + P],
                                           src[:, h, m * P:m * P + P], ident)
                    ins.then_inc(rows_ps, 1)
            pe.wait_ge(t_init, 1)

            def level_first(lev, b):
                m, h0, n = b // 2, 4 * (b % 2), 4 * lev + b
                if n >= 4:
                    pe.wait_ge(t_done, n - 3)
                if n >= 2:
                    pe.wait_ge(xx_ready, n - 1)
                for h in range(4):
                    ins = pe.matmul(ps[:, b % 2, h * P:h * P + P], NT[:, m, h0 + h, :], T[:, m, h0 + h, :],
                                    start=True, stop=True)
                ins.then_inc(nt_ps, 1)

            def level_second(lev, b):
                m, h0, n = b // 2, 4 * (b % 2), 4 * lev + b
                pe.wait_ge(xx_ready, n + 1)
                if n >= 1:
                    pe.wait_ge(t_done, n)
                for h in range(4):
                    c = slice(h * P, h * P + P)
                    pe.matmul(ps[:, 2, c], TT[:, m, h0 + h, :], XX[:, b % 2, h, :], start=True, stop=True)
                    ins = pe.matmul(ps[:, 3, c], XX[:, b % 2, h, :], TT[:, m, h0 + h, :], start=True, stop=True)
                ins.then_inc(tx_ps, 1)

            for lev in range(LEVELS):
                level_first(lev, 0)
                for b in range(4):
                    if b < 3:
                        level_first(lev, b + 1)
                    level_second(lev, b)
            pe.wait_ge(t_done, 4 * LEVELS)
            pe.wait_ge(rows_sb, 4)
            for b in range(4):
                m, h0 = b // 2, 4 * (b % 2)
                for h in range(4):
                    ins = pe.matmul(ps[:, 4 + b, h * P:h * P + P], kw[:, m, h0 + h, :], TT[:, m, h0 + h, :],
                                    start=True, stop=True)
                ins.then_inc(wt_ps, 1)
            pe.wait_ge(wt_sb, 4)
            for n in range(4):
                m, par_ = n // 2, n % 2
                rows = slice(CK * par_, CK * par_ + CK)
                for h in range(CH):
                    o = ps[rows, h // 4, (h % 4) * P:(h % 4) * P + P]
                    if n and h == 0:
                        pe.wait_ge(s_ready, n)
                        pe.wait_ge(vnew_done, n)
                    ins = pe.matmul(o, TT[:, m, h, rows], dv[:, m, h, :], start=True, stop=n == 0)
                    if n:
                        ins = pe.matmul(o, WT[:, m, h, rows], S[n][:, h, :], start=False, stop=True)
                ins.then_inc(v_ps, 1)
                if n:
                    if n == 2:
                        pe.wait_ge(o_sum, 1)
                    for h in range(CH):
                        ins = pe.matmul(ps[rows, 4 + h // 4, (h % 4) * P:(h % 4) * P + P],
                                        qTd[:, h, CK * n:CK * n + CK], S[n][:, h, :], start=True, stop=True)
                pe.wait_ge(vnew_done, n + 1)
                if n < 3:
                    for h in range(CH):
                        ins = pe.matmul(ps[:, 2 + h // 4, (h % 4) * P:(h % 4) * P + P], kdec[rows, m, h, :],
                                        vnew[rows, m, h, :], start=True, stop=True)
                    ins.then_inc(kv_ps, 1)
                if par_:
                    for h in range(CH):
                        ins = pe.matmul(ps[:, 6 + h // 4, (h % 4) * P:(h % 4) * P + P], intraT[:, m, h, :],
                                        vnew[:, m, h, :], start=True, stop=True)
                    ins.then_inc(o2_ps, 1)
            pe.wait_ge(o_rows, TM)
            xt_transposes(pe, "gdn", (4, 5, 6, 7), src=gate)
            pe.wait_ge(xt_lo, XT["gdn"] + 4)
            out_product(OD_OUT, 2)
            norm_transposes(2, "ln2")
            mlp(MLP_B, 1)



def constant_tile():
    import numpy as np
    c = np.zeros((P, C_W), np.float32)
    i, j = np.arange(P)[:, None], np.arange(P)[None, :]
    same = i // CK == j // CK
    c[:, C_ID:C_ID + P] = i == j
    c[:, C_UP:C_UP + P] = same & (i <= j)
    c[:, C_SAME:C_SAME + P] = same
    c[:, C_NEG:C_NEG + P] = np.where(same & (i <= j), 0.0, NEG)
    for lev in range(LEVELS):
        b = 2 ** lev
        c[:, C_LVL + lev * P:C_LVL + lev * P + P] = (i // (2 * b) == j // (2 * b)) & (i // b % 2 == 1) & (j // b % 2 == 0)
    for n in range(2):
        c[:, C_CH + n * P:C_CH + n * P + P] = i // CK == n
    c[:, C_T:C_T + 16] = np.arange(16)
    c[:, C_T + 16:C_T + 32] = 16 * np.arange(16)
    c[:, C_ONE:C_ONE + 2] = 1.0
    c[:, C_FLIP:C_FLIP + P] = i + j == P - 1
    return c


def bucket_rows():
    import numpy as np
    d = 255 - np.arange(GW)
    n = np.maximum(d, 0)
    exact = BUCKETS // 2
    nf = np.maximum(n, 1).astype(np.float32)
    large = exact + (np.log(nf / np.float32(exact)) / np.float32(math.log(128 / exact)) * (BUCKETS - exact)).astype(np.int32)
    bucket = np.where(n < exact, n, np.minimum(large, BUCKETS - 1))
    h = np.zeros((BUCKETS + 1, GW), np.float32)
    h[np.where(d >= 0, bucket, BUCKETS), np.arange(GW)] = 1.0
    return h


_INS = ['x', 'rel_table', 'ev_w_in', 'ev_w_out', 's5_lambda_re', 's5_lambda_im', 's5_b_re', 's5_b_im',
        's5_c_re', 's5_c_im', 's5_d', 's5_log_dt', 's5_w_glu', 's5_b_glu', 'od_w_in', 'od_conv_w',
        'od_a_log', 'od_dt_bias', 'od_norm_w', 'od_w_out', 'ln_mix_g', 'ln_mix_b', 'mlp_w1', 'mlp_w2',
        'ln_ffn_g', 'ln_ffn_b']
_OUTS = [((1, SEQ, DM), 'float32')]


def kernel(**inputs):
    import numpy as _np
    import concourse.bacc as _bacc
    from concourse import mybir as _mybir
    from concourse.bass_utils import run_bass_kernel_spmd as _run

    nc = _bacc.Bacc("TRN2", target_bir_lowering=False, num_devices=1)
    arrays, args = {}, []
    given = {n: inputs[n] for n in _INS} | {"consts": constant_tile(), "onehot": bucket_rows()}
    for name, a in given.items():
        a = _np.ascontiguousarray(a)
        arrays[f"in_{name}_dram"] = a
        args.append(nc.dram_tensor(f"in_{name}_dram", a.shape, _mybir.dt.from_np(a.dtype), kind="ExternalInput").ap())
    for i, (shape, dtype) in enumerate(_OUTS):
        dt = _mybir.dt.from_np(_np.dtype(dtype))
        args.append(nc.dram_tensor(f"out_{i}_dram", shape, dt, kind="ExternalOutput").ap())
    build(nc, *args)
    r = _run(nc, [arrays], core_ids=[0])
    return r.results[0]["out_0_dram"]
```

```python
import math
from contextlib import ExitStack

import concourse.bass as bass
from concourse import mybir

P = 128
SEQ = 256
DM = 1024
TM = SEQ // P
KC = DM // P
NW = 512
AH, AD = 8, 64
AW = AH * AD
SG, SH, SN = 32, 16, 64
SW = SG * SH
NJ = SG // 2
CH, CD, CONV, CK = 8, 128, 4, 64
FF = 4 * DM
FB = FF // NW
ALPHA = 4.0 ** 0.25
LN_EPS, RMS_EPS, L2_EPS = 1e-5, 1e-6, 1e-6
NEG = -1e30
BUCKETS = 32
GW = 384
ROUND = 1.5 * 2.0 ** 23
ROUND16 = 1.5 * 2.0 ** 9
TWO_PI = 2 * math.pi
PI_A, PI_B = 6.28125, 1.9350051879882812e-3
PI_C = TWO_PI - PI_A - PI_B

RAW, SPL = 8, 4
EV_IN, EV_OUT, GLU = 0, 16, 20
MLP_A = 26
OD_IN = MLP_A + 8 * FB
OD_OUT = OD_IN + 32
MLP_B = OD_OUT + 8
SLABS = MLP_B + 8 * FB

C_ID, C_UP, C_SAME, C_NEG, C_LVL = 0, 128, 256, 384, 512
LEVELS = 6
C_CH = C_LVL + LEVELS * P
C_T = C_CH + 2 * P
C_ONE = C_T + 32
C_FLIP = C_ONE + 2
C_PAR = C_FLIP + P
C_W = C_PAR + 2


def build(nc, x, rel_table, ev_w_in, ev_w_out, lam_re, lam_im, b_re, b_im, c_re, c_im, s5_d,
          log_dt, w_glu, b_glu, od_w_in, conv_w, a_log, dt_bias, norm_w, od_w_out,
          ln_mix_g, ln_mix_b, mlp_w1, mlp_w2, ln_ffn_g, ln_ffn_b, consts, onehot, out):
    f32, f32r = mybir.dt.float32, mybir.dt.float32r
    ALU, ACT, AX = mybir.AluOpType, mybir.ActivationFunctionType, mybir.AxisListType
    MUL, ADD, SUB, MAX = ALU.mult, ALU.add, ALU.subtract, ALU.max

    ctx = ExitStack()
    with ctx:
        def sb(name, shape, dt=f32):
            return ctx.enter_context(nc.sbuf_tensor(name, shape, dt))

        def sem(name):
            return ctx.enter_context(nc.semaphore(name))

        raw = sb("raw", [P, RAW, 2, NW])
        whi = sb("whi", [P, SPL, 2, NW], f32r)
        wlo = sb("wlo", [P, SPL, 2, NW], f32r)
        xrow = sb("xrow", [P, TM, DM])
        xh = sb("xh", [P, KC, SEQ], f32r)
        xl = sb("xl", [P, KC, SEQ], f32r)
        fh = sb("fh", [P, 4, SEQ], f32r)
        fl = sb("fl", [P, 4, SEQ], f32r)
        stage = sb("stage", [P, 2, TM, NW])
        cst = sb("cst", [P, C_W])
        lnp = sb("lnp", [P, 2, DM])
        lns = sb("lns", [P, TM, 2, 6])
        lnm = sb("lnm", [P, TM, 2])
        lnr = sb("lnr", [P, TM])
        arena = sb("arena", [P, 22000])
        ps = ctx.enter_context(nc.psum_tensor("ps", [P, 8, NW], f32))

        ident = cst[:, C_ID:C_ID + P]

        class Carve:
            def __init__(self):
                self.at = 0

            def __call__(self, *shape, rows=P):
                n = int(math.prod(shape))
                v = arena[0:rows, self.at:self.at + n]
                self.at += n
                if len(shape) == 1:
                    return v
                names = "abcd"[:len(shape)]
                return v.rearrange(f"p ({' '.join(names)}) -> p {' '.join(names)}",
                                   **dict(zip(names, shape)))

        A = Carve()
        uT, qT, kT = A(4, SEQ), A(4, SEQ), A(4, SEQ)
        vrow = A(TM, AW)
        bias = A(AH, GW)
        tab33 = A(AH, rows=BUCKETS + 1)
        att_s, att_p, att_pt = A(GW), A(GW), A(GW)
        hot, biasrow = att_s[0:BUCKETS + 1], att_p[0:AH]
        att_nm, att_sum, att_rs = A(2 * AH), A(TM, AH), A(TM, AH)
        prow = A(P, rows=104)
        yT, zs = A(4, SEQ), A(4, SEQ)
        early1 = stage[:, 1].rearrange("p a b -> p (a b)")
        lamr, lami, lrd, th, nn, rr, den, s1 = (early1[0:NJ, P * k:P * k + P] for k in range(8))
        s2, aim, ar1, t16 = (yT.rearrange("p a b -> p (a b)")[0:NJ, P * k:P * k + P] for k in range(4))
        par16 = zs.rearrange("p a b -> p (a b)")[0:NJ, 0:5 * P].rearrange("p (a b) -> p a b", a=5)
        ldt = A(2, rows=NJ)
        par = A(5, NJ)
        ph, pr = A(NJ, 32), A(NJ, 32)
        sint, cost = A(NJ, 32), A(NJ, 32)
        bre, bim, btmp, btm2 = (vrow.rearrange("p a b -> p (a b)")[:, 256 * k:256 * k + 256]
                                .rearrange("p (a b) -> p a b", a=NJ) for k in range(4))
        craw = kT.rearrange("p a b -> p (a b)")[:, 0:2 * 4 * SN].rearrange("p (a b c) -> p a b c", a=2, b=4)
        bpad = lnp[:, 0, :].rearrange("p (a b c) -> p a b c", a=2, b=NJ)
        bT = A(2, 4, P)
        cpad = lnp[:, 1, :].rearrange("p (a b c) -> p a b c", a=2, b=4)
        cT = A(2, 4, P)
        tcos, tsin, ttmp = A(2, 2, SEQ), A(2, 2, SEQ), A(2, SEQ)
        pa, pb, pc, pd = A(2, SEQ), A(2, SEQ), A(2, SEQ), A(2, SEQ)
        gre, gim = A(2, SEQ), A(2, SEQ)
        hre, him = A(2, SEQ), A(2, SEQ)
        sre, sim = (v.rearrange("p a b -> p (a b)").rearrange("p (a b) -> p a b", a=2) for v in (pr, ph))
        params = sb("params", [P, 104])
        half_pi = sb("half_pi", [P, 1])

        A = Carve()
        convT = A(24, SEQ)
        kTd, qTd, vTd = convT[:, 0:8, :], convT[:, 8:16, :], convT[:, 16:24, :]
        gate = A(TM, DM)
        dv, kw, kdec = A(TM, CH, CD), A(TM, CH, CD), A(TM, CH, CD)
        NT, intraT = A(TM, CH, P), A(TM, CH, P)
        TT = A(TM, CH, P)
        T = vTd.rearrange("p a (b c) -> p (a b) c", b=2).rearrange("p (m h) c -> p m h c", m=TM)
        XX = lnp[:, 0, :].rearrange("p (a b c) -> p a b c", a=2, b=4)
        dec = A(4, P)
        SM = A(24, TM, CH)
        sm = [SM[:, i] for i in range(24)]
        (BETA, XG, AXX, E1, W1, LW, DD, EQ, GR, EG, NEGEG, EKD, GC, IK, RK, DINV, SSK, SSQ, RQ, BRK2,
         BRK, CC, BB) = range(23)
        ba_b = sm[BB]
        WT = T
        vnew = kw
        S = [None, NT[:, 0], NT[:, 1], lnp[:, 1, :].rearrange("p (a b) -> p a b", a=CH)]
        obuf = XX.rearrange("p a b c -> p (a b c)")
        sqT = kdec[:, 0].rearrange("p a b -> p (a b)").rearrange("p (a b) -> p a b", a=4)

        def osq(m):
            return intraT[:, m].rearrange("p a b -> p (a b)")

        wba = sb("wba", [P, KC, 16])
        nw = sb("nw", [P, CD])
        wbh = sb("wbh", [P, KC, 16], f32r)
        wbl = sb("wbl", [P, KC, 16], f32r)
        alog = sb("alog", [P, CH])
        dtb = sb("dtb", [P, CH])
        egl = sb("egl", [P, 4, CH])
        scratch = nc.dram_tensor("bias_rows", [AH, GW], f32, kind="Internal").ap()

        loaded = [sem(f"slab_loaded{i}") for i in range(RAW)]
        hi_ready = sem("hi_ready")
        lo_ready = sem("lo_ready")
        slab_used = sem("slab_used")
        s_x = [sem(f"x_loaded{m}") for m in range(TM)]
        acc_ready = sem("acc_ready")
        s_cst, s_small, s_lnp = sem("consts_loaded"), sem("small_loaded"), sem("lnp_loaded")
        s_bias_in, s_bias_out = sem("bias_rows_stored"), sem("bias_loaded")
        s_out = sem("out_stored")
        s_l1 = sem("layer1_small_loaded")
        s_zero, s_c, c_padded, s_ident = sem("pads_cleared"), sem("c_loaded"), sem("c_padded"), sem("ident_loaded")
        dve_ch, act_ch, pool_ch = sem("dve_chain"), sem("act_chain"), sem("pool_chain")
        xt_ps, xt_hi, xt_lo = sem("xt_in_psum"), sem("xt_hi"), sem("xt_lo")
        ln_var, ln_rstd, ln_done = sem("ln_var"), sem("ln_rstd"), sem("ln_done")
        h_row, ht_ps, ht_hi, ht_lo = sem("h_rows"), sem("ht_in_psum"), sem("ht_hi"), sem("ht_lo")
        g_row, t_ps, t_sb = sem("proj_rows"), sem("projT_in_psum"), sem("projT")

        s_tab, s_prow, s_b, s_wba, wb_split = (
            sem("s_tab"), sem("s_prow"), sem("s_b"), sem("s_wba"), sem("wb_split"))
        tab_ready, phases_ready, rot_ready, rot_done, scan_done = (
            sem("tab_ready"), sem("phases_ready"), sem("rot_ready"), sem("rot_done"), sem("scan_done"))
        unrot_sin, unrot_cos, states_ready, h_relu = (
            sem("unrot_sin"), sem("unrot_cos"), sem("states_ready"), sem("h_relu"))
        t_init, gate_w, s5_dt, s5_ang, s5_mag = (
            sem("t_init"), sem("gate_w"), sem("s5_dt"), sem("s5_ang"), sem("s5_mag"))
        s5_par, par_ps, prow_ps, bias_ps, bias_row_sb = (
            sem("s5_par"), sem("par_ps"), sem("prow_ps"), sem("bias_ps"), sem("bias_row_sb"))
        params_sb, ph_done, b_padded, b_ps, bT_sb = (
            sem("params_sb"), sem("ph_done"), sem("b_padded"), sem("b_ps"), sem("bT_sb"))
        c_ps, cT_sb, x_ps, y_done, y_sum = (
            sem("c_ps"), sem("cT_sb"), sem("x_ps"), sem("y_done"), sem("y_sum"))
        gelu_hi, gelu_lo, z_ps, z_sig, ssm_rows = (
            sem("gelu_hi"), sem("gelu_lo"), sem("z_ps"), sem("z_sig"), sem("ssm_rows"))
        ssm_hi, ssm_lo, att_sc, att_max, att_exp = (
            sem("ssm_hi"), sem("ssm_lo"), sem("att_sc"), sem("att_max"), sem("att_exp"))
        att_pt_ps, att_pt_sb, att_o, att_rows, conv_done = (
            sem("att_pt_ps"), sem("att_pt_sb"), sem("att_o"), sem("att_rows"), sem("conv_done"))
        sq_done, ss_ps, v_silu, t1_ps, g1_row = (
            sem("sq_done"), sem("ss_ps"), sem("v_silu"), sem("t1_ps"), sem("g1_row"))
        ba_ps, ba_sb, gate_exp, cum_ps, cum_exp = (
            sem("ba_ps"), sem("ba_sb"), sem("gate_exp"), sem("cum_ps"), sem("cum_exp"))
        g_ready, dec_in, dec_ready, norm_in, norm_out = (
            sem("g_ready"), sem("dec_in"), sem("dec_ready"), sem("norm_in"), sem("norm_out"))
        kk_ps, nt_ready, rows_ps, rows_sb, nt_ps = (
            sem("kk_ps"), sem("nt_ready"), sem("rows_ps"), sem("rows_sb"), sem("nt_ps"))
        xx_ready, tx_ps, t_done, wt_ps, wt_sb = (
            sem("xx_ready"), sem("tx_ps"), sem("t_done"), sem("wt_ps"), sem("wt_sb"))
        v_ps, vnew_done, kv_ps, s_ready, o2_ps = (
            sem("v_ps"), sem("vnew_done"), sem("kv_ps"), sem("s_ready"), sem("o2_ps"))
        o2_sb, o_sum, o_sq, rms_in, rms_out = (
            sem("o2_sb"), sem("o_sum"), sem("o_sq"), sem("rms_in"), sem("rms_out"))
        o_rows = sem("o_rows")

        block = ctx.enter_context(nc.Block())

        def bc(ap, shape):
            return ap.to_broadcast(shape)

        def psq(b, n=1):
            return ps[:, b:b + n, :].rearrange("p a b -> p (a b)")

        def in_slab(w, col, k):
            return w[256 * k:256 * k + 256, col:col + NW].rearrange("(a p) n -> p a n", p=P)

        EV_COLS = [3 * AW, 0, AW, 2 * AW]
        OD_COLS = [DM, DM + NW, 0, NW, 2 * DM, 2 * DM + NW, 3 * DM, 3 * DM + NW]

        def hi(act, s, i=0):
            act.wait_ge(loaded[s % RAW], 16 * (s // RAW + 1) + 16 * i)
            if s >= SPL:
                act.wait_ge(slab_used, s - SPL + 1 + 8 * i)
            act.activation(whi[:, s % SPL], raw[:, s % RAW], ACT.Copy).then_inc(hi_ready, 1)

        def lo(dve, s, i=0):
            dve.wait_ge(hi_ready, s + 1 + 8 * i)
            dve.tensor_tensor(wlo[:, s % SPL], raw[:, s % RAW], whi[:, s % SPL].bitcast(f32),
                              SUB).then_inc(lo_ready, 1)

        def row_product(pe, s, m, bank, left, k0, first, last):
            lh, ll = left
            q, rows, o = s % SPL, slice(m * P, m * P + P), ps[:, bank, :]
            for kk in range(2):
                a, b = first and kk == 0, last and kk == 1
                pe.matmul(o, lh[:, k0 + kk, rows], whi[:, q, kk, :], start=a, stop=False)
                pe.matmul(o, lh[:, k0 + kk, rows], wlo[:, q, kk, :], start=False, stop=False)
                ins = pe.matmul(o, ll[:, k0 + kk, rows], whi[:, q, kk, :], start=False, stop=b)
            return ins

        def slab_product(pe, s, banks, left, k0, first, last, i=0):
            pe.wait_ge(lo_ready, s + 1 + 8 * i)
            for m in range(TM):
                ins = row_product(pe, s, m, banks[m], left, k0, first, last)
            ins.then_inc(slab_used, 1)

        def four_slabs(pe, s0, m, steps, left, acc=None):
            for k, (bank, k0, first, last) in enumerate(steps):
                if m == 0:
                    pe.wait_ge(lo_ready, s0 + k + 1)
                ins = row_product(pe, s0 + k, m, bank, left, k0, first, last)
                if m == TM - 1:
                    ins.then_inc(slab_used, 1)
                elif acc is not None and last:
                    ins.then_inc(acc, 1)

        def xt_transposes(pe, m, banks, src):
            for q, bank in enumerate(banks):
                for j in range(4):
                    c = 4 * q + j
                    ins = pe.transpose(ps[:, bank, j * P:j * P + P], src[:, m, c * P:c * P + P], ident)
                ins.then_inc(xt_ps, 1)

        XT_X, XT_ATT, XT_LN0, XT_LN1, XT_GDN, XT_LN2 = 0, 4, 6, 10, 14, 18

        def xt_upper(act, at, m, banks):
            for q, bank in enumerate(banks):
                act.wait_ge(xt_ps, at + q + 1)
                act.activation(xh[:, 4 * q:4 * q + 4, m * P:m * P + P],
                               ps[:, bank, :].rearrange("p (a b) -> p a b", a=4), ACT.Copy).then_inc(xt_hi, 1)

        def xt_lower(dve, at, m, banks):
            for q, bank in enumerate(banks):
                dve.wait_ge(xt_hi, at + q + 1)
                dve.tensor_tensor(xl[:, 4 * q:4 * q + 4, m * P:m * P + P],
                                  ps[:, bank, :].rearrange("p (a b) -> p a b", a=4),
                                  xh[:, 4 * q:4 * q + 4, m * P:m * P + P].bitcast(f32), SUB).then_inc(xt_lo, 1)

        SUM_END = (GLU + 6, MLP_A + 8 * FB, OD_OUT + 8, MLP_B + 8 * FB)
        LAST_HALF = (2, 2, 4, 2)

        def ln_stats(dve, r, m, chain):
            for j in range(2):
                if m == 0:
                    dve.wait_ge(acc_ready, 2 * r + j + 1)
                else:
                    dve.wait_ge(slab_used, SUM_END[r] - (LAST_HALF[r] if j == 0 else 0))
                half = xrow[:, m, j * NW:j * NW + NW]
                chain(dve.scalar_tensor_tensor(half, half, ALPHA, ps[:, 2 * m + j, :], MUL, ADD))
                ins = dve.bn_stats(lns[:, m, j, :], half)
            chain(ins)
            chain(dve.bn_aggr(lnm[:, m, :], lns[:, m, :, :]))
            chain(dve.tensor_scalar(lnr[:, m:m + 1], lnm[:, m, 1:2], LN_EPS, None, ADD))
            dve.reciprocal(lnr[:, m:m + 1], lnr[:, m:m + 1]).then_inc(ln_var, 1)

        def ln_sqrt(act, r, m):
            act.wait_ge(ln_var, 2 * r + m + 1)
            act.activation(lnr[:, m:m + 1], lnr[:, m:m + 1], ACT.Sqrt).then_inc(ln_rstd, 1)

        def ln_apply(dve, r, m, chain):
            if m == 0:
                dve.wait_ge(s_lnp, 32 * (r + 1))
            chain(dve.scalar_tensor_tensor(xrow[:, m, :], xrow[:, m, :], lnm[:, m, 0:1], lnp[:, 0, :],
                                           SUB, MUL))
            dve.wait_ge(ln_rstd, 2 * r + m + 1)
            dve.scalar_tensor_tensor(xrow[:, m, :], xrow[:, m, :], lnr[:, m:m + 1], lnp[:, 1, :],
                                     MUL, ADD).then_inc(ln_done, 1)

        def norm_act(act, r, at, s0):
            ln_sqrt(act, r, 0)
            for s in range(s0, s0 + 4):
                hi(act, s)
            xt_upper(act, at, 0, (4, 5))
            ln_sqrt(act, r, 1)
            xt_upper(act, at + 2, 1, (6, 7))

        def norm_dve(dve, r, at, chain):
            ln_stats(dve, r, 0, chain)
            ln_apply(dve, r, 0, chain)
            ln_stats(dve, r, 1, chain)
            xt_lower(dve, at, 0, (4, 5))
            ln_apply(dve, r, 1, chain)
            xt_lower(dve, at + 2, 1, (6, 7))

        def norm_pe(pe, r, at, m):
            pe.wait_ge(ln_done, TM * r + m + 1)
            xt_transposes(pe, m, (4 + 2 * m, 5 + 2 * m), xrow)
            pe.wait_ge(xt_lo, at + 2 * m + 2)

        @block.sync
        def _(sp):
            def load(s, src, i=0):
                if s >= RAW:
                    sp.wait_ge(lo_ready, s - RAW + 1 + 8 * i)
                sp.dma_start(raw[:, s % RAW], src).then_inc(loaded[s % RAW], 16)

            def load_row(s, w, row, col, i=0):
                load(s, w[bass.ds(row, 256), bass.ds(col, NW)].rearrange("(a p) n -> p a n", p=P), i)

            for m in range(TM):
                sp.dma_start(xrow[:, m, :], x[0, m * P:m * P + P, :]).then_inc(s_x[m], 16)
            for g in range(4):
                for k in range(4):
                    load(EV_IN + 4 * g + k, in_slab(ev_w_in[0], EV_COLS[g], k))
            for n in range(2):
                for k in range(2):
                    load(EV_OUT + 2 * n + k, in_slab(ev_w_out[0], n * NW, k))
            for k in range(2):
                load(GLU + k, in_slab(w_glu[0], 0, k))
            for n in range(2):
                for k in range(2):
                    load(GLU + 2 + 2 * n + k, in_slab(ev_w_out[0], n * NW, 2 + k))

            def mlp_loads(base, layer):
                w1, w2 = mlp_w1[layer], mlp_w2[layer]
                for k in range(4):
                    load(base + k, in_slab(w1, 0, k))
                with sp.Fori(0, FB - 1) as j:
                    for k in range(4):
                        load_row(base + 4 + k, w1, 256 * k, NW * j + NW, j)
                    for n in range(2):
                        for k in range(2):
                            load_row(base + 8 + 2 * n + k, w2, NW * j + 256 * k, NW * n, j)
                for n in range(2):
                    for k in range(2):
                        load(base + 8 * FB - 4 + 2 * n + k, in_slab(w2, NW * n, 2 * (FB - 1) + k))

            mlp_loads(MLP_A, 0)
            for g in range(8):
                for k in range(4):
                    load(OD_IN + 4 * g + k, in_slab(od_w_in[0], OD_COLS[g], k))
            for n in range(2):
                for k in range(4):
                    load(OD_OUT + 4 * n + k, in_slab(od_w_out[0], n * NW, k))
            mlp_loads(MLP_B, 1)
            for m in range(TM):
                sp.wait_ge(ln_done, 6 + m + 1)
                sp.dma_start(out[0, m * P:m * P + P, :], xrow[:, m, :]).then_inc(s_out, 16)
            sp.wait_ge(s_out, 16 * TM)


        def chained(eng, s):
            n = [0]

            def chain(ins):
                n[0] += 1
                ins.then_inc(s, 1)
                eng.wait_ge(s, n[0])
            return chain

        def inverse_step(dve, lev, b, chain):
            m, h0, n = b // 2, 4 * (b % 2), 4 * lev + b
            dve.wait_ge(tx_ps, n + 1)
            t, tt = T[:, m, h0:h0 + 4, :], TT[:, m, h0:h0 + 4, :]
            dve.tensor_tensor(t, t, ps[:, 2, :].rearrange("p (a b) -> p a b", a=4), SUB)
            dve.tensor_tensor(tt, tt, ps[:, 3, :].rearrange("p (a b) -> p a b", a=4), SUB).then_inc(t_done, 1)

        @block.gpsimd
        def _(pool):
            chain = chained(pool, pool_ch)
            chain(pool.memset(tab33[BUCKETS:BUCKETS + 1, :], NEG))
            chain(pool.memset(bpad.rearrange("p a b c -> p (a b c)"), 0.0))
            chain(pool.memset(half_pi[:, :], math.pi / 2))
            pool.sem_inc(s_zero, 1)
            pool.wait_ge(s_cst, 32)
            pool.wait_ge(s_c, 32)
            for r in range(2):
                for g in range(2):
                    ins = pool.tensor_scalar(cpad[:, r, :, SN * g:SN * g + SN], craw[:, r],
                                             cst[:, C_PAR + g:C_PAR + g + 1], None, MUL)
            ins.then_inc(c_padded, 1)

            def tables(q):
                j, t = 2 * q, q % 2
                fine = [v[:, j:j + 2, 0:16].unsqueeze(2).to_broadcast([P, 2, 16, 16]) for v in (cost, sint)]
                rough = [v[:, j:j + 2, 16:32].unsqueeze(3).to_broadcast([P, 2, 16, 16]) for v in (cost, sint)]
                tc, ts_, tt = [v.rearrange("p j (a b) -> p j a b", a=16) for v in (tcos[:, t], tsin[:, t], ttmp)]
                if q:
                    pool.wait_ge(tab_ready, q)
                if q >= 2:
                    pool.wait_ge(unrot_cos, q - 1)
                    pool.wait_ge(unrot_sin, q - 1)
                pool.tensor_tensor(tc, rough[0], fine[0], MUL)
                chain(pool.tensor_tensor(tt, rough[1], fine[1], MUL))
                chain(pool.tensor_tensor(tc, tc, tt, SUB))
                pool.tensor_tensor(ts_, rough[1], fine[0], MUL)
                chain(pool.tensor_tensor(tt, rough[0], fine[1], MUL))
                pool.tensor_tensor(ts_, ts_, tt, ADD).then_inc(tab_ready, 1)

            pool.wait_ge(phases_ready, 2)
            tables(0)
            tables(1)
            for q in range(NJ // 2):
                pool.wait_ge(scan_done, q + 1)
                if q:
                    pool.wait_ge(states_ready, q)
                pool.tensor_tensor(sre, tsin[:, q % 2], gim, MUL)
                pool.tensor_tensor(sim, tsin[:, q % 2], gre, MUL).then_inc(unrot_sin, 1)
                if q + 2 < NJ // 2:
                    tables(q + 2)

            def squares(layer, i=0, j0=0):
                for m in range(TM):
                    pool.wait_ge(h_relu, TM * (FB * layer + j0) + m + 1 + TM * i)
                    pool.tensor_tensor(stage[:, 0, m, :], stage[:, 0, m, :], stage[:, 0, m, :],
                                       MUL).then_inc(h_row, 1)

            for s in range(MLP_A, MLP_A + 4):
                lo(pool, s)
            with pool.Fori(0, FB) as j:
                squares(0, j)
            for s in range(OD_IN, OD_IN + 4):
                lo(pool, s)
            pool.wait_ge(g1_row, TM * 8)
            for m in range(TM):
                g3 = gate[:, m, :].rearrange("p (h d) -> p h d", h=CH)
                ins = pool.tensor_tensor(g3, g3, nw[:, :].unsqueeze(1).to_broadcast([P, CH, CD]), MUL)
            ins.then_inc(gate_w, 1)
            pool.wait_ge(rows_ps, 4)
            for m in range(TM):
                for h in range(CH):
                    pool.tensor_copy(T[:, m, h, :], ident)
                    ins = pool.tensor_copy(TT[:, m, h, :], ident)
            ins.then_inc(t_init, 1)
            for s in range(MLP_B, MLP_B + 4):
                lo(pool, s)
            with pool.Fori(0, FB) as j:
                squares(1, j)

        @block.scalar
        def _(act):
            chain = chained(act, act_ch)
            act.dma_start(ldt, log_dt[0].rearrange("(j g) -> j g", g=2)).then_inc(s_small, 16)
            act.dma_start(lamr, lam_re[0].rearrange("(j g) n -> j (g n)", g=2)).then_inc(s_small, 16)
            act.dma_start(lami, lam_im[0].rearrange("(j g) n -> j (g n)", g=2)).then_inc(s_small, 16)
            act.dma_start(cst[:, 0:C_UP], consts[:, 0:C_UP]).then_inc(s_ident, 16)
            act.dma_start(tab33[0:BUCKETS, :], rel_table).then_inc(s_tab, 16)
            act.dma_start(hot, onehot).then_inc(s_tab, 16)
            act.dma_start(cst[:, C_LVL:], consts[:, C_LVL:]).then_inc(s_cst, 16)
            act.dma_start(prow[0:96, :], conv_w[0].rearrange("k (c p) -> (k c) p", p=P)).then_inc(s_prow, 16)
            act.dma_start(prow[96:100, :], s5_d[0].rearrange("(c p) -> c p", p=P)).then_inc(s_prow, 16)
            act.dma_start(prow[100:104, :], b_glu[0].rearrange("(c p) -> c p", p=P)).then_inc(s_prow, 16)
            for r, src in enumerate((c_re, c_im)):
                act.dma_start(craw[:, r], src[0].rearrange("(c g) h n -> (g h) c n", g=8)).then_inc(s_c, 16)
            act.dma_start(bre, b_re[0].rearrange("(j g) n h -> (g n) j h", g=2)).then_inc(s_b, 16)
            act.dma_start(bim, b_im[0].rearrange("(j g) n h -> (g n) j h", g=2)).then_inc(s_b, 16)
            act.dma_start(cst[:, C_UP:C_LVL], consts[:, C_UP:C_LVL]).then_inc(s_cst, 16)
            act.dma_start(wba[:, :, :], od_w_in[0][:, 4 * DM:4 * DM + 16].rearrange("(a p) n -> p a n", p=P)).then_inc(s_wba, 16)
            act.dma_start(alog[:, :], a_log.to_broadcast([P, CH])).then_inc(s_l1, 16)
            act.dma_start(dtb[:, :], dt_bias.to_broadcast([P, CH])).then_inc(s_l1, 16)
            act.dma_start(nw[:, :], norm_w.to_broadcast([P, CD])).then_inc(s_l1, 16)
            act.wait_ge(s_small, 48)
            act.activation(ldt, ldt, ACT.Exp).then_inc(s5_dt, 1)
            hi(act, 0)
            act.wait_ge(s5_ang, 1)
            act.activation(par16[:, 0, :], lrd, ACT.Exp).then_inc(s5_mag, 1)
            act.activation(s1, rr, ACT.Sin).then_inc(s5_mag, 1)
            act.activation(s2, t16, ACT.Sin).then_inc(s5_mag, 1)
            for m in range(TM):
                xt_upper(act, XT_X + 2 * m, m, (4 + 2 * m, 5 + 2 * m))
            for s in range(1, 4):
                hi(act, s)
            act.wait_ge(bias_row_sb, 1)
            act.dma_start(scratch, biasrow).then_inc(s_bias_in, 16)
            act.wait_ge(s_bias_in, 16)
            for off, c0, n in ((P, 0, P), (0, P, SEQ)):
                act.dma_start(bias[:, :, c0:c0 + n],
                              bass.AP(tensor=scratch.tensor, offset=off,
                                      ap=[[1, P], [GW, AH], [1, n]])).then_inc(s_bias_out, 16)
            act.wait_ge(ph_done, 1)
            act.wait_ge(s_zero, 1)
            act.activation(sint, ph, ACT.Sin, scale=6.283185).then_inc(phases_ready, 1)
            chain(act.activation(pr, ph, ACT.Abs))
            act.activation(cost, pr, ACT.Sin, scale=-6.283185, bias=half_pi[:, 0:1]).then_inc(phases_ready, 1)

            def rows_out(g, dst):
                for m in range(TM):
                    act.wait_ge(slab_used, EV_IN + 4 * g + 4)
                    act.activation(dst[:, m, :], ps[:, 4 + m, :], ACT.Copy).then_inc(g_row, 1)

            def transposed_out(g, dst, scale):
                act.wait_ge(t_ps, g + 1)
                act.activation(dst.rearrange("p a b -> p (a b)"), psq(2, 2), ACT.Copy,
                               scale=scale).then_inc(t_sb, 1)

            rows_out(0, stage[:, 0])
            for s in range(4, 8):
                hi(act, s)
            transposed_out(0, uT, 1.0)
            hi(act, 8)
            hi(act, 9)
            rows_out(1, stage[:, 1])
            act.wait_ge(s_wba, 16)
            act.activation(wbh[:, :, :], wba[:, :, :], ACT.Copy).then_inc(wb_split, 1)
            hi(act, 10)
            hi(act, 11)
            transposed_out(1, qT, AD ** -0.5)
            hi(act, 12)
            hi(act, 13)
            rows_out(2, stage[:, 0])
            hi(act, 14)
            hi(act, 15)
            transposed_out(2, kT, 1.0)
            rows_out(3, vrow)
            for s in range(EV_OUT, EV_OUT + 4):
                hi(act, s)

            for h in range(AH):
                act.wait_ge(att_max, h + 1)
                if h >= 1:
                    act.wait_ge(att_pt_ps, h)
                for m in range(TM):
                    c0, n = (0, P) if m == 0 else (P, SEQ)
                    ins = act.activation(att_p[:, c0:c0 + n], ps[:, 4, c0:c0 + n], ACT.Exp,
                                         bias=att_nm[:, 2 * h + m:2 * h + m + 1],
                                         accum_out=att_sum[:, m, h:h + 1])
                ins.then_inc(att_exp, 1)
                act.wait_ge(att_pt_ps, h + 1)
                if h >= 1:
                    act.wait_ge(att_o, h)
                act.activation(att_pt, ps[:, 5, 0:GW], ACT.Copy).then_inc(att_pt_sb, 1)
            for m in range(TM):
                xt_upper(act, XT_ATT + m, m, (4 + m,))

            for c in range(4):
                act.wait_ge(y_sum, c + 1)
                chain(act.activation(yT[:, c, :], yT[:, c, :], ACT.Gelu_apprx_tanh))
                act.activation(fh[:, c, :], yT[:, c, :], ACT.Copy).then_inc(gelu_hi, 1)
            for s in range(GLU, GLU + 4):
                hi(act, s)
            for c in range(4):
                act.wait_ge(slab_used, GLU + 2)
                act.activation(zs[:, c, :], ps[:, 6 + c // 2, (c % 2) * SEQ:(c % 2) * SEQ + SEQ], ACT.Sigmoid,
                               bias=params[:, 100 + c:101 + c]).then_inc(z_sig, 1)
            for c in range(4):
                act.wait_ge(ssm_rows, c + 1)
                act.activation(xh[:, 4 + c, :], yT[:, c, :], ACT.Copy).then_inc(ssm_hi, 1)
            for s in range(GLU + 4, GLU + 6):
                hi(act, s)

            def lnp_load(g, b):
                for k, w in enumerate((g, b)):
                    act.dma_start(lnp[:, k, :], w.unsqueeze(0).to_broadcast([P, DM])).then_inc(s_lnp, 16)

            lnp_load(ln_mix_g[0], ln_mix_b[0])
            norm_act(act, 0, XT_LN0, MLP_A)
            act.wait_ge(ln_done, TM * 1)
            lnp_load(ln_ffn_g[0], ln_ffn_b[0])

            def relu(layer, i=0, j0=0):
                base = (MLP_A, MLP_B)[layer] + 8 * j0 + (0 if j0 else 4)
                for m in range(TM):
                    act.wait_ge(slab_used, base + 8 * i)
                    act.activation(stage[:, 0, m, :], ps[:, 4 + m, :], ACT.Relu).then_inc(h_relu, 1)

            def ht_upper(layer, i=0, j0=0):
                for q in range(2):
                    act.wait_ge(ht_ps, 2 * (FB * layer + j0) + q + 1 + 2 * i)
                    act.activation(fh[:, 2 * q:2 * q + 2, :],
                                   ps[:, 6 + q, :].rearrange("p (a b) -> p a b", a=2),
                                   ACT.Copy).then_inc(ht_hi, 1)

            def mlp(base, layer):
                relu(layer)
                for k in range(4, 8):
                    hi(act, base + k)

                with act.Fori(0, FB - 1) as j:
                    hi(act, base + 8, j)
                    hi(act, base + 9, j)
                    ht_upper(layer, j)
                    hi(act, base + 10, j)
                    hi(act, base + 11, j)
                    relu(layer, j, 1)
                    for k in range(12, 16):
                        hi(act, base + k, j)
                ht_upper(layer, 0, FB - 1)

            mlp(MLP_A, 0)

            norm_act(act, 1, XT_LN1, OD_IN)

            def conv_silu(g):
                act.wait_ge(conv_done, g + 1)
                v = convT[:, 4 * g:4 * g + 4, :]
                ins = act.activation(v, v, ACT.Silu)
                if g < 4:
                    chain(ins)
                    if g:
                        act.wait_ge(ss_ps, g)
                    act.activation(sqT, v, ACT.Square).then_inc(sq_done, 1)
                else:
                    ins.then_inc(v_silu, 1)

            def od_rows_out(g):
                b = 4 + 2 * (g % 2)
                if g >= 2:
                    act.wait_ge(t1_ps, min(g - 1, 6))
                for m in range(TM):
                    act.wait_ge(slab_used, OD_IN + 4 * g + 4)
                    if g < 6:
                        act.activation(stage[:, g % 2, m, :], ps[:, b + m, :], ACT.Copy).then_inc(g1_row, 1)
                    else:
                        act.activation(gate[:, m, (g - 6) * NW:(g - 5) * NW], ps[:, b + m, :],
                                       ACT.Silu).then_inc(g1_row, 1)

            for g in range(8):
                for k in range(4):
                    hi(act, OD_IN + 4 * (g + 1) + k)
                od_rows_out(g)
                if g >= 2:
                    conv_silu(g - 2)

            act.wait_ge(ba_sb, 1)
            act.activation(sm[BETA], ba_b, ACT.Exp, scale=-1.0).then_inc(gate_exp, 1)
            act.activation(alog[:, :], alog[:, :], ACT.Exp).then_inc(gate_exp, 1)
            act.wait_ge(ba_sb, 2)
            act.activation(sm[E1], sm[AXX], ACT.Exp, scale=-1.0).then_inc(gate_exp, 1)
            act.wait_ge(ba_sb, 3)
            act.activation(sm[LW], sm[W1], ACT.Ln).then_inc(gate_exp, 1)
            act.wait_ge(norm_in, 1)
            act.activation(sm[RK], sm[IK], ACT.Sqrt).then_inc(norm_out, 1)
            act.activation(sm[DINV], sm[SSK], ACT.Sqrt).then_inc(norm_out, 1)
            act.activation(sm[RQ], sm[SSQ], ACT.Sqrt).then_inc(norm_out, 1)
            act.wait_ge(ba_sb, 4)
            act.activation(sm[EG], sm[GC], ACT.Exp).then_inc(cum_exp, 1)
            act.activation(egl[:, :, :].rearrange("p a b -> p (a b)"), ps[:, 1, 64:96], ACT.Exp).then_inc(cum_exp, 1)
            act.activation(sm[EKD], sm[EKD], ACT.Exp).then_inc(cum_exp, 1)
            for b in range(4):
                act.wait_ge(dec_in, b + 1)
                act.activation(dec, dec, ACT.Exp).then_inc(dec_ready, 1)
            for b in range(4):
                act.wait_ge(wt_ps, b + 1)
                act.activation(WT[:, b // 2, 4 * (b % 2):4 * (b % 2) + 4, :],
                               ps[:, 4 + b, :].rearrange("p (a b) -> p a b", a=4), ACT.Copy).then_inc(wt_sb, 1)
            for m in range(TM):
                act.wait_ge(o2_ps, m + 1)
                if m:
                    act.wait_ge(o_rows, m)
                act.activation(obuf, psq(6, 2), ACT.Copy).then_inc(o2_sb, 1)
                act.wait_ge(o_sum, m + 1)
                act.activation(osq(m), obuf, ACT.Square).then_inc(o_sq, 1)
                act.wait_ge(rms_in, m + 1)
                act.activation(sm[CC][:, m, :], sm[CC][:, m, :], ACT.Sqrt).then_inc(rms_out, 1)
                if m == 0:
                    xt_upper(act, XT_GDN, 0, (6, 7))
            act.wait_ge(o_rows, TM)
            lnp_load(ln_mix_g[1], ln_mix_b[1])
            xt_upper(act, XT_GDN + 2, 1, (4, 5))
            for s in range(OD_OUT + 4, OD_OUT + 8):
                hi(act, s)
            norm_act(act, 2, XT_LN2, MLP_B)
            act.wait_ge(ln_done, TM * 3)
            lnp_load(ln_ffn_g[1], ln_ffn_b[1])
            mlp(MLP_B, 1)
            for m in range(TM):
                ln_sqrt(act, 3, m)

        @block.vector
        def _(dve):
            chain = chained(dve, dve_ch)
            dve.wait_ge(s5_dt, 1)
            dtb3 = ldt.unsqueeze(2).to_broadcast([NJ, 2, SN])

            def v3(a):
                return a.rearrange("p (g n) -> p g n", g=2)

            chain(dve.tensor_scalar(lamr, lamr, -1e-4, None, ALU.min))
            dve.tensor_tensor(v3(lrd), v3(lamr), dtb3, MUL)
            chain(dve.tensor_tensor(v3(th), v3(lami), dtb3, MUL))
            chain(dve.tensor_scalar(nn, th, 1 / TWO_PI, ROUND, MUL, ADD))
            chain(dve.tensor_scalar(nn, nn, ROUND, None, SUB))
            chain(dve.scalar_tensor_tensor(rr, nn, -PI_A, th, MUL, ADD))
            chain(dve.scalar_tensor_tensor(rr, nn, -PI_B, rr, MUL, ADD))
            chain(dve.scalar_tensor_tensor(rr, nn, -PI_C, rr, MUL, ADD))
            chain(dve.tensor_scalar(rr, rr, 3.1415925, -3.1415925, ALU.min, MAX))
            dve.tensor_scalar(t16, rr, 0.5, None, MUL).then_inc(s5_ang, 1)
            dve.tensor_tensor(den, lamr, lamr, MUL)
            chain(dve.tensor_tensor(th, lami, lami, MUL))
            chain(dve.tensor_tensor(den, den, th, ADD))
            chain(dve.reciprocal(den, den))
            dve.wait_ge(s5_mag, 3)
            mag = par16[:, 0, :]
            chain(dve.tensor_tensor(s2, s2, s2, MUL))
            chain(dve.tensor_scalar(ar1, s2, -2.0, 1.0, MUL, ADD))
            dve.tensor_tensor(aim, mag, s1, MUL)
            chain(dve.tensor_tensor(ar1, ar1, mag, MUL))
            chain(dve.tensor_scalar(ar1, ar1, 1.0, None, SUB))
            dve.tensor_tensor(th, ar1, lamr, MUL)
            chain(dve.tensor_tensor(s1, aim, lami, MUL))
            chain(dve.tensor_tensor(th, th, s1, ADD))
            dve.tensor_tensor(par16[:, 1, :], th, den, MUL)
            chain(dve.tensor_tensor(s1, aim, lamr, MUL))
            chain(dve.tensor_tensor(s2, ar1, lami, MUL))
            chain(dve.tensor_tensor(s1, s1, s2, SUB))
            dve.tensor_tensor(par16[:, 2, :], s1, den, MUL)
            chain(dve.tensor_scalar(rr, rr, 1 / TWO_PI, None, MUL))
            chain(dve.tensor_scalar(par16[:, 3, :], rr, ROUND16, ROUND16, ADD, SUB))
            dve.tensor_tensor(par16[:, 4, :], rr, par16[:, 3, :], SUB).then_inc(s5_par, 1)
            dve.wait_ge(par_ps, 1)
            chain(dve.tensor_copy(par.rearrange("p a b -> p (a b)"), ps[:, 0, 0:5 * NJ]))
            dve.wait_ge(prow_ps, 1)
            dve.tensor_copy(params[:, :], ps[:, 0, 128:232]).then_inc(params_sb, 1)
            dve.wait_ge(bias_ps, 1)
            dve.tensor_copy(biasrow, ps[0:AH, 1, 0:GW]).then_inc(bias_row_sb, 1)
            def perp(k):
                return par[:, k, :].unsqueeze(2).to_broadcast([P, NJ, 32])
            tv = cst[:, C_T:C_T + 32].unsqueeze(1).to_broadcast([P, NJ, 32])
            chain(dve.tensor_tensor(ph, perp(3), tv, MUL))
            for step in range(2):
                chain(dve.tensor_scalar(pr, ph, ROUND, ROUND, ADD, SUB))
                chain(dve.tensor_tensor(ph, ph, pr, SUB))
                if step == 0:
                    chain(dve.tensor_tensor(pr, perp(4), tv, MUL))
                    chain(dve.tensor_tensor(ph, ph, pr, ADD))
            dve.sem_inc(ph_done, 1)
            for m in range(TM):
                xt_lower(dve, XT_X + 2 * m, m, (4 + 2 * m, 5 + 2 * m))
            for s in range(0, 4):
                lo(dve, s)
            dve.wait_ge(s_b, 32)
            dve.wait_ge(s_zero, 1)

            def coef(k):
                return par[:, k, :].unsqueeze(2).to_broadcast([P, NJ, SH])
            for r, (b1, b2, op) in enumerate(((bre, bim, SUB), (bim, bre, ADD))):
                dve.tensor_tensor(btmp, coef(1), b1, MUL)
                chain(dve.tensor_tensor(btm2, coef(2), b2, MUL))
                for g in range(2):
                    rows = slice(SN * g, SN * g + SN)
                    ins = dve.tensor_tensor(bpad[rows, r, :, SH * g:SH * g + SH], btmp[rows], btm2[rows], op)
                chain(ins)
            dve.sem_inc(b_padded, 1)
            for s in range(4, 8):
                lo(dve, s)
            dve.wait_ge(b_ps, 1)
            dve.tensor_copy(bT.rearrange("p a b c -> p (a b c)"), psq(2, 2)).then_inc(bT_sb, 1)
            dve.wait_ge(c_ps, 1)
            dve.tensor_copy(cT[:, 0].rearrange("p b c -> p (b c)"), psq(0))
            dve.tensor_scalar(cT[:, 1].rearrange("p b c -> p (b c)"), psq(1), -1.0, None, MUL).then_inc(cT_sb, 1)

            def rotate(q):
                tc, ts_ = tcos[:, q % 2], tsin[:, q % 2]
                xre, xim = ps[:, 0:2, 0:SEQ], ps[:, 0:2, SEQ:2 * SEQ]
                dve.wait_ge(x_ps, q + 1)
                dve.wait_ge(tab_ready, q + 1)
                dve.tensor_tensor(pa, xre, tc, MUL)
                dve.tensor_tensor(pb, xim, ts_, MUL)
                dve.tensor_tensor(pc, xim, tc, MUL)
                dve.tensor_tensor(pd, xre, ts_, MUL).then_inc(rot_ready, 1)
                dve.wait_ge(rot_ready, q + 1)
                dve.tensor_tensor(pa, pa, pb, ADD)
                dve.tensor_tensor(pc, pc, pd, SUB).then_inc(rot_done, 1)

            def scans(q):
                dve.wait_ge(rot_done, q + 1)
                if q >= 1:
                    dve.wait_ge(unrot_sin, q)
                for jj in range(2):
                    decay = par[:, 0, 2 * q + jj:2 * q + jj + 1].to_broadcast([P, SEQ])
                    dve.tensor_tensor_scan(gre[:, jj, :], decay, pa[:, jj, :], 0.0, MUL, ADD)
                    ins = dve.tensor_tensor_scan(gim[:, jj, :], decay, pc[:, jj, :], 0.0, MUL, ADD)
                ins.then_inc(scan_done, 1)
                dve.wait_ge(scan_done, q + 1)
                tc = tcos[:, q % 2]
                if q >= 1:
                    dve.wait_ge(y_done, q)
                dve.tensor_tensor(hre, tc, gre, MUL)
                dve.tensor_tensor(him, tc, gim, MUL).then_inc(unrot_cos, 1)

            def unrotate(q):
                dve.wait_ge(unrot_cos, q + 1)
                dve.wait_ge(unrot_sin, q + 1)
                dve.tensor_tensor(hre, hre, sre, SUB)
                dve.tensor_tensor(him, him, sim, ADD).then_inc(states_ready, 1)

            def skip_sum(c):
                dve.wait_ge(y_done, 2 * c + 2)
                dve.scalar_tensor_tensor(yT[:, c, :], uT[:, c, :], params[:, 96 + c:97 + c],
                                         ps[:, 6 + c % 2, 0:SEQ], MUL, ADD).then_inc(y_sum, 1)

            lo(dve, 8)
            lo(dve, 9)
            rotate(0)
            scans(0)
            lo(dve, 10)
            lo(dve, 11)
            rotate(1)
            unrotate(0)
            lo(dve, 12)
            lo(dve, 13)
            scans(1)
            rotate(2)
            unrotate(1)
            lo(dve, 14)
            lo(dve, 15)
            scans(2)
            rotate(3)
            skip_sum(0)
            unrotate(2)
            for s in range(EV_OUT, EV_OUT + 4):
                lo(dve, s)

            def head(h):
                dve.wait_ge(att_sc, h + 1)
                dve.reduce_max(att_nm[:, 2 * h:2 * h + 1], ps[:, 4, 0:P], AX.X)
                chain(dve.reduce_max(att_nm[:, 2 * h + 1:2 * h + 2], ps[:, 4, P:GW], AX.X))
                dve.tensor_scalar(att_nm[:, 2 * h:2 * h + 2], att_nm[:, 2 * h:2 * h + 2], -1.0, None,
                                  MUL).then_inc(att_max, 1)

            for q in range(3, 8):
                scans(q)
                if q < 7:
                    head(2 * (q - 3))
                    rotate(q + 1)
                unrotate(q)
                if q < 7:
                    head(2 * (q - 3) + 1)
                if q % 2 == 0:
                    skip_sum(q // 2 - 1)
            skip_sum(3)

            dve.wait_ge(att_exp, AH)
            chain(dve.reciprocal(att_rs.rearrange("p a b -> p (a b)"), att_sum.rearrange("p a b -> p (a b)")))
            dve.wait_ge(att_o, AH)
            for m in range(TM):
                dve.tensor_tensor(stage[:, 1, m, :].rearrange("p (h d) -> p h d", h=AH),
                                  ps[:, 2 + m, :].rearrange("p (h d) -> p h d", h=AH),
                                  att_rs[:, m, :].unsqueeze(2).to_broadcast([P, AH, AD]),
                                  MUL).then_inc(att_rows, 1)
            for m in range(TM):
                xt_lower(dve, XT_ATT + m, m, (4 + m,))
            for c in range(4):
                dve.wait_ge(gelu_hi, c + 1)
                dve.tensor_tensor(fl[:, c, :], yT[:, c, :], fh[:, c, :].bitcast(f32), SUB).then_inc(gelu_lo, 1)
            for s in range(GLU, GLU + 4):
                lo(dve, s)
            for c in range(4):
                dve.wait_ge(z_sig, c + 1)
                dve.tensor_tensor(yT[:, c, :], yT[:, c, :], zs[:, c, :], MUL).then_inc(ssm_rows, 1)
            for c in range(4):
                dve.wait_ge(ssm_hi, c + 1)
                dve.tensor_tensor(xl[:, 4 + c, :], yT[:, c, :], xh[:, 4 + c, :].bitcast(f32), SUB).then_inc(ssm_lo, 1)
            for s in range(GLU + 4, GLU + 6):
                lo(dve, s)
            dve.wait_ge(wb_split, 1)
            dve.tensor_tensor(wbl[:, :, :], wba[:, :, :], wbh[:, :, :].bitcast(f32), SUB).then_inc(wb_split, 1)
            norm_dve(dve, 0, XT_LN0, chain)

            def ht_lower(layer, i=0, j0=0):
                for q in range(2):
                    dve.wait_ge(ht_hi, 2 * (FB * layer + j0) + q + 1 + 2 * i)
                    dve.tensor_tensor(fl[:, 2 * q:2 * q + 2, :],
                                      ps[:, 6 + q, :].rearrange("p (a b) -> p a b", a=2),
                                      fh[:, 2 * q:2 * q + 2, :].bitcast(f32), SUB).then_inc(ht_lo, 1)

            def mlp(base, layer):
                dve.wait_ge(lo_ready, base + 4)
                for k in range(4, 8):
                    lo(dve, base + k)
                with dve.Fori(0, FB - 1) as j:
                    lo(dve, base + 8, j)
                    lo(dve, base + 9, j)
                    ht_lower(layer, j)
                    lo(dve, base + 10, j)
                    lo(dve, base + 11, j)
                    for k in range(12, 16):
                        lo(dve, base + k, j)
                ht_lower(layer, 0, FB - 1)

            mlp(MLP_A, 0)

            norm_dve(dve, 1, XT_LN1, chain)
            dve.wait_ge(lo_ready, OD_IN + 4)
            dve.wait_ge(ba_ps, 1)
            dve.wait_ge(s_l1, 48)
            ba = ps[:, 1, 0:32].rearrange("p (m c) -> p m c", m=TM)
            dve.tensor_copy(ba_b, ba[:, :, 0:CH]).then_inc(ba_sb, 1)
            chain(dve.tensor_tensor(sm[XG], ba[:, :, CH:2 * CH],
                                    dtb[:, :].unsqueeze(1).to_broadcast([P, TM, CH]), ADD))
            chain(dve.tensor_scalar(sm[AXX], sm[XG], -1.0, None, MUL))
            dve.tensor_tensor(sm[AXX], sm[AXX], sm[XG], MAX).then_inc(ba_sb, 1)

            def conv(g):
                dve.wait_ge(t1_ps, g + 1)
                c0 = OD_COLS[g] // P
                for tap in range(CONV - 1, -1, -1):
                    d = CONV - 1 - tap
                    for c in range(4):
                        w = params[:, 24 * tap + c0 + c:24 * tap + c0 + c + 1]
                        src = ps[:, 2 + c // 2, (c % 2) * SEQ:(c % 2) * SEQ + SEQ - d]
                        o = convT[:, 4 * g + c, d:SEQ]
                        if d == 0:
                            ins = dve.tensor_scalar(o, src, w, None, MUL)
                        else:
                            ins = dve.scalar_tensor_tensor(o, src, w, o, MUL, ADD)
                    if tap:
                        chain(ins)
                ins.then_inc(conv_done, 1)

            for g in range(8):
                for k in range(4):
                    lo(dve, OD_IN + 4 * (g + 1) + k)
                if 1 <= g <= 6:
                    conv(g - 1)

            dve.wait_ge(gate_exp, 3)
            chain(dve.tensor_scalar(sm[BETA], sm[BETA], 1.0, None, ADD))
            dve.reciprocal(sm[BETA], sm[BETA])
            dve.tensor_scalar(sm[W1], sm[E1], 1.0, None, ADD).then_inc(ba_sb, 1)
            dve.wait_ge(ba_sb, 3)
            chain(dve.tensor_scalar(sm[DD], sm[W1], 1.0, None, SUB))
            chain(dve.tensor_scalar(sm[EQ], sm[DD], 0.0, None, ALU.is_equal))
            chain(dve.tensor_tensor(sm[DD], sm[DD], sm[EQ], ADD))
            chain(dve.reciprocal(sm[DD], sm[DD]))
            chain(dve.tensor_tensor(sm[E1], sm[E1], sm[DD], MUL))
            dve.wait_ge(gate_exp, 4)
            chain(dve.tensor_tensor(sm[LW], sm[LW], sm[EQ], ADD))
            chain(dve.tensor_tensor(sm[E1], sm[E1], sm[LW], MUL))
            chain(dve.scalar_tensor_tensor(sm[GR], sm[XG], 0.0, sm[E1], MAX, ADD))
            dve.scalar_tensor_tensor(sm[GR], sm[GR], -1.0, alog[:, :].unsqueeze(1).to_broadcast([P, TM, CH]),
                                     MUL, MUL).then_inc(g_ready, 1)
            dve.wait_ge(ss_ps, 4)
            ss = ps[:, 0, 0:32].rearrange("p (c m) -> p m c", m=TM)
            chain(dve.tensor_scalar(sm[SSK], ss[:, :, 0:CH], L2_EPS, None, ADD))
            chain(dve.reciprocal(sm[IK], sm[SSK]))
            chain(dve.tensor_scalar(sm[SSQ], ss[:, :, CH:2 * CH], L2_EPS, None, ADD))
            chain(dve.reciprocal(sm[SSQ], sm[SSQ]))
            chain(dve.tensor_tensor(sm[BRK2], sm[BETA], sm[IK], MUL))
            dve.sem_inc(norm_in, 1)
            dve.wait_ge(cum_ps, 1)
            chain(dve.tensor_copy(sm[GC], ps[:, 1, 32:48].rearrange("p (a b) -> p a b", a=2)))
            dve.tensor_tensor(sm[EKD], ps[:, 1, 48:64].rearrange("p (a b) -> p a b", a=2), sm[GC],
                              SUB).then_inc(ba_sb, 1)
            negm = cst[:, C_NEG:C_NEG + P]
            dve.wait_ge(norm_out, 3)
            for b in range(4):
                m, h0, base = b // 2, 4 * (b % 2), 2 + 3 * (b % 2)
                dve.wait_ge(kk_ps, b + 1)
                for h in range(4):
                    ins = dve.scalar_tensor_tensor(dec[:, h, :], ps[:, base, h * P:h * P + P],
                                                   sm[GC][:, m, h0 + h:h0 + h + 1], negm, SUB, ADD)
                ins.then_inc(dec_in, 1)
                dve.wait_ge(dec_ready, b + 1)
                for h in range(4):
                    dve.scalar_tensor_tensor(intraT[:, m, h0 + h, :], ps[:, base + 2, h * P:h * P + P],
                                             sm[RK][:, m, h0 + h:h0 + h + 1], dec[:, h, :], MUL, MUL)
                for h in range(4):
                    ins = dve.scalar_tensor_tensor(NT[:, m, h0 + h, :], ps[:, base + 1, h * P:h * P + P],
                                                   sm[BRK2][:, m, h0 + h:h0 + h + 1], dec[:, h, :], MUL, MUL)
                chain(ins)
                dve.sem_inc(nt_ready, 1)

            dve.wait_ge(cum_exp, 3)

            def rowb(v, m):
                return v[:, m, :].unsqueeze(2).to_broadcast([P, CH, CD])
            chain(dve.tensor_tensor(sm[BRK], sm[BETA], sm[RK], MUL))
            chain(dve.tensor_tensor(sm[EKD], sm[EKD], sm[RK], MUL))
            chain(dve.tensor_scalar(sm[NEGEG], sm[EG], -1.0, None, MUL))
            chain(dve.tensor_scalar(sm[RQ], sm[RQ], CD ** -0.5, None, MUL))
            for m in range(TM):
                dve.wait_ge(rows_ps, 2 * m + 1)
                dve.tensor_tensor(dv[:, m], psq(4, 2).rearrange("p (a b) -> p a b", a=CH),
                                  rowb(sm[DINV], m), MUL).then_inc(rows_sb, 1)
                dve.wait_ge(rows_ps, 2 * m + 2)
                kr = psq(6, 2).rearrange("p (a b) -> p a b", a=CH)
                dve.tensor_tensor(kw[:, m], kr, rowb(sm[NEGEG], m), MUL)
                dve.tensor_tensor(kdec[:, m], kr, rowb(sm[EKD], m), MUL).then_inc(rows_sb, 1)

            dve.wait_ge(t_init, 1)
            for lev in range(LEVELS):
                mask = cst[:, C_LVL + lev * P:C_LVL + lev * P + P].unsqueeze(1).to_broadcast([P, 4, P])
                for b in range(4):
                    m, h0, n = b // 2, 4 * (b % 2), 4 * lev + b
                    dve.wait_ge(nt_ps, n + 1)
                    if n >= 2:
                        dve.wait_ge(tx_ps, n - 1)
                    dve.tensor_tensor(XX[:, b % 2], ps[:, b % 2, :].rearrange("p (a b) -> p a b", a=4), mask,
                                      MUL).then_inc(xx_ready, 1)
                    if b >= 1:
                        inverse_step(dve, lev, b - 1, chain)
                inverse_step(dve, lev, 3, chain)

            for n in range(4):
                m, rows = n // 2, slice(CK * (n % 2), CK * (n % 2) + CK)
                if n == 3:
                    xt_lower(dve, XT_GDN, 0, (6, 7))
                dve.wait_ge(v_ps, n + 1)
                dve.tensor_tensor(vnew[rows, m], psq(0, 2)[rows].rearrange("p (a b) -> p a b", a=CH),
                                  sm[BRK][rows, m, :].unsqueeze(2).to_broadcast([CK, CH, CD]),
                                  MUL).then_inc(vnew_done, 1)
                if n < 3:
                    s4 = S[n + 1]
                    if n:
                        chain(dve.tensor_tensor(s4, S[n], egl[:, n, :].unsqueeze(2).to_broadcast([P, CH, CD]), MUL))
                    dve.wait_ge(kv_ps, n + 1)
                    kv = psq(2, 2).rearrange("p (a b) -> p a b", a=CH)
                    if n:
                        dve.tensor_tensor(s4, s4, kv, ADD).then_inc(s_ready, 1)
                    else:
                        dve.tensor_copy(s4, kv).then_inc(s_ready, 1)
                if n % 2:
                    rr_ = slice(0, P) if m else slice(CK, P)
                    nr = P if m else CK
                    dve.wait_ge(o2_sb, m + 1)
                    chain(dve.tensor_tensor(osq(m)[rr_].rearrange("p (a b) -> p a b", a=CH),
                                            psq(4, 2)[rr_].rearrange("p (a b) -> p a b", a=CH),
                                            sm[EG][rr_, m, :].unsqueeze(2).to_broadcast([nr, CH, CD]), MUL))
                    chain(dve.tensor_tensor(obuf[rr_], obuf[rr_], osq(m)[rr_], ADD))
                    dve.sem_inc(o_sum, 1)
                    dve.wait_ge(o_sq, m + 1)
                    cc, rq = sm[CC][:, m, :], sm[RQ][:, m, :]
                    chain(dve.reduce_sum(cc, osq(m).rearrange("p (a b) -> p a b", a=CH), AX.X))
                    chain(dve.tensor_tensor(cc, cc, rq, MUL))
                    chain(dve.tensor_tensor(cc, cc, rq, MUL))
                    chain(dve.tensor_scalar(cc, cc, 1.0 / CD, RMS_EPS, MUL, ADD))
                    dve.reciprocal(cc, cc).then_inc(rms_in, 1)
                    dve.wait_ge(rms_out, m + 1)
                    chain(dve.tensor_tensor(cc, cc, rq, MUL))
                    ob3 = obuf.rearrange("p (a b) -> p a b", a=CH)
                    chain(dve.tensor_tensor(ob3, ob3, cc.unsqueeze(2).to_broadcast([P, CH, CD]), MUL))
                    dve.wait_ge(gate_w, 1)
                    dve.tensor_tensor(gate[:, m, :], gate[:, m, :], obuf, MUL).then_inc(o_rows, 1)
            xt_lower(dve, XT_GDN + 2, 1, (4, 5))
            for s in range(OD_OUT + 4, OD_OUT + 8):
                lo(dve, s)
            norm_dve(dve, 2, XT_LN2, chain)
            mlp(MLP_B, 1)
            for m in range(TM):
                ln_stats(dve, 3, m, chain)
                ln_apply(dve, 3, m, chain)

        @block.tensor
        def _(pe):
            left_x, left_f = (xh, xl), (fh, fl)

            def project(g, ks=range(4)):
                if g >= 1 and ks[0] == 0:
                    pe.wait_ge(g_row, TM * g)
                for k in ks:
                    slab_product(pe, EV_IN + 4 * g + k, (4, 5), left_x, 2 * k, k == 0, k == 3)

            def transpose_rows(g):
                pe.wait_ge(g_row, TM * (g + 1))
                if g >= 1:
                    pe.wait_ge(t_sb, g)
                for c in range(4):
                    for m in range(TM):
                        ins = pe.transpose(ps[:, 2 + c // 2, (c % 2) * SEQ + m * P:(c % 2) * SEQ + m * P + P],
                                           stage[:, g % 2, m, c * P:c * P + P], ident)
                ins.then_inc(t_ps, 1)

            pe.wait_ge(s_ident, 16)
            for m in range(TM):
                pe.wait_ge(s_x[m], 16)
                xt_transposes(pe, m, (4 + 2 * m, 5 + 2 * m), xrow)
            pe.wait_ge(s_prow, 48)
            pe.transpose(ps[:, 0, 128:232], prow, ident[0:104, 0:104]).then_inc(prow_ps, 1)
            pe.wait_ge(s_tab, 32)
            pe.wait_ge(pool_ch, 1)
            pe.matmul(ps[0:AH, 1, 0:GW], tab33, hot, start=True, stop=True).then_inc(bias_ps, 1)
            pe.wait_ge(s5_par, 1)
            for k in range(5):
                ins = pe.transpose(ps[:, 0, NJ * k:NJ * k + NJ], par16[:, k, :], ident[0:NJ, 0:NJ])
            ins.then_inc(par_ps, 1)
            pe.wait_ge(xt_lo, 4)
            project(0)
            project(1, (0, 1))
            transpose_rows(0)
            project(1, (2, 3))
            pe.wait_ge(b_padded, 1)
            pe.wait_ge(t_sb, 1)
            for r in range(2):
                for c in range(4):
                    ins = pe.transpose(ps[:, 2 + r, c * P:c * P + P],
                                       bpad[:, r, 4 * c:4 * c + 4, :].rearrange("p a b -> p (a b)"), ident)
            ins.then_inc(b_ps, 1)
            pe.wait_ge(c_padded, 1)
            pe.wait_ge(bias_row_sb, 1)
            pe.wait_ge(params_sb, 1)
            for r in range(2):
                for c in range(4):
                    ins = pe.transpose(ps[:, r, c * P:c * P + P], cpad[:, r, c, :], ident)
            ins.then_inc(c_ps, 1)

            def inputs(q):
                if q == 0:
                    pe.wait_ge(t_sb, 1)
                    pe.wait_ge(cT_sb, 1)
                else:
                    pe.wait_ge(rot_ready, q)
                c = q // 2
                for jj in range(2):
                    i = 2 * (q % 2) + jj
                    rows = slice(32 * i, 32 * i + 32)
                    for r in range(2):
                        ins = pe.matmul(ps[:, jj, r * SEQ:r * SEQ + SEQ], bT[rows, r, c, :], uT[rows, c, :],
                                        start=True, stop=True)
                ins.then_inc(x_ps, 1)

            def outputs(q):
                c = q // 2
                pe.wait_ge(states_ready, q + 1)
                if c >= 2:
                    pe.wait_ge(y_sum, c - 1)
                for jj in range(2):
                    i = 2 * (q % 2) + jj
                    o = ps[32 * i:32 * i + 32, 6 + c % 2, 0:SEQ]
                    pe.matmul(o, cT[:, 0, c, 32 * i:32 * i + 32], hre[:, jj, :], start=True, stop=False)
                    ins = pe.matmul(o, cT[:, 1, c, 32 * i:32 * i + 32], him[:, jj, :], start=False, stop=True)
                ins.then_inc(y_done, 1)

            project(2, (0, 1))
            inputs(0)
            inputs(1)
            project(2, (2, 3))
            pe.wait_ge(bT_sb, 1)
            transpose_rows(1)
            inputs(2)
            outputs(0)
            project(3, (0, 1))
            outputs(1)
            project(3, (2, 3))
            transpose_rows(2)
            inputs(3)
            outputs(2)
            pe.wait_ge(g_row, TM * 4)
            pe.wait_ge(t_sb, 3)
            pe.wait_ge(s_bias_out, 32)

            def scores(h):
                if h >= 1:
                    pe.wait_ge(att_exp, h)
                c, r = h // 2, slice(AD * (h % 2), AD * (h % 2) + AD)
                flip = cst[:, C_FLIP:C_FLIP + P]
                pe.matmul(ps[:, 4, 0:P], flip, bias[:, h, 0:P], start=True, stop=False)
                pe.matmul(ps[:, 4, 0:P], qT[r, c, 0:P], kT[r, c, 0:P], start=False, stop=True)
                pe.matmul(ps[:, 4, P:GW], flip, bias[:, h, P:GW], start=True, stop=False)
                pe.matmul(ps[:, 4, P:GW], qT[r, c, P:SEQ], kT[r, c, :], start=False, stop=True).then_inc(att_sc, 1)

            def weighted(h):
                pe.wait_ge(att_exp, h + 1)
                if h >= 1:
                    pe.wait_ge(att_pt_sb, h)
                for b in range(3):
                    ins = pe.transpose(ps[:, 5, b * P:b * P + P], att_p[:, b * P:b * P + P], ident)
                ins.then_inc(att_pt_ps, 1)
                pe.wait_ge(att_pt_sb, h + 1)
                v = slice(h * AD, h * AD + AD)
                pe.matmul(ps[:, 2, v], att_pt[:, 0:P], vrow[:, 0, v], start=True, stop=True)
                pe.matmul(ps[:, 3, v], att_pt[:, P:2 * P], vrow[:, 0, v], start=True, stop=False)
                pe.matmul(ps[:, 3, v], att_pt[:, 2 * P:GW], vrow[:, 1, v], start=False, stop=True).then_inc(att_o, 1)

            for q in range(3, 7):
                h = 2 * (q - 3)
                scores(h)
                inputs(q + 1)
                weighted(h)
                scores(h + 1)
                outputs(q)
                weighted(h + 1)
            outputs(7)
            for m in range(TM):
                pe.wait_ge(att_rows, m + 1)
                xt_transposes(pe, m, (4 + m,), stage[:, 1])
            pe.wait_ge(xt_lo, XT_LN0)
            for n in range(2):
                for k in range(2):
                    slab_product(pe, EV_OUT + 2 * n + k, (n, 2 + n), left_x, 2 * k, k == 0, False)
            pe.wait_ge(gelu_lo, 4)
            pe.wait_ge(lo_ready, GLU + 2)
            for c in range(4):
                o = ps[:, 6 + c // 2, (c % 2) * SEQ:(c % 2) * SEQ + SEQ]
                cols = slice(c * P, c * P + P)
                for k in range(4):
                    q, kk = (GLU + k // 2) % SPL, k % 2
                    pe.matmul(o, whi[:, q, kk, cols], fh[:, k, :], start=k == 0, stop=False)
                    pe.matmul(o, whi[:, q, kk, cols], fl[:, k, :], start=False, stop=False)
                    ins = pe.matmul(o, wlo[:, q, kk, cols], fh[:, k, :], start=False, stop=k == 3)
            ins.then_inc(slab_used, 2)

            pe.wait_ge(ssm_lo, 4)
            for m in range(TM):
                four_slabs(pe, GLU + 2, m, [(2 * m + n, 4 + 2 * k, False, k == 1) for n in range(2) for k in range(2)],
                           left_x, acc_ready)

            def hidden_slabs(base, ks, i=0):
                for k in ks:
                    slab_product(pe, base + k, (4, 5), left_x, 2 * (k % 4), k % 4 == 0, k % 4 == 3, i)

            def hidden_transposes(layer, i=0, j0=0):
                b = FB * layer + j0
                pe.wait_ge(h_row, TM * (b + 1) + TM * i)
                if layer or j0:
                    pe.wait_ge(ht_lo, 2 * b + 2 * i)
                for c in range(4):
                    for m in range(TM):
                        ins = pe.transpose(ps[:, 6 + c // 2, (c % 2) * SEQ + m * P:(c % 2) * SEQ + m * P + P],
                                           stage[:, 0, m, c * P:c * P + P], ident)
                    if c % 2:
                        ins.then_inc(ht_ps, 1)

            def down(base, layer, i=0, j0=0, first=False, last=False):
                pe.wait_ge(ht_lo, 2 * (FB * layer + j0 + 1) + 2 * i)
                if last:
                    for m in range(TM):
                        four_slabs(pe, base + 8 * FB - 4, m,
                                   [(2 * m + n, 2 * k, False, k == 1) for n in range(2) for k in range(2)],
                                   left_f, acc_ready)
                    return
                for n in range(2):
                    for k in range(2):
                        slab_product(pe, base + 8 * j0 + 8 + 2 * n + k,
                                     (n, 2 + n), left_f, 2 * k, first and k == 0, False, i)

            def first_four(r, at, s0):
                for m in range(TM):
                    norm_pe(pe, r, at, m)
                    four_slabs(pe, s0, m, [(4 + m, 2 * k, k == 0, k == 3) for k in range(4)], left_x)

            def mlp(base, layer):
                first_four(2 * layer, (XT_LN0, XT_LN2)[layer], base)

                def step(i, j0, first):
                    pe.wait_ge(h_relu, TM * (FB * layer + j0 + 1) + TM * i)
                    hidden_slabs(base + 8 * j0 + 4, (0, 1), i)
                    hidden_transposes(layer, i, j0)
                    hidden_slabs(base + 8 * j0 + 4, (2, 3), i)
                    down(base, layer, i, j0, first=first)

                step(0, 0, True)
                with pe.Fori(0, FB - 2) as j:
                    step(j, 1, False)
                hidden_transposes(layer, 0, FB - 1)
                down(base, layer, 0, FB - 1, last=True)

            mlp(MLP_A, 0)

            first_four(1, XT_LN1, OD_IN)
            pe.wait_ge(wb_split, 2)
            for m in range(TM):
                rows = slice(m * P, m * P + P)
                for k in range(KC):
                    o = ps[:, 1, 16 * m:16 * m + 16]
                    pe.matmul(o, xh[:, k, rows], wbh[:, k, :], start=k == 0, stop=False)
                    pe.matmul(o, xh[:, k, rows], wbl[:, k, :], start=False, stop=False)
                    ins = pe.matmul(o, xl[:, k, rows], wbh[:, k, :], start=False, stop=k == KC - 1)
            ins.then_inc(ba_ps, 1)

            def od_project(g):
                b = 4 + 2 * (g % 2)
                if g >= 2:
                    pe.wait_ge(g1_row, TM * (g - 1))
                for k in range(4 if g else 0):
                    slab_product(pe, OD_IN + 4 * g + k, (b, b + 1), left_x, 2 * k, k == 0, k == 3)

            def od_transposes(g):
                pe.wait_ge(g1_row, TM * (g + 1))
                if g:
                    pe.wait_ge(conv_done, g)
                for c in range(4):
                    for m in range(TM):
                        ins = pe.transpose(ps[:, 2 + c // 2, (c % 2) * SEQ + m * P:(c % 2) * SEQ + m * P + P],
                                           stage[:, g % 2, m, c * P:c * P + P], ident)
                ins.then_inc(t1_ps, 1)

            one = cst[:, C_ONE:C_ONE + 1]

            def lengths(g):
                pe.wait_ge(sq_done, g + 1)
                for c in range(4):
                    for m in range(TM):
                        i = 2 * (4 * g + c) + m
                        ins = pe.matmul(ps[:, 0, i:i + 1], sqT[:, c, m * P:m * P + P], one, start=True, stop=True)
                ins.then_inc(ss_ps, 1)

            for g in range(8):
                od_project(g)
                if 1 <= g <= 6:
                    od_transposes(g - 1)
                if 3 <= g <= 6:
                    lengths(g - 3)

            up, same = cst[:, C_UP:C_UP + P], cst[:, C_SAME:C_SAME + P]
            pe.wait_ge(s_cst, 32)
            pe.wait_ge(g_ready, 1)
            for m in range(TM):
                gr = sm[GR][:, m, :]
                pe.matmul(ps[:, 1, 32 + 8 * m:40 + 8 * m], up, gr, start=True, stop=True)
                pe.matmul(ps[:, 1, 48 + 8 * m:56 + 8 * m], same, gr, start=True, stop=True)
                for c in range(2):
                    n = 2 * m + c
                    ins = pe.matmul(ps[:, 1, 64 + 8 * n:72 + 8 * n], cst[:, C_CH + c * P:C_CH + c * P + P], gr,
                                    start=True, stop=True)
            ins.then_inc(cum_ps, 1)
            pe.wait_ge(g1_row, TM * 8)
            for b in range(4):
                m, h0, base = b // 2, 4 * (b % 2), 2 + 3 * (b % 2)
                rows = slice(m * P, m * P + P)
                if b >= 2:
                    pe.wait_ge(nt_ready, b - 1)
                for h in range(4):
                    c = slice(h * P, h * P + P)
                    pe.matmul(ps[:, base, c], sm[GR][:, m, h0 + h:h0 + h + 1].to_broadcast([P, P]), up,
                              start=True, stop=True)
                    pe.matmul(ps[:, base + 1, c], kTd[:, h0 + h, rows], kTd[:, h0 + h, rows], start=True, stop=True)
                    ins = pe.matmul(ps[:, base + 2, c], kTd[:, h0 + h, rows], qTd[:, h0 + h, rows],
                                    start=True, stop=True)
                ins.then_inc(kk_ps, 1)
            pe.wait_ge(nt_ready, 4)
            pe.wait_ge(v_silu, 2)
            for m in range(TM):
                for v, src in ((0, vTd), (1, kTd)):
                    if m:
                        pe.wait_ge(rows_sb, 2 * m - 1 + v)
                    for h in range(CH):
                        ins = pe.transpose(ps[:, 4 + 2 * v + h // 4, (h % 4) * P:(h % 4) * P + P],
                                           src[:, h, m * P:m * P + P], ident)
                    ins.then_inc(rows_ps, 1)
            pe.wait_ge(t_init, 1)

            def level_first(lev, b):
                m, h0, n = b // 2, 4 * (b % 2), 4 * lev + b
                if n >= 4:
                    pe.wait_ge(t_done, n - 3)
                if n >= 2:
                    pe.wait_ge(xx_ready, n - 1)
                for h in range(4):
                    ins = pe.matmul(ps[:, b % 2, h * P:h * P + P], NT[:, m, h0 + h, :], T[:, m, h0 + h, :],
                                    start=True, stop=True)
                ins.then_inc(nt_ps, 1)

            def level_second(lev, b):
                m, h0, n = b // 2, 4 * (b % 2), 4 * lev + b
                pe.wait_ge(xx_ready, n + 1)
                if n >= 1:
                    pe.wait_ge(t_done, n)
                for h in range(4):
                    c = slice(h * P, h * P + P)
                    pe.matmul(ps[:, 2, c], TT[:, m, h0 + h, :], XX[:, b % 2, h, :], start=True, stop=True)
                    ins = pe.matmul(ps[:, 3, c], XX[:, b % 2, h, :], TT[:, m, h0 + h, :], start=True, stop=True)
                ins.then_inc(tx_ps, 1)

            for lev in range(LEVELS):
                level_first(lev, 0)
                for b in range(4):
                    if b < 3:
                        level_first(lev, b + 1)
                    level_second(lev, b)
            pe.wait_ge(t_done, 4 * LEVELS)
            pe.wait_ge(rows_sb, 4)
            for b in range(4):
                m, h0 = b // 2, 4 * (b % 2)
                for h in range(4):
                    ins = pe.matmul(ps[:, 4 + b, h * P:h * P + P], kw[:, m, h0 + h, :], TT[:, m, h0 + h, :],
                                    start=True, stop=True)
                ins.then_inc(wt_ps, 1)
            pe.wait_ge(wt_sb, 4)
            for n in range(4):
                m, par_ = n // 2, n % 2
                rows = slice(CK * par_, CK * par_ + CK)
                for h in range(CH):
                    o = ps[rows, h // 4, (h % 4) * P:(h % 4) * P + P]
                    if n and h == 0:
                        pe.wait_ge(s_ready, n)
                        pe.wait_ge(vnew_done, n)
                    ins = pe.matmul(o, TT[:, m, h, rows], dv[:, m, h, :], start=True, stop=n == 0)
                    if n:
                        ins = pe.matmul(o, WT[:, m, h, rows], S[n][:, h, :], start=False, stop=True)
                ins.then_inc(v_ps, 1)
                if n:
                    if n == 2:
                        pe.wait_ge(o_sum, 1)
                    for h in range(CH):
                        ins = pe.matmul(ps[rows, 4 + h // 4, (h % 4) * P:(h % 4) * P + P],
                                        qTd[:, h, CK * n:CK * n + CK], S[n][:, h, :], start=True, stop=True)
                pe.wait_ge(vnew_done, n + 1)
                if n == 3:
                    pe.wait_ge(xt_lo, XT_GDN + 2)
                if n < 3:
                    for h in range(CH):
                        ins = pe.matmul(ps[:, 2 + h // 4, (h % 4) * P:(h % 4) * P + P], kdec[rows, m, h, :],
                                        vnew[rows, m, h, :], start=True, stop=True)
                    ins.then_inc(kv_ps, 1)
                if n == 2:
                    pe.wait_ge(o_rows, 1)
                    xt_transposes(pe, 0, (6, 7), gate)
                if par_:
                    for h in range(CH):
                        ins = pe.matmul(ps[:, 6 + h // 4, (h % 4) * P:(h % 4) * P + P], intraT[:, m, h, :],
                                        vnew[:, m, h, :], start=True, stop=True)
                    ins.then_inc(o2_ps, 1)
            def out_slabs(n, m):
                four_slabs(pe, OD_OUT + 4 * n, m, [(2 * m + n, 2 * k, k == 0, k == 3) for k in range(4)],
                           left_x, acc_ready)

            out_slabs(0, 0)
            pe.wait_ge(o_rows, TM)
            xt_transposes(pe, 1, (4, 5), gate)
            pe.wait_ge(xt_lo, XT_GDN + 4)
            out_slabs(0, 1)
            out_slabs(1, 0)
            out_slabs(1, 1)
            mlp(MLP_B, 1)



def constant_tile():
    import numpy as np
    c = np.zeros((P, C_W), np.float32)
    i, j = np.arange(P)[:, None], np.arange(P)[None, :]
    same = i // CK == j // CK
    c[:, C_ID:C_ID + P] = i == j
    c[:, C_UP:C_UP + P] = same & (i <= j)
    c[:, C_SAME:C_SAME + P] = same
    c[:, C_NEG:C_NEG + P] = np.where(same & (i <= j), 0.0, NEG)
    for lev in range(LEVELS):
        b = 2 ** lev
        c[:, C_LVL + lev * P:C_LVL + lev * P + P] = (i // (2 * b) == j // (2 * b)) & (i // b % 2 == 1) & (j // b % 2 == 0)
    for n in range(2):
        c[:, C_CH + n * P:C_CH + n * P + P] = i // CK == n
    c[:, C_T:C_T + 16] = np.arange(16)
    c[:, C_T + 16:C_T + 32] = 16 * np.arange(16)
    c[:, C_ONE:C_ONE + 2] = 1.0
    c[:, C_FLIP:C_FLIP + P] = i + j == P - 1
    for n in range(2):
        c[:, C_PAR + n:C_PAR + n + 1] = i // SH % 2 == n
    return c


def bucket_rows():
    import numpy as np
    d = 255 - np.arange(GW)
    n = np.maximum(d, 0)
    exact = BUCKETS // 2
    nf = np.maximum(n, 1).astype(np.float32)
    large = exact + (np.log(nf / np.float32(exact)) / np.float32(math.log(128 / exact)) * (BUCKETS - exact)).astype(np.int32)
    bucket = np.where(n < exact, n, np.minimum(large, BUCKETS - 1))
    h = np.zeros((BUCKETS + 1, GW), np.float32)
    h[np.where(d >= 0, bucket, BUCKETS), np.arange(GW)] = 1.0
    return h


_INS = ['x', 'rel_table', 'ev_w_in', 'ev_w_out', 's5_lambda_re', 's5_lambda_im', 's5_b_re', 's5_b_im',
        's5_c_re', 's5_c_im', 's5_d', 's5_log_dt', 's5_w_glu', 's5_b_glu', 'od_w_in', 'od_conv_w',
        'od_a_log', 'od_dt_bias', 'od_norm_w', 'od_w_out', 'ln_mix_g', 'ln_mix_b', 'mlp_w1', 'mlp_w2',
        'ln_ffn_g', 'ln_ffn_b']
_OUTS = [((1, SEQ, DM), 'float32')]


def kernel(**inputs):
    import numpy as _np
    import concourse.bacc as _bacc
    from concourse import mybir as _mybir
    from concourse.bass_utils import run_bass_kernel_spmd as _run

    nc = _bacc.Bacc("TRN2", target_bir_lowering=False, num_devices=1)
    arrays, args = {}, []
    given = {n: inputs[n] for n in _INS} | {"consts": constant_tile(), "onehot": bucket_rows()}
    for name, a in given.items():
        a = _np.ascontiguousarray(a)
        arrays[f"in_{name}_dram"] = a
        args.append(nc.dram_tensor(f"in_{name}_dram", a.shape, _mybir.dt.from_np(a.dtype), kind="ExternalInput").ap())
    for i, (shape, dtype) in enumerate(_OUTS):
        dt = _mybir.dt.from_np(_np.dtype(dtype))
        args.append(nc.dram_tensor(f"out_{i}_dram", shape, dt, kind="ExternalOutput").ap())
    build(nc, *args)
    r = _run(nc, [arrays], core_ids=[0])
    return r.results[0]["out_0_dram"]
```

```python
import math
from contextlib import ExitStack

import concourse.bass as bass
from concourse import mybir

P = 128
SEQ = 256
DM = 1024
TM = SEQ // P
KC = DM // P
NW = 512
AH, AD = 8, 64
AW = AH * AD
SG, SH, SN = 32, 16, 64
SW = SG * SH
NJ = SG // 2
CH, CD, CONV, CK = 8, 128, 4, 64
FF = 4 * DM
FB = FF // NW
ALPHA = 4.0 ** 0.25
LN_EPS, RMS_EPS, L2_EPS = 1e-5, 1e-6, 1e-6
NEG = -1e30
BUCKETS = 32
GW = 384
ROUND = 1.5 * 2.0 ** 23
ROUND16 = 1.5 * 2.0 ** 9
TWO_PI = 2 * math.pi
PI_A, PI_B = 6.28125, 1.9350051879882812e-3
PI_C = TWO_PI - PI_A - PI_B

RAW, SPL = 8, 4
EV_IN, EV_OUT, GLU = 0, 16, 20
MLP_A = 26
OD_IN = MLP_A + 8 * FB
OD_OUT = OD_IN + 32
MLP_B = OD_OUT + 8
SLABS = MLP_B + 8 * FB

C_ID, C_UP, C_SAME, C_NEG, C_PAIR = 0, 128, 256, 384, 512
C_LVL = C_PAIR + P
LEVELS = 5
HP = P // 2
C_CH = C_LVL + LEVELS * HP
C_T = C_CH + 2 * P
C_ONE = C_T + 32
C_FLIP = C_ONE + 2
C_PAR = C_FLIP + P
C_W = C_PAR + 2


def build(nc, x, rel_table, ev_w_in, ev_w_out, lam_re, lam_im, b_re, b_im, c_re, c_im, s5_d,
          log_dt, w_glu, b_glu, od_w_in, conv_w, a_log, dt_bias, norm_w, od_w_out,
          ln_mix_g, ln_mix_b, mlp_w1, mlp_w2, ln_ffn_g, ln_ffn_b, consts, onehot, out):
    f32, f32r = mybir.dt.float32, mybir.dt.float32r
    ALU, ACT, AX = mybir.AluOpType, mybir.ActivationFunctionType, mybir.AxisListType
    MUL, ADD, SUB, MAX = ALU.mult, ALU.add, ALU.subtract, ALU.max

    ctx = ExitStack()
    with ctx:
        def sb(name, shape, dt=f32):
            return ctx.enter_context(nc.sbuf_tensor(name, shape, dt))

        def sem(name):
            return ctx.enter_context(nc.semaphore(name))

        raw = sb("raw", [P, RAW, 2, NW])
        whi = sb("whi", [P, SPL, 2, NW], f32r)
        wlo = sb("wlo", [P, SPL, 2, NW], f32r)
        xrow = sb("xrow", [P, TM, DM])
        xh = sb("xh", [P, KC, SEQ], f32r)
        xl = sb("xl", [P, KC, SEQ], f32r)
        fh = sb("fh", [P, 4, SEQ], f32r)
        fl = sb("fl", [P, 4, SEQ], f32r)
        stage = sb("stage", [P, 2, TM, NW])
        cst = sb("cst", [P, C_W])
        lnp = sb("lnp", [P, 2, DM])
        lns = sb("lns", [P, TM, 2, 6])
        lnm = sb("lnm", [P, TM, 2])
        lnr = sb("lnr", [P, TM])
        arena = sb("arena", [P, 22000])
        ps = ctx.enter_context(nc.psum_tensor("ps", [P, 8, NW], f32))

        ident = cst[:, C_ID:C_ID + P]

        class Carve:
            def __init__(self):
                self.at = 0

            def __call__(self, *shape, rows=P):
                n = int(math.prod(shape))
                v = arena[0:rows, self.at:self.at + n]
                self.at += n
                if len(shape) == 1:
                    return v
                names = "abcd"[:len(shape)]
                return v.rearrange(f"p ({' '.join(names)}) -> p {' '.join(names)}",
                                   **dict(zip(names, shape)))

        A = Carve()
        uT, qT, kT = A(4, SEQ), A(4, SEQ), A(4, SEQ)
        vrow = A(TM, AW)
        bias = A(AH, GW)
        tab33 = A(AH, rows=BUCKETS + 1)
        att_s, att_p, att_pt = A(GW), A(GW), A(GW)
        hot, biasrow = att_s[0:BUCKETS + 1], att_p[0:AH]
        att_nm, att_sum, att_rs = A(2 * AH), A(TM, AH), A(TM, AH)
        yT, zs = A(4, SEQ), A(4, SEQ)
        early1 = stage[:, 1].rearrange("p a b -> p (a b)")
        lamr, lami, lrd, th, nn, rr, den, s1 = (early1[0:NJ, P * k:P * k + P] for k in range(8))
        s2, aim, ar1, t16 = (yT.rearrange("p a b -> p (a b)")[0:NJ, P * k:P * k + P] for k in range(4))
        prow = yT[0:104, 3, 0:P]
        par16 = zs.rearrange("p a b -> p (a b)")[0:NJ, 0:5 * P].rearrange("p (a b) -> p a b", a=5)
        ldt = A(2, rows=NJ)
        par = A(5, NJ)
        ph, pr = A(NJ, 32), A(NJ, 32)
        sint, cost = A(NJ, 32), A(NJ, 32)
        bre, bim, btmp, btm2 = (vrow.rearrange("p a b -> p (a b)")[:, 256 * k:256 * k + 256]
                                .rearrange("p (a b) -> p a b", a=NJ) for k in range(4))
        craw = kT.rearrange("p a b -> p (a b)")[:, 0:2 * 4 * SN].rearrange("p (a b c) -> p a b c", a=2, b=4)
        bpad = lnp[:, 0, :].rearrange("p (a b c) -> p a b c", a=2, b=NJ)
        bT = A(2, 4, P)
        uTh, uTl = fh, fl
        bTh, bTl = (v[:, 4:8, :].rearrange("p a (b c) -> p (a b) c", b=2)
                    .rearrange("p (r c) n -> p r c n", r=2) for v in (xh, xl))
        cpad = lnp[:, 1, :].rearrange("p (a b c) -> p a b c", a=2, b=4)
        cT = A(2, 4, P)
        tcos, tsin, ttmp = A(2, 2, SEQ), A(2, 2, SEQ), A(2, SEQ)
        pa, pb, pc, pd = A(2, SEQ), A(2, SEQ), A(2, SEQ), A(2, SEQ)
        gre, gim = A(2, SEQ), A(2, SEQ)
        hre, him = A(2, SEQ), A(2, SEQ)
        sre, sim = (v.rearrange("p a b -> p (a b)").rearrange("p (a b) -> p a b", a=2) for v in (pr, ph))
        params = sb("params", [P, 104])
        half_pi = sb("half_pi", [P, 1])

        A = Carve()
        convT = A(24, SEQ)
        kTd, qTd, vTd = convT[:, 0:8, :], convT[:, 8:16, :], convT[:, 16:24, :]
        gate = A(TM, DM)
        dv, kw, kdec = A(TM, CH, CD), A(TM, CH, CD), A(TM, CH, CD)
        NT, intraT = A(TM, CH, P), A(TM, CH, P)
        TT = A(TM, CH, P)
        T = vTd.rearrange("p a (b c) -> p (a b) c", b=2).rearrange("p (m h) c -> p m h c", m=TM)
        XX = lnp[:, 0, :].rearrange("p (a b c) -> p a b c", a=4, b=4)
        dec = A(2, 4, P)
        SM = A(24, TM, CH)
        sm = [SM[:, i] for i in range(24)]
        (BETA, XG, AXX, E1, W1, LW, DD, EQ, GR, EG, NEGEG, EKD, GC, IK, RK, DINV, SSK, SSQ, RQ, BRK2,
         BRK, CC, BB) = range(23)
        ba_b = sm[BB]
        baT = kw[0:16, 0].rearrange("p a b -> p (a b)")[:, 0:SEQ]
        WT = T
        vnew = kTd.rearrange("p a (b c) -> p (a b) c", b=2).rearrange("p (m h) c -> p m h c", m=TM)
        S = [None, NT[:, 0], NT[:, 1], lnp[:, 1, :].rearrange("p (a b) -> p a b", a=CH)]
        obuf = [XX.rearrange("p a b c -> p (a b c)"), kdec[:, 0].rearrange("p a b -> p (a b)")]
        sqT = kdec[:, 0].rearrange("p a b -> p (a b)").rearrange("p (a b) -> p a b", a=4)

        def osq(m):
            return intraT[:, m].rearrange("p a b -> p (a b)")

        wba = sb("wba", [P, KC, 16])
        nw = sb("nw", [P, CD])
        wbh = sb("wbh", [P, KC, 16], f32r)
        wbl = sb("wbl", [P, KC, 16], f32r)
        alog = sb("alog", [P, CH])
        dtb = sb("dtb", [P, CH])
        egl = sb("egl", [P, 4, CH])
        scratch = nc.dram_tensor("bias_rows", [AH, GW], f32, kind="Internal").ap()

        loaded = [sem(f"slab_loaded{i}") for i in range(RAW)]
        hi_ready = sem("hi_ready")
        lo_ready = sem("lo_ready")
        slab_used = sem("slab_used")
        ub_hi, ub_lo = sem("u_and_b_hi"), sem("u_and_b_lo")
        s_x = [sem(f"x_loaded{m}") for m in range(TM)]
        acc_ready = sem("acc_ready")
        s_cst, s_small, s_lnp = sem("consts_loaded"), sem("small_loaded"), sem("lnp_loaded")
        s_bias_in, s_bias_out = sem("bias_rows_stored"), sem("bias_loaded")
        s_out = sem("out_stored")
        s_l1 = sem("layer1_small_loaded")
        s_zero, s_c, c_padded, s_ident = sem("pads_cleared"), sem("c_loaded"), sem("c_padded"), sem("ident_loaded")
        dve_ch, act_ch, pool_ch = sem("dve_chain"), sem("act_chain"), sem("pool_chain")
        xt_ps, xt_hi, xt_lo = sem("xt_in_psum"), sem("xt_hi"), sem("xt_lo")
        ln_var, ln_rstd, ln_done = sem("ln_var"), sem("ln_rstd"), sem("ln_done")
        h_row, ht_ps, ht_hi, ht_lo = sem("h_rows"), sem("ht_in_psum"), sem("ht_hi"), sem("ht_lo")
        g_row, t_ps, t_sb = sem("proj_rows"), sem("projT_in_psum"), sem("projT")

        s_tab, s_prow, s_b, s_wba, wb_split = (
            sem("s_tab"), sem("s_prow"), sem("s_b"), sem("s_wba"), sem("wb_split"))
        tab_ready, phases_ready, rot_ready, rot_done, scan_done = (
            sem("tab_ready"), sem("phases_ready"), sem("rot_ready"), sem("rot_done"), sem("scan_done"))
        unrot_sin, unrot_cos, states_ready, h_relu = (
            sem("unrot_sin"), sem("unrot_cos"), sem("states_ready"), sem("h_relu"))
        t_init, tt_ps, tt_sb, t_first, conv_first = (
            sem("tt_init"), sem("tt_ps"), sem("tt_sb"), sem("t_first"), sem("conv_first"))
        gate_w, s5_dt, s5_ang, s5_mag = (
            sem("gate_w"), sem("s5_dt"), sem("s5_ang"), sem("s5_mag"))
        s5_par, par_ps, prow_ps, bias_ps, bias_row_sb = (
            sem("s5_par"), sem("par_ps"), sem("prow_ps"), sem("bias_ps"), sem("bias_row_sb"))
        params_sb, ph_done, b_padded, b_ps, bT_sb = (
            sem("params_sb"), sem("ph_done"), sem("b_padded"), sem("b_ps"), sem("bT_sb"))
        c_ps, cT_sb, x_ps, y_done, y_sum = (
            sem("c_ps"), sem("cT_sb"), sem("x_ps"), sem("y_done"), sem("y_sum"))
        gelu_hi, gelu_lo, z_sig, ssm_rows = (
            sem("gelu_hi"), sem("gelu_lo"), sem("z_sig"), sem("ssm_rows"))
        ssm_hi, ssm_lo, att_sc, att_max, att_exp = (
            sem("ssm_hi"), sem("ssm_lo"), sem("att_sc"), sem("att_max"), sem("att_exp"))
        att_pt_ps, att_pt_sb, att_o, att_rows, conv_done = (
            sem("att_pt_ps"), sem("att_pt_sb"), sem("att_o"), sem("att_rows"), sem("conv_done"))
        sq_done, ss_ps, v_silu, t1_ps, g1_row = (
            sem("sq_done"), sem("ss_ps"), sem("v_silu"), sem("t1_ps"), sem("g1_row"))
        baT_ps, baT_sb = sem("baT_ps"), sem("baT_sb")
        ba_ps, ba_sb, gate_exp, cum_ps, cum_exp = (
            sem("ba_ps"), sem("ba_sb"), sem("gate_exp"), sem("cum_ps"), sem("cum_exp"))
        g_ready, dec_in, dec_ready, norm_in, norm_out = (
            sem("g_ready"), sem("dec_in"), sem("dec_ready"), sem("norm_in"), sem("norm_out"))
        kk_ps, nt_ready, rows_ps, rows_sb, nt_ps = (
            sem("kk_ps"), sem("nt_ready"), sem("rows_ps"), sem("rows_sb"), sem("nt_ps"))
        xx_ready, tx_ps, t_done, wt_ps, wt_sb = (
            sem("xx_ready"), sem("tx_ps"), sem("t_done"), sem("wt_ps"), sem("wt_sb"))
        v_ps, vnew_done, kv_ps, s_ready, o2_ps = (
            sem("v_ps"), sem("vnew_done"), sem("kv_ps"), sem("s_ready"), sem("o2_ps"))
        o2_sb, o_state, o_sum, o_sq, rms_in, rms_out = (
            sem("o2_sb"), sem("o_state"), sem("o_sum"), sem("o_sq"), sem("rms_in"), sem("rms_out"))
        gated = sem("gated")
        o_rows, s_scaled = sem("o_rows"), sem("states_scaled")

        block = ctx.enter_context(nc.Block())

        def psq(b, n=1):
            return ps[:, b:b + n, :].rearrange("p a b -> p (a b)")

        def in_slab(w, col, k):
            return w[256 * k:256 * k + 256, col:col + NW].rearrange("(a p) n -> p a n", p=P)

        EV_COLS = [3 * AW, 0, AW, 2 * AW]
        OD_COLS = [DM, DM + NW, 0, NW, 2 * DM, 2 * DM + NW, 3 * DM, 3 * DM + NW]

        FIRST_SPLIT = 3

        def x_bank(q):
            return 0 if q < 7 else 4

        def hi(act, s, i=0):
            act.wait_ge(loaded[s % RAW], 16 * (s // RAW + 1) + 16 * i)
            if s >= SPL:
                act.wait_ge(slab_used, s - SPL + 1 + 8 * i)
            act.activation(whi[:, s % SPL], raw[:, s % RAW], ACT.Copy).then_inc(hi_ready, 1)

        def lo(dve, s, i=0):
            dve.wait_ge(hi_ready, s + 1 + 8 * i)
            dve.tensor_tensor(wlo[:, s % SPL], raw[:, s % RAW], whi[:, s % SPL].bitcast(f32),
                              SUB).then_inc(lo_ready, 1)

        def row_product(pe, s, m, bank, left, k0, first, last):
            lh, ll = left
            q, rows, o = s % SPL, slice(m * P, m * P + P), ps[:, bank, :]
            for kk in range(2):
                a, b = first and kk == 0, last and kk == 1
                pe.matmul(o, lh[:, k0 + kk, rows], whi[:, q, kk, :], start=a, stop=False)
                pe.matmul(o, lh[:, k0 + kk, rows], wlo[:, q, kk, :], start=False, stop=False)
                ins = pe.matmul(o, ll[:, k0 + kk, rows], whi[:, q, kk, :], start=False, stop=b)
            return ins

        def slab_product(pe, s, banks, left, k0, first, last, i=0):
            pe.wait_ge(lo_ready, s + 1 + 8 * i)
            for m in range(TM):
                ins = row_product(pe, s, m, banks[m], left, k0, first, last)
            ins.then_inc(slab_used, 1)

        def four_slabs(pe, s0, m, steps, left, acc=None, halfway=None):
            for k, (bank, k0, first, last) in enumerate(steps):
                if k == 2 and halfway is not None:
                    halfway()
                if m == 0:
                    pe.wait_ge(lo_ready, s0 + k + 1)
                ins = row_product(pe, s0 + k, m, bank, left, k0, first, last)
                if m == TM - 1:
                    ins.then_inc(slab_used, 1)
                elif acc is not None and last:
                    ins.then_inc(acc, 1)

        def xt_transposes(pe, m, banks, src):
            for q, bank in enumerate(banks):
                for j in range(4):
                    c = 4 * q + j
                    ins = pe.transpose(ps[:, bank, j * P:j * P + P], src[:, m, c * P:c * P + P], ident)
                ins.then_inc(xt_ps, 1)

        XT_X, XT_ATT, XT_LN0, XT_LN1, XT_GDN, XT_LN2 = 0, 4, 6, 10, 14, 18

        def xt_upper(act, at, m, banks):
            for q, bank in enumerate(banks):
                act.wait_ge(xt_ps, at + q + 1)
                act.activation(xh[:, 4 * q:4 * q + 4, m * P:m * P + P],
                               ps[:, bank, :].rearrange("p (a b) -> p a b", a=4), ACT.Copy).then_inc(xt_hi, 1)

        def xt_lower(dve, at, m, banks):
            for q, bank in enumerate(banks):
                dve.wait_ge(xt_hi, at + q + 1)
                dve.tensor_tensor(xl[:, 4 * q:4 * q + 4, m * P:m * P + P],
                                  ps[:, bank, :].rearrange("p (a b) -> p a b", a=4),
                                  xh[:, 4 * q:4 * q + 4, m * P:m * P + P].bitcast(f32), SUB).then_inc(xt_lo, 1)

        SUM_END = (GLU + 6, MLP_A + 8 * FB, OD_OUT + 8, MLP_B + 8 * FB)
        LAST_HALF = (2, 2, 4, 2)

        def ln_stats(dve, r, m, chain):
            for j in range(2):
                if m == 0:
                    dve.wait_ge(acc_ready, 2 * r + j + 1)
                else:
                    dve.wait_ge(slab_used, SUM_END[r] - (LAST_HALF[r] if j == 0 else 0))
                half = xrow[:, m, j * NW:j * NW + NW]
                chain(dve.scalar_tensor_tensor(half, half, ALPHA, ps[:, 2 * m + j, :], MUL, ADD))
                ins = dve.bn_stats(lns[:, m, j, :], half)
            chain(ins)
            chain(dve.bn_aggr(lnm[:, m, :], lns[:, m, :, :]))
            chain(dve.tensor_scalar(lnr[:, m:m + 1], lnm[:, m, 1:2], LN_EPS, None, ADD))
            dve.reciprocal(lnr[:, m:m + 1], lnr[:, m:m + 1]).then_inc(ln_var, 1)

        def ln_sqrt(act, r, m):
            act.wait_ge(ln_var, 2 * r + m + 1)
            act.activation(lnr[:, m:m + 1], lnr[:, m:m + 1], ACT.Sqrt).then_inc(ln_rstd, 1)

        def ln_apply(dve, r, m, chain):
            if m == 0:
                dve.wait_ge(s_lnp, 32 * (r + 1))
            chain(dve.scalar_tensor_tensor(xrow[:, m, :], xrow[:, m, :], lnm[:, m, 0:1], lnp[:, 0, :],
                                           SUB, MUL))
            dve.wait_ge(ln_rstd, 2 * r + m + 1)
            dve.scalar_tensor_tensor(xrow[:, m, :], xrow[:, m, :], lnr[:, m:m + 1], lnp[:, 1, :],
                                     MUL, ADD).then_inc(ln_done, 1)

        def norm_act(act, r, at, s0):
            ln_sqrt(act, r, 0)
            for s in range(s0, s0 + 4):
                hi(act, s)
            xt_upper(act, at, 0, (4, 5))
            ln_sqrt(act, r, 1)
            xt_upper(act, at + 2, 1, (6, 7))

        def norm_dve(dve, r, at, chain):
            ln_stats(dve, r, 0, chain)
            ln_apply(dve, r, 0, chain)
            ln_stats(dve, r, 1, chain)
            xt_lower(dve, at, 0, (4, 5))
            ln_apply(dve, r, 1, chain)
            xt_lower(dve, at + 2, 1, (6, 7))

        def norm_pe(pe, r, at, m):
            pe.wait_ge(ln_done, TM * r + m + 1)
            xt_transposes(pe, m, (4 + 2 * m, 5 + 2 * m), xrow)

        @block.sync
        def _(sp):
            def load(s, src, i=0):
                if s >= RAW:
                    sp.wait_ge(lo_ready, s - RAW + 1 + 8 * i)
                sp.dma_start(raw[:, s % RAW], src).then_inc(loaded[s % RAW], 16)

            def load_row(s, w, row, col, i=0):
                load(s, w[bass.ds(row, 256), bass.ds(col, NW)].rearrange("(a p) n -> p a n", p=P), i)

            for m in range(TM):
                sp.dma_start(xrow[:, m, :], x[0, m * P:m * P + P, :]).then_inc(s_x[m], 16)
            for g in range(4):
                for k in range(4):
                    load(EV_IN + 4 * g + k, in_slab(ev_w_in[0], EV_COLS[g], k))
            for n in range(2):
                for k in range(2):
                    load(EV_OUT + 2 * n + k, in_slab(ev_w_out[0], n * NW, k))
            for k in range(2):
                load(GLU + k, in_slab(w_glu[0], 0, k))
            for n in range(2):
                for k in range(2):
                    load(GLU + 2 + 2 * n + k, in_slab(ev_w_out[0], n * NW, 2 + k))

            def mlp_loads(base, layer):
                w1, w2 = mlp_w1[layer], mlp_w2[layer]
                for k in range(4):
                    load(base + k, in_slab(w1, 0, k))
                with sp.Fori(0, FB - 1) as j:
                    for k in range(4):
                        load_row(base + 4 + k, w1, 256 * k, NW * j + NW, j)
                    for n in range(2):
                        for k in range(2):
                            load_row(base + 8 + 2 * n + k, w2, NW * j + 256 * k, NW * n, j)
                for n in range(2):
                    for k in range(2):
                        load(base + 8 * FB - 4 + 2 * n + k, in_slab(w2, NW * n, 2 * (FB - 1) + k))

            mlp_loads(MLP_A, 0)
            for g in range(8):
                for k in range(4):
                    load(OD_IN + 4 * g + k, in_slab(od_w_in[0], OD_COLS[g], k))
            for n in range(2):
                for k in range(4):
                    load(OD_OUT + 4 * n + k, in_slab(od_w_out[0], n * NW, k))
            mlp_loads(MLP_B, 1)
            for m in range(TM):
                sp.wait_ge(ln_done, 6 + m + 1)
                sp.dma_start(out[0, m * P:m * P + P, :], xrow[:, m, :]).then_inc(s_out, 16)
            sp.wait_ge(s_out, 16 * TM)


        def chained(eng, s):
            n = [0]

            def chain(ins):
                n[0] += 1
                ins.then_inc(s, 1)
                eng.wait_ge(s, n[0])
            return chain

        def tile4(v, b):
            return v[:, b // 2, 4 * (b % 2):4 * (b % 2) + 4, :]

        def left(v, lev):
            return v.rearrange("p h (c two b) -> p h c two b", two=2, b=2 ** lev)[:, :, :, 0, :]

        def half_bank(b, k, lev):
            return ps[:, b, SEQ * k:SEQ * k + SEQ].rearrange("p (h c b) -> p h c b", h=4, b=2 ** lev)

        @block.gpsimd
        def _(pool):
            chain = chained(pool, pool_ch)
            chain(pool.memset(tab33[BUCKETS:BUCKETS + 1, :], NEG))
            chain(pool.memset(bpad.rearrange("p a b c -> p (a b c)"), 0.0))
            chain(pool.memset(half_pi[:, :], math.pi / 2))
            pool.sem_inc(s_zero, 1)
            pool.wait_ge(s_cst, 32)
            pool.wait_ge(s_c, 32)
            for r in range(2):
                for g in range(2):
                    ins = pool.tensor_scalar(cpad[:, r, :, SN * g:SN * g + SN], craw[:, r],
                                             cst[:, C_PAR + g:C_PAR + g + 1], None, MUL)
            ins.then_inc(c_padded, 1)

            def tables(q):
                j, t = 2 * q, q % 2
                fine = [v[:, j:j + 2, 0:16].unsqueeze(2).to_broadcast([P, 2, 16, 16]) for v in (cost, sint)]
                rough = [v[:, j:j + 2, 16:32].unsqueeze(3).to_broadcast([P, 2, 16, 16]) for v in (cost, sint)]
                tc, ts_, tt = [v.rearrange("p j (a b) -> p j a b", a=16) for v in (tcos[:, t], tsin[:, t], ttmp)]
                if q:
                    pool.wait_ge(tab_ready, q)
                if q >= 2:
                    pool.wait_ge(unrot_cos, q - 1)
                    pool.wait_ge(unrot_sin, q - 1)
                pool.tensor_tensor(tc, rough[0], fine[0], MUL)
                chain(pool.tensor_tensor(tt, rough[1], fine[1], MUL))
                chain(pool.tensor_tensor(tc, tc, tt, SUB))
                pool.tensor_tensor(ts_, rough[1], fine[0], MUL)
                chain(pool.tensor_tensor(tt, rough[0], fine[1], MUL))
                pool.tensor_tensor(ts_, ts_, tt, ADD).then_inc(tab_ready, 1)

            pool.wait_ge(phases_ready, 2)
            tables(0)
            tables(1)
            for q in range(NJ // 2):
                pool.wait_ge(scan_done, q + 1)
                if q:
                    pool.wait_ge(states_ready, q)
                pool.tensor_tensor(sre, tsin[:, q % 2], gim, MUL)
                pool.tensor_tensor(sim, tsin[:, q % 2], gre, MUL).then_inc(unrot_sin, 1)
                if q + 2 < NJ // 2:
                    tables(q + 2)

            def squares(layer, i=0, j0=0):
                for m in range(TM):
                    pool.wait_ge(h_relu, TM * (FB * layer + j0) + m + 1 + TM * i)
                    pool.tensor_tensor(stage[:, 0, m, :], stage[:, 0, m, :], stage[:, 0, m, :],
                                       MUL).then_inc(h_row, 1)

            for s in range(MLP_A, MLP_A + 4):
                lo(pool, s)
            with pool.Fori(0, FB) as j:
                squares(0, j)
            for s in range(OD_IN, OD_IN + 4):
                lo(pool, s)
            for b in range(4):
                pool.wait_ge(nt_ready, b + 1)
                pair = cst[:, C_PAIR:C_PAIR + P].unsqueeze(1).to_broadcast([P, 4, P])
                chain(pool.tensor_tensor(tile4(TT, b), tile4(NT, b), pair, MUL))
                pool.tensor_tensor(tile4(TT, b), tile4(TT, b), ident.unsqueeze(1).to_broadcast([P, 4, P]),
                                   ADD).then_inc(t_init, 1)
            pool.wait_ge(g1_row, TM * 8)
            for m in range(TM):
                g3 = gate[:, m, :].rearrange("p (h d) -> p h d", h=CH)
                ins = pool.tensor_tensor(g3, g3, nw[:, :].unsqueeze(1).to_broadcast([P, CH, CD]), MUL)
            ins.then_inc(gate_w, 1)
            pool.wait_ge(gate_w, 1)
            for n in (1, 2):
                for hh in range(2):
                    heads = slice(4 * hh, 4 * hh + 4)
                    pool.wait_ge(s_ready, 2 * n + hh - 1)
                    pool.tensor_tensor(S[n + 1][:, heads, :], S[n][:, heads, :],
                                       egl[:, n, heads].unsqueeze(2).to_broadcast([P, 4, CD]),
                                       MUL).then_inc(s_scaled, 1)
            for m in range(TM):
                pool.wait_ge(o_sum, m + 1)
                pool.tensor_tensor(gate[:, m, :], gate[:, m, :], obuf[m], MUL).then_inc(gated, 1)
            for s in range(MLP_B, MLP_B + 4):
                lo(pool, s)
            with pool.Fori(0, FB) as j:
                squares(1, j)

        @block.scalar
        def _(act):
            chain = chained(act, act_ch)
            act.dma_start(ldt, log_dt[0].rearrange("(j g) -> j g", g=2)).then_inc(s_small, 16)
            act.dma_start(lamr, lam_re[0].rearrange("(j g) n -> j (g n)", g=2)).then_inc(s_small, 16)
            act.dma_start(lami, lam_im[0].rearrange("(j g) n -> j (g n)", g=2)).then_inc(s_small, 16)
            act.dma_start(cst[:, 0:C_UP], consts[:, 0:C_UP]).then_inc(s_ident, 16)
            act.dma_start(tab33[0:BUCKETS, :], rel_table).then_inc(s_tab, 16)
            act.dma_start(hot, onehot).then_inc(s_tab, 16)
            act.dma_start(cst[:, C_PAIR:], consts[:, C_PAIR:]).then_inc(s_cst, 16)
            act.dma_start(prow[0:96, :], conv_w[0].rearrange("k (c p) -> (k c) p", p=P)).then_inc(s_prow, 16)
            act.dma_start(prow[96:100, :], s5_d[0].rearrange("(c p) -> c p", p=P)).then_inc(s_prow, 16)
            act.dma_start(prow[100:104, :], b_glu[0].rearrange("(c p) -> c p", p=P)).then_inc(s_prow, 16)
            for r, src in enumerate((c_re, c_im)):
                act.dma_start(craw[:, r], src[0].rearrange("(c g) h n -> (g h) c n", g=8)).then_inc(s_c, 16)

            def rows_out(g, dst):
                for m in range(TM):
                    act.wait_ge(slab_used, EV_IN + 4 * g + 4)
                    act.activation(dst[:, m, :], ps[:, 4 + m, :], ACT.Copy).then_inc(g_row, 1)

            def transposed_out(g, dst, scale):
                act.wait_ge(t_ps, g + 1)
                act.activation(dst.rearrange("p a b -> p (a b)"), psq(2, 2), ACT.Copy,
                               scale=scale).then_inc(t_sb, 1)

            act.wait_ge(s_small, 48)
            act.activation(ldt, ldt, ACT.Exp).then_inc(s5_dt, 1)
            for m in range(TM):
                xt_upper(act, XT_X + 2 * m, m, (4 + 2 * m, 5 + 2 * m))
            for s in range(4):
                hi(act, s)
            act.dma_start(bre, b_re[0].rearrange("(j g) n h -> (g n) j h", g=2)).then_inc(s_b, 16)
            act.dma_start(bim, b_im[0].rearrange("(j g) n h -> (g n) j h", g=2)).then_inc(s_b, 16)
            act.dma_start(cst[:, C_UP:C_PAIR], consts[:, C_UP:C_PAIR]).then_inc(s_cst, 16)
            act.dma_start(wba[:, :, :], od_w_in[0][:, 4 * DM:4 * DM + 16].rearrange("(a p) n -> p a n", p=P)).then_inc(s_wba, 16)
            act.dma_start(alog[:, :], a_log.to_broadcast([P, CH])).then_inc(s_l1, 16)
            act.dma_start(dtb[:, :], dt_bias.to_broadcast([P, CH])).then_inc(s_l1, 16)
            act.dma_start(nw[:, :], norm_w.to_broadcast([P, CD])).then_inc(s_l1, 16)
            hi(act, 4)
            act.wait_ge(s5_ang, 1)
            act.activation(par16[:, 0, :], lrd, ACT.Exp).then_inc(s5_mag, 1)
            act.activation(s1, rr, ACT.Sin).then_inc(s5_mag, 1)
            act.activation(s2, t16, ACT.Sin).then_inc(s5_mag, 1)
            hi(act, 5)
            hi(act, 6)
            rows_out(0, stage[:, 0])
            hi(act, 7)
            hi(act, 8)
            transposed_out(0, uT, 1.0)
            hi(act, 9)
            act.wait_ge(bias_row_sb, 1)
            act.dma_start(scratch, biasrow).then_inc(s_bias_in, 16)
            hi(act, 10)
            rows_out(1, stage[:, 1])
            hi(act, 11)
            act.wait_ge(s_bias_in, 16)
            for off, c0, n in ((P, 0, P), (0, P, SEQ)):
                act.dma_start(bias[:, :, c0:c0 + n],
                              bass.AP(tensor=scratch.tensor, offset=off,
                                      ap=[[1, P], [GW, AH], [1, n]])).then_inc(s_bias_out, 16)
            act.wait_ge(ph_done, 1)
            act.wait_ge(s_zero, 1)
            act.activation(sint, ph, ACT.Sin, scale=6.283185).then_inc(phases_ready, 1)
            chain(act.activation(pr, ph, ACT.Abs))
            act.activation(cost, pr, ACT.Sin, scale=-6.283185, bias=half_pi[:, 0:1]).then_inc(phases_ready, 1)
            hi(act, 12)
            hi(act, 13)
            hi(act, 14)
            rows_out(2, stage[:, 0])
            transposed_out(1, qT, AD ** -0.5)
            hi(act, 15)
            hi(act, EV_OUT)
            hi(act, EV_OUT + 1)
            hi(act, EV_OUT + 2)
            transposed_out(2, kT, 1.0)
            rows_out(3, vrow)
            act.activation(uTh[:, :, :], uT, ACT.Copy).then_inc(ub_hi, 1)
            act.activation(bTh, bT, ACT.Copy).then_inc(ub_hi, 1)
            hi(act, EV_OUT + 3)
            act.wait_ge(s_wba, 16)
            act.activation(wbh[:, :, :], wba[:, :, :], ACT.Copy).then_inc(wb_split, 1)

            for h in range(AH):
                act.wait_ge(att_max, h + 1)
                if h >= 1:
                    act.wait_ge(att_pt_ps, h)
                for m in range(TM):
                    c0, n = (0, P) if m == 0 else (P, SEQ)
                    ins = act.activation(att_p[:, c0:c0 + n], ps[:, 4, c0:c0 + n], ACT.Exp,
                                         bias=att_nm[:, 2 * h + m:2 * h + m + 1],
                                         accum_out=att_sum[:, m, h:h + 1])
                ins.then_inc(att_exp, 1)
                act.wait_ge(att_pt_ps, h + 1)
                if h >= 1:
                    act.wait_ge(att_o, h)
                act.activation(att_pt, ps[:, 5, 0:GW], ACT.Copy).then_inc(att_pt_sb, 1)
            for m in range(TM):
                xt_upper(act, XT_ATT + m, m, (4 + m,))

            hi(act, GLU)
            hi(act, GLU + 1)
            for c in range(4):
                act.wait_ge(y_sum, c + 1)
                chain(act.activation(yT[:, c, :], yT[:, c, :], ACT.Gelu_apprx_tanh))
                if c == 0:
                    act.wait_ge(x_ps, NJ // 2)
                act.activation(fh[:, c, :], yT[:, c, :], ACT.Copy).then_inc(gelu_hi, 1)
            hi(act, GLU + 2)
            hi(act, GLU + 3)
            for c in range(4):
                act.wait_ge(slab_used, GLU + 2)
                act.activation(zs[:, c, :], ps[:, 6 + c // 2, (c % 2) * SEQ:(c % 2) * SEQ + SEQ], ACT.Sigmoid,
                               bias=params[:, 100 + c:101 + c]).then_inc(z_sig, 1)
            for c in range(4):
                act.wait_ge(ssm_rows, c + 1)
                act.activation(xh[:, 4 + c, :], yT[:, c, :], ACT.Copy).then_inc(ssm_hi, 1)
            for s in range(GLU + 4, GLU + 6):
                hi(act, s)

            def lnp_load(g, b):
                for k, w in enumerate((g, b)):
                    act.dma_start(lnp[:, k, :], w.unsqueeze(0).to_broadcast([P, DM])).then_inc(s_lnp, 16)

            lnp_load(ln_mix_g[0], ln_mix_b[0])
            norm_act(act, 0, XT_LN0, MLP_A)
            act.wait_ge(ln_done, TM * 1)
            lnp_load(ln_ffn_g[0], ln_ffn_b[0])

            def relu(layer, i=0, j0=0):
                base = (MLP_A, MLP_B)[layer] + 8 * j0 + (0 if j0 else 4)
                for m in range(TM):
                    act.wait_ge(slab_used, base + 8 * i)
                    act.activation(stage[:, 0, m, :], ps[:, 4 + m, :], ACT.Relu).then_inc(h_relu, 1)

            def ht_upper(layer, i=0, j0=0):
                for q in range(2):
                    act.wait_ge(ht_ps, 2 * (FB * layer + j0) + q + 1 + 2 * i)
                    act.activation(fh[:, 2 * q:2 * q + 2, :],
                                   ps[:, 6 + q, :].rearrange("p (a b) -> p a b", a=2),
                                   ACT.Copy).then_inc(ht_hi, 1)

            def mlp(base, layer):
                relu(layer)
                for k in range(4, 8):
                    hi(act, base + k)

                with act.Fori(0, FB - 1) as j:
                    hi(act, base + 8, j)
                    hi(act, base + 9, j)
                    ht_upper(layer, j)
                    hi(act, base + 10, j)
                    hi(act, base + 11, j)
                    relu(layer, j, 1)
                    for k in range(12, 16):
                        hi(act, base + k, j)
                ht_upper(layer, 0, FB - 1)

            mlp(MLP_A, 0)

            norm_act(act, 1, XT_LN1, OD_IN)

            def conv_last_tap(g):
                act.wait_ge(t1_ps, g + 1)
                c0 = OD_COLS[g] // P
                for c in range(4):
                    i = 24 * (CONV - 1) + c0 + c
                    ins = act.activation(convT[:, 4 * g + c, :], ps[:, 2 + c // 2, (c % 2) * SEQ:(c % 2) * SEQ + SEQ],
                                         ACT.Copy, scale=params[:, i:i + 1])
                ins.then_inc(conv_first, 1)

            def conv_silu(g):
                act.wait_ge(conv_done, g + 1)
                v = convT[:, 4 * g:4 * g + 4, :]
                ins = act.activation(v, v, ACT.Silu)
                if g < 4:
                    chain(ins)
                    if g:
                        act.wait_ge(ss_ps, g)
                    act.activation(sqT, v, ACT.Square).then_inc(sq_done, 1)
                else:
                    ins.then_inc(v_silu, 1)

            def od_rows_out(g):
                b = 4 + 2 * (g % 2)
                if g >= 2:
                    act.wait_ge(t1_ps, min(g - 1, 6))
                for m in range(TM):
                    act.wait_ge(slab_used, OD_IN + 4 * g + 4)
                    if g < 6:
                        act.activation(stage[:, g % 2, m, :], ps[:, b + m, :], ACT.Copy).then_inc(g1_row, 1)
                    else:
                        act.activation(gate[:, m, (g - 6) * NW:(g - 5) * NW], ps[:, b + m, :],
                                       ACT.Silu).then_inc(g1_row, 1)

            for g in range(7):
                hi(act, OD_IN + 4 * (g + 1))
                if g == 1:
                    act.wait_ge(ba_sb, 3)
                    act.activation(sm[LW], sm[W1], ACT.Ln).then_inc(gate_exp, 1)
                hi(act, OD_IN + 4 * (g + 1) + 1)
                if g == 0:
                    act.wait_ge(baT_ps, 1)
                    act.activation(baT, ps[0:16, 0, 0:SEQ], ACT.Copy).then_inc(baT_sb, 1)
                if 1 <= g <= 6:
                    conv_last_tap(g - 1)
                for k in (2, 3):
                    hi(act, OD_IN + 4 * (g + 1) + k)
                if g == 6:
                    act.wait_ge(norm_in, 1)
                    act.activation(sm[RK], sm[IK], ACT.Sqrt).then_inc(norm_out, 1)
                    act.activation(sm[DINV], sm[SSK], ACT.Sqrt).then_inc(norm_out, 1)
                    act.activation(sm[RQ], sm[SSQ], ACT.Sqrt).then_inc(norm_out, 1)
                od_rows_out(g)
                if g == 0:
                    act.wait_ge(ba_sb, 1)
                    act.activation(sm[BETA], ba_b, ACT.Exp, scale=-1.0).then_inc(gate_exp, 1)
                    act.activation(alog[:, :], alog[:, :], ACT.Exp).then_inc(gate_exp, 1)
                    act.wait_ge(ba_sb, 2)
                    act.activation(sm[E1], sm[AXX], ACT.Exp, scale=-1.0).then_inc(gate_exp, 1)
                if g == 1:
                    act.wait_ge(ba_sb, 4)
                    act.activation(sm[EG], sm[GC], ACT.Exp).then_inc(cum_exp, 1)
                    act.activation(egl[:, :, :].rearrange("p a b -> p (a b)"), ps[:, 1, 64:96],
                                   ACT.Exp).then_inc(cum_exp, 1)
                    act.activation(sm[EKD], sm[EKD], ACT.Exp).then_inc(cum_exp, 1)
                if g >= 1:
                    conv_silu(g - 1)
            for b in range(4):
                act.wait_ge(dec_in, b + 1)
                act.activation(dec[:, b % 2], dec[:, b % 2], ACT.Exp).then_inc(dec_ready, 1)
            od_rows_out(7)

            def out_of_bank(b, dst, s):
                act.activation(tile4(dst, b), ps[:, 4 + b, :].rearrange("p (a b) -> p a b", a=4),
                               ACT.Copy).then_inc(s, 1)
            for b in range(4):
                act.wait_ge(tt_ps, b + 1)
                out_of_bank(b, T, t_first)
            for n in range(4, 4 * LEVELS + 4):
                act.wait_ge(tt_ps, n + 1)
                out_of_bank(n % 4, TT, tt_sb)
            for b in range(4):
                act.wait_ge(wt_ps, b + 1)
                out_of_bank(b, WT, wt_sb)
            for s in range(OD_OUT, OD_OUT + 4):
                hi(act, s)
            for m in range(TM):
                if m == 0:
                    act.wait_ge(o2_ps, 1)
                    act.activation(obuf[0], psq(6, 2), ACT.Copy).then_inc(o2_sb, 1)
                act.wait_ge(o_sum, m + 1)
                act.activation(osq(m), obuf[m], ACT.Square).then_inc(o_sq, 1)
                act.wait_ge(rms_in, m + 1)
                act.activation(sm[CC][:, m, :], sm[CC][:, m, :], ACT.Sqrt).then_inc(rms_out, 1)
                if m == 0:
                    act.wait_ge(o2_ps, 2)
                    act.activation(obuf[1], psq(6, 2), ACT.Copy).then_inc(o2_sb, 1)
                    xt_upper(act, XT_GDN, 0, (2, 3))
            act.wait_ge(o_rows, TM)
            lnp_load(ln_mix_g[1], ln_mix_b[1])
            xt_upper(act, XT_GDN + 2, 1, (4, 5))
            for s in range(OD_OUT + 4, OD_OUT + 8):
                hi(act, s)
            norm_act(act, 2, XT_LN2, MLP_B)
            act.wait_ge(ln_done, TM * 3)
            lnp_load(ln_ffn_g[1], ln_ffn_b[1])
            mlp(MLP_B, 1)
            for m in range(TM):
                ln_sqrt(act, 3, m)

        @block.vector
        def _(dve):
            chain = chained(dve, dve_ch)
            for m in range(TM):
                xt_lower(dve, XT_X + 2 * m, m, (4 + 2 * m, 5 + 2 * m))
            for s in range(4):
                lo(dve, s)
            dve.wait_ge(s5_dt, 1)
            dtb3 = ldt.unsqueeze(2).to_broadcast([NJ, 2, SN])

            def v3(a):
                return a.rearrange("p (g n) -> p g n", g=2)

            chain(dve.tensor_scalar(lamr, lamr, -1e-4, None, ALU.min))
            dve.tensor_tensor(v3(lrd), v3(lamr), dtb3, MUL)
            chain(dve.tensor_tensor(v3(th), v3(lami), dtb3, MUL))
            chain(dve.tensor_scalar(nn, th, 1 / TWO_PI, ROUND, MUL, ADD))
            chain(dve.tensor_scalar(nn, nn, ROUND, None, SUB))
            chain(dve.scalar_tensor_tensor(rr, nn, -PI_A, th, MUL, ADD))
            chain(dve.scalar_tensor_tensor(rr, nn, -PI_B, rr, MUL, ADD))
            chain(dve.scalar_tensor_tensor(rr, nn, -PI_C, rr, MUL, ADD))
            chain(dve.tensor_scalar(rr, rr, 3.1415925, -3.1415925, ALU.min, MAX))
            dve.tensor_scalar(t16, rr, 0.5, None, MUL).then_inc(s5_ang, 1)
            lo(dve, 4)
            dve.tensor_tensor(den, lamr, lamr, MUL)
            chain(dve.tensor_tensor(th, lami, lami, MUL))
            chain(dve.tensor_tensor(den, den, th, ADD))
            chain(dve.reciprocal(den, den))
            lo(dve, 5)
            dve.wait_ge(s5_mag, 3)
            mag = par16[:, 0, :]
            chain(dve.tensor_tensor(s2, s2, s2, MUL))
            chain(dve.tensor_scalar(ar1, s2, -2.0, 1.0, MUL, ADD))
            dve.tensor_tensor(aim, mag, s1, MUL)
            chain(dve.tensor_tensor(ar1, ar1, mag, MUL))
            chain(dve.tensor_scalar(ar1, ar1, 1.0, None, SUB))
            dve.tensor_tensor(th, ar1, lamr, MUL)
            chain(dve.tensor_tensor(s1, aim, lami, MUL))
            chain(dve.tensor_tensor(th, th, s1, ADD))
            dve.tensor_tensor(par16[:, 1, :], th, den, MUL)
            chain(dve.tensor_tensor(s1, aim, lamr, MUL))
            chain(dve.tensor_tensor(s2, ar1, lami, MUL))
            chain(dve.tensor_tensor(s1, s1, s2, SUB))
            dve.tensor_tensor(par16[:, 2, :], s1, den, MUL)
            chain(dve.tensor_scalar(rr, rr, 1 / TWO_PI, None, MUL))
            chain(dve.tensor_scalar(par16[:, 3, :], rr, ROUND16, ROUND16, ADD, SUB))
            dve.tensor_tensor(par16[:, 4, :], rr, par16[:, 3, :], SUB).then_inc(s5_par, 1)
            lo(dve, 6)
            lo(dve, 7)
            dve.wait_ge(par_ps, 1)
            chain(dve.tensor_copy(par.rearrange("p a b -> p (a b)"), ps[:, 0, 0:5 * NJ]))
            dve.wait_ge(prow_ps, 1)
            dve.tensor_copy(params[:, :], ps[:, 0, 128:232]).then_inc(params_sb, 1)
            dve.wait_ge(bias_ps, 1)
            dve.tensor_copy(biasrow, ps[0:AH, 1, 0:GW]).then_inc(bias_row_sb, 1)
            lo(dve, 8)
            dve.wait_ge(s_b, 32)
            dve.wait_ge(s_zero, 1)

            def coef(k):
                return par[:, k, :].unsqueeze(2).to_broadcast([P, NJ, SH])
            for r, (b1, b2, op) in enumerate(((bre, bim, SUB), (bim, bre, ADD))):
                dve.tensor_tensor(btmp, coef(1), b1, MUL)
                chain(dve.tensor_tensor(btm2, coef(2), b2, MUL))
                for g in range(2):
                    rows = slice(SN * g, SN * g + SN)
                    ins = dve.tensor_tensor(bpad[rows, r, :, SH * g:SH * g + SH], btmp[rows], btm2[rows], op)
                chain(ins)
            dve.sem_inc(b_padded, 1)
            lo(dve, 9)
            def perp(k):
                return par[:, k, :].unsqueeze(2).to_broadcast([P, NJ, 32])
            tv = cst[:, C_T:C_T + 32].unsqueeze(1).to_broadcast([P, NJ, 32])
            chain(dve.tensor_tensor(ph, perp(3), tv, MUL))
            for step in range(2):
                chain(dve.tensor_scalar(pr, ph, ROUND, ROUND, ADD, SUB))
                chain(dve.tensor_tensor(ph, ph, pr, SUB))
                if step == 0:
                    chain(dve.tensor_tensor(pr, perp(4), tv, MUL))
                    chain(dve.tensor_tensor(ph, ph, pr, ADD))
            dve.sem_inc(ph_done, 1)
            lo(dve, 10)
            lo(dve, 11)
            dve.wait_ge(b_ps, 1)
            dve.tensor_copy(bT.rearrange("p a b c -> p (a b c)"), psq(2, 2)).then_inc(bT_sb, 1)
            dve.wait_ge(c_ps, 1)
            dve.tensor_copy(cT[:, 0].rearrange("p b c -> p (b c)"), psq(0))
            dve.tensor_scalar(cT[:, 1].rearrange("p b c -> p (b c)"), psq(1), -1.0, None, MUL).then_inc(cT_sb, 1)


            def rotate(q):
                tc, ts_ = tcos[:, q % 2], tsin[:, q % 2]
                x0 = x_bank(q)
                xre, xim = ps[:, x0:x0 + 2, 0:SEQ], ps[:, x0:x0 + 2, SEQ:2 * SEQ]
                dve.wait_ge(x_ps, q + 1)
                dve.wait_ge(tab_ready, q + 1)
                dve.tensor_tensor(pa, xre, tc, MUL)
                dve.tensor_tensor(pb, xim, ts_, MUL)
                dve.tensor_tensor(pc, xim, tc, MUL)
                dve.tensor_tensor(pd, xre, ts_, MUL).then_inc(rot_ready, 1)
                dve.wait_ge(rot_ready, q + 1)
                dve.tensor_tensor(pa, pa, pb, ADD)
                dve.tensor_tensor(pc, pc, pd, SUB).then_inc(rot_done, 1)

            def scans(q):
                dve.wait_ge(rot_done, q + 1)
                if q >= 1:
                    dve.wait_ge(unrot_sin, q)
                for jj in range(2):
                    decay = par[:, 0, 2 * q + jj:2 * q + jj + 1].to_broadcast([P, SEQ])
                    dve.tensor_tensor_scan(gre[:, jj, :], decay, pa[:, jj, :], 0.0, MUL, ADD)
                    ins = dve.tensor_tensor_scan(gim[:, jj, :], decay, pc[:, jj, :], 0.0, MUL, ADD)
                ins.then_inc(scan_done, 1)
                dve.wait_ge(scan_done, q + 1)
                tc = tcos[:, q % 2]
                if q >= 1:
                    dve.wait_ge(y_done, q)
                dve.tensor_tensor(hre, tc, gre, MUL)
                dve.tensor_tensor(him, tc, gim, MUL).then_inc(unrot_cos, 1)

            def unrotate(q):
                dve.wait_ge(unrot_cos, q + 1)
                dve.wait_ge(unrot_sin, q + 1)
                dve.tensor_tensor(hre, hre, sre, SUB)
                dve.tensor_tensor(him, him, sim, ADD).then_inc(states_ready, 1)

            def skip_sum(c):
                dve.wait_ge(y_done, 2 * c + 2)
                dve.scalar_tensor_tensor(yT[:, c, :], uT[:, c, :], params[:, 96 + c:97 + c],
                                         ps[:, 6 + c % 2, 0:SEQ], MUL, ADD).then_inc(y_sum, 1)

            def head(h):
                dve.wait_ge(att_sc, h + 1)
                dve.reduce_max(att_nm[:, 2 * h:2 * h + 1], ps[:, 4, 0:P], AX.X)
                chain(dve.reduce_max(att_nm[:, 2 * h + 1:2 * h + 2], ps[:, 4, P:GW], AX.X))
                dve.tensor_scalar(att_nm[:, 2 * h:2 * h + 2], att_nm[:, 2 * h:2 * h + 2], -1.0, None,
                                  MUL).then_inc(att_max, 1)

            rotate(0)
            lo(dve, 12)
            scans(0)
            lo(dve, 13)
            rotate(1)
            unrotate(0)
            lo(dve, 14)
            lo(dve, 15)
            lo(dve, EV_OUT)
            for q in range(1, NJ // 2):
                scans(q)
                if q == 7:
                    lo(dve, GLU + 1)
                if q < 7:
                    rotate(q + 1)
                if q <= 4:
                    head(2 * q - 2)
                if q == 5:
                    dve.wait_ge(att_exp, AH)
                    chain(dve.reciprocal(att_rs.rearrange("p a b -> p (a b)"),
                                         att_sum.rearrange("p a b -> p (a b)")))
                    dve.wait_ge(att_o, AH)
                    for m in range(TM):
                        dve.tensor_tensor(stage[:, 1, m, :].rearrange("p (h d) -> p h d", h=AH),
                                          ps[:, 2 + m, :].rearrange("p (h d) -> p h d", h=AH),
                                          att_rs[:, m, :].unsqueeze(2).to_broadcast([P, AH, AD]),
                                          MUL).then_inc(att_rows, 1)
                unrotate(q)
                if q == 5:
                    for m in range(TM):
                        xt_lower(dve, XT_ATT + m, m, (4 + m,))
                if q == 1:
                    dve.wait_ge(ub_hi, 2)
                    dve.tensor_tensor(uTl[:, :, :], uT, uTh[:, :, :].bitcast(f32), SUB)
                    dve.tensor_tensor(bTl, bT, bTh.bitcast(f32), SUB).then_inc(ub_lo, 1)
                if q <= 4:
                    head(2 * q - 1)
                if q <= 3:
                    lo(dve, EV_OUT + q)
                if q % 2 == 0:
                    skip_sum(q // 2 - 1)
                if q == 6:
                    lo(dve, GLU)
            skip_sum(3)

            for c in range(4):
                dve.wait_ge(gelu_hi, c + 1)
                dve.tensor_tensor(fl[:, c, :], yT[:, c, :], fh[:, c, :].bitcast(f32), SUB).then_inc(gelu_lo, 1)
            lo(dve, GLU + 2)
            lo(dve, GLU + 3)
            for c in range(4):
                dve.wait_ge(z_sig, c + 1)
                dve.tensor_tensor(yT[:, c, :], yT[:, c, :], zs[:, c, :], MUL).then_inc(ssm_rows, 1)
            for c in range(4):
                dve.wait_ge(ssm_hi, c + 1)
                dve.tensor_tensor(xl[:, 4 + c, :], yT[:, c, :], xh[:, 4 + c, :].bitcast(f32), SUB).then_inc(ssm_lo, 1)
            for s in range(GLU + 4, GLU + 6):
                lo(dve, s)
            dve.wait_ge(wb_split, 1)
            dve.tensor_tensor(wbl[:, :, :], wba[:, :, :], wbh[:, :, :].bitcast(f32), SUB).then_inc(wb_split, 1)
            norm_dve(dve, 0, XT_LN0, chain)

            def ht_lower(layer, i=0, j0=0):
                for q in range(2):
                    dve.wait_ge(ht_hi, 2 * (FB * layer + j0) + q + 1 + 2 * i)
                    dve.tensor_tensor(fl[:, 2 * q:2 * q + 2, :],
                                      ps[:, 6 + q, :].rearrange("p (a b) -> p a b", a=2),
                                      fh[:, 2 * q:2 * q + 2, :].bitcast(f32), SUB).then_inc(ht_lo, 1)

            def mlp(base, layer):
                dve.wait_ge(lo_ready, base + 4)
                for k in range(4, 8):
                    lo(dve, base + k)
                with dve.Fori(0, FB - 1) as j:
                    lo(dve, base + 8, j)
                    lo(dve, base + 9, j)
                    ht_lower(layer, j)
                    lo(dve, base + 10, j)
                    lo(dve, base + 11, j)
                    for k in range(12, 16):
                        lo(dve, base + k, j)
                ht_lower(layer, 0, FB - 1)

            mlp(MLP_A, 0)

            norm_dve(dve, 1, XT_LN1, chain)
            dve.wait_ge(lo_ready, OD_IN + 4)
            def conv(g):
                dve.wait_ge(conv_first, g + 1)
                c0 = OD_COLS[g] // P
                for tap in range(CONV - 2, -1, -1):
                    d = CONV - 1 - tap
                    for c in range(4):
                        w = params[:, 24 * tap + c0 + c:24 * tap + c0 + c + 1]
                        src = ps[:, 2 + c // 2, (c % 2) * SEQ:(c % 2) * SEQ + SEQ - d]
                        o = convT[:, 4 * g + c, d:SEQ]
                        ins = dve.scalar_tensor_tensor(o, src, w, o, MUL, ADD)
                    if tap:
                        chain(ins)
                ins.then_inc(conv_done, 1)

            def gates_start():
                dve.wait_ge(ba_ps, 1)
                dve.wait_ge(s_l1, 48)
                ba = ps[:, 1, 0:32].rearrange("p (m c) -> p m c", m=TM)
                dve.tensor_copy(ba_b, ba[:, :, 0:CH]).then_inc(ba_sb, 1)
                chain(dve.tensor_tensor(sm[XG], ba[:, :, CH:2 * CH],
                                        dtb[:, :].unsqueeze(1).to_broadcast([P, TM, CH]), ADD))
                chain(dve.tensor_scalar(sm[AXX], sm[XG], -1.0, None, MUL))
                dve.tensor_tensor(sm[AXX], sm[AXX], sm[XG], MAX).then_inc(ba_sb, 1)

            def gates_middle():
                dve.wait_ge(gate_exp, 3)
                chain(dve.tensor_scalar(sm[BETA], sm[BETA], 1.0, None, ADD))
                dve.reciprocal(sm[BETA], sm[BETA])
                dve.tensor_scalar(sm[W1], sm[E1], 1.0, None, ADD).then_inc(ba_sb, 1)
                dve.wait_ge(ba_sb, 3)
                chain(dve.tensor_scalar(sm[DD], sm[W1], 1.0, None, SUB))
                chain(dve.tensor_scalar(sm[EQ], sm[DD], 0.0, None, ALU.is_equal))
                chain(dve.tensor_tensor(sm[DD], sm[DD], sm[EQ], ADD))
                chain(dve.reciprocal(sm[DD], sm[DD]))
                chain(dve.tensor_tensor(sm[E1], sm[E1], sm[DD], MUL))

            def gates_end():
                dve.wait_ge(gate_exp, 4)
                chain(dve.tensor_tensor(sm[LW], sm[LW], sm[EQ], ADD))
                chain(dve.tensor_tensor(sm[E1], sm[E1], sm[LW], MUL))
                chain(dve.scalar_tensor_tensor(sm[GR], sm[XG], 0.0, sm[E1], MAX, ADD))
                dve.scalar_tensor_tensor(sm[GR], sm[GR], -1.0, alog[:, :].unsqueeze(1).to_broadcast([P, TM, CH]),
                                         MUL, MUL).then_inc(g_ready, 1)

            def sums_out():
                dve.wait_ge(cum_ps, 1)
                chain(dve.tensor_copy(sm[GC], ps[:, 1, 32:48].rearrange("p (a b) -> p a b", a=2)))
                dve.tensor_tensor(sm[EKD], ps[:, 1, 48:64].rearrange("p (a b) -> p a b", a=2), sm[GC],
                                  SUB).then_inc(ba_sb, 1)

            def norms():
                dve.wait_ge(ss_ps, 4)
                ss = ps[:, 0, 0:32].rearrange("p (c m) -> p m c", m=TM)
                dve.tensor_scalar(sm[SSK], ss[:, :, 0:CH], L2_EPS, None, ADD)
                chain(dve.tensor_scalar(sm[SSQ], ss[:, :, CH:2 * CH], L2_EPS, None, ADD))
                dve.reciprocal(sm[SSQ], sm[SSQ])
                chain(dve.reciprocal(sm[IK], sm[SSK]))
                dve.tensor_tensor(sm[BRK2], sm[BETA], sm[IK], MUL).then_inc(norm_in, 1)

            for g in range(7):
                lo(dve, OD_IN + 4 * (g + 1))
                if g == 1:
                    gates_end()
                if g == 6:
                    norms()
                lo(dve, OD_IN + 4 * (g + 1) + 1)
                if g >= 1:
                    conv(g - 1)
                lo(dve, OD_IN + 4 * (g + 1) + 2)
                if g == 1:
                    sums_out()
                lo(dve, OD_IN + 4 * (g + 1) + 3)
                if g == 0:
                    gates_start()
                    gates_middle()

            negm = cst[:, C_NEG:C_NEG + P]
            dve.wait_ge(norm_out, 3)

            def decay_logs(b):
                m, h0, base = b // 2, 4 * (b % 2), 3 * (b % 2)
                dve.wait_ge(kk_ps, b + 1)
                if b >= 2:
                    dve.wait_ge(nt_ready, b - 1)
                for h in range(4):
                    ins = dve.scalar_tensor_tensor(dec[:, b % 2, h, :], ps[:, base, h * P:h * P + P],
                                                   sm[GC][:, m, h0 + h:h0 + h + 1], negm, SUB, ADD)
                ins.then_inc(dec_in, 1)

            def decayed(b):
                m, h0, base = b // 2, 4 * (b % 2), 3 * (b % 2)
                dve.wait_ge(dec_ready, b + 1)
                for h in range(4):
                    dve.scalar_tensor_tensor(intraT[:, m, h0 + h, :], ps[:, base + 2, h * P:h * P + P],
                                             sm[RK][:, m, h0 + h:h0 + h + 1], dec[:, b % 2, h, :], MUL, MUL)
                for h in range(4):
                    ins = dve.scalar_tensor_tensor(NT[:, m, h0 + h, :], ps[:, base + 1, h * P:h * P + P],
                                                   sm[BRK2][:, m, h0 + h:h0 + h + 1], dec[:, b % 2, h, :], MUL, MUL)
                ins.then_inc(nt_ready, 1)

            decay_logs(0)
            dve.wait_ge(cum_exp, 3)
            dve.tensor_tensor(sm[BRK], sm[BETA], sm[RK], MUL)
            dve.tensor_tensor(sm[EKD], sm[EKD], sm[RK], MUL)
            dve.tensor_scalar(sm[NEGEG], sm[EG], -1.0, None, MUL)
            chain(dve.tensor_scalar(sm[RQ], sm[RQ], CD ** -0.5, None, MUL))
            decay_logs(1)
            decayed(0)
            decayed(1)
            decay_logs(2)
            decay_logs(3)
            decayed(2)
            decayed(3)

            def rowb(v, m):
                return v[:, m, :].unsqueeze(2).to_broadcast([P, CH, CD])
            for m in range(TM):
                dve.wait_ge(rows_ps, 2 * m + 1)
                dve.tensor_tensor(dv[:, m], psq(0, 2).rearrange("p (a b) -> p a b", a=CH),
                                  rowb(sm[DINV], m), MUL).then_inc(rows_sb, 1)
                dve.wait_ge(rows_ps, 2 * m + 2)
                kr = psq(2 + 2 * m, 2).rearrange("p (a b) -> p a b", a=CH)
                dve.tensor_tensor(kw[:, m], kr, rowb(sm[NEGEG], m), MUL)
                dve.tensor_tensor(kdec[:, m], kr, rowb(sm[EKD], m), MUL).then_inc(rows_sb, 1)

            def mask_level(lev):
                c = C_LVL + (lev - 1) * HP
                mask = cst[:, c:c + HP].unsqueeze(1).to_broadcast([P, 4, HP])
                for b in range(4):
                    dve.wait_ge(nt_ps, 4 * lev + b - 3)
                    dve.tensor_tensor(XX[:, b], ps[:, b, 0:SEQ].rearrange("p (a b) -> p a b", a=4), mask,
                                      MUL).then_inc(xx_ready, 1)

            mask_level(1)
            for lev in range(1, LEVELS + 1):
                for b in range(4):
                    dve.wait_ge(tx_ps, 4 * lev + b - 3)
                    t = left(tile4(T, b), lev)
                    dve.tensor_tensor(t, t, half_bank(b, 1, lev), SUB).then_inc(t_done, 1)
                if lev < LEVELS:
                    mask_level(lev + 1)

            def new_values(n):
                m, rows = n // 2, slice(CK * (n % 2), CK * (n % 2) + CK)
                for hh in range(2):
                    heads = slice(4 * hh, 4 * hh + 4)
                    dve.wait_ge(v_ps, 2 * n + hh + 1)
                    dve.tensor_tensor(vnew[rows, m, heads], ps[rows, hh, :].rearrange("p (a b) -> p a b", a=4),
                                      sm[BRK][rows, m, heads].unsqueeze(2).to_broadcast([CK, 4, CD]),
                                      MUL).then_inc(vnew_done, 1)

            def next_state(n):
                for hh in range(2):
                    s4 = S[n + 1][:, 4 * hh:4 * hh + 4, :]
                    kv = ps[:, 2 + hh, :].rearrange("p (a b) -> p a b", a=4)
                    dve.wait_ge(kv_ps, 2 * n + hh + 1)
                    if n:
                        dve.wait_ge(s_scaled, 2 * n + hh - 1)
                        dve.tensor_tensor(s4, s4, kv, ADD).then_inc(s_ready, 1)
                    else:
                        dve.tensor_copy(s4, kv).then_inc(s_ready, 1)

            def out_state_part(m):
                rr_, nr = (slice(0, P), P) if m else (slice(CK, P), CK)
                dve.wait_ge(o2_ps, m + 1)
                dve.tensor_tensor(osq(m)[rr_].rearrange("p (a b) -> p a b", a=CH),
                                  psq(4, 2)[rr_].rearrange("p (a b) -> p a b", a=CH),
                                  sm[EG][rr_, m, :].unsqueeze(2).to_broadcast([nr, CH, CD]), MUL).then_inc(o_state, 1)

            def out_sum(m):
                rr_ = slice(0, P) if m else slice(CK, P)
                dve.wait_ge(o_state, m + 1)
                dve.wait_ge(o2_sb, m + 1)
                dve.tensor_tensor(obuf[m][rr_], obuf[m][rr_], osq(m)[rr_], ADD).then_inc(o_sum, 1)

            def out_norm(m):
                dve.wait_ge(o_sq, m + 1)
                cc, rq = sm[CC][:, m, :], sm[RQ][:, m, :]
                chain(dve.reduce_sum(cc, osq(m).rearrange("p (a b) -> p a b", a=CH), AX.X))
                chain(dve.tensor_tensor(cc, cc, rq, MUL))
                chain(dve.tensor_tensor(cc, cc, rq, MUL))
                chain(dve.tensor_scalar(cc, cc, 1.0 / CD, RMS_EPS, MUL, ADD))
                dve.reciprocal(cc, cc).then_inc(rms_in, 1)

            def out_gate(m):
                cc, rq = sm[CC][:, m, :], sm[RQ][:, m, :]
                dve.wait_ge(rms_out, m + 1)
                chain(dve.tensor_tensor(cc, cc, rq, MUL))
                dve.wait_ge(gated, m + 1)
                g3 = gate[:, m, :].rearrange("p (a b) -> p a b", a=CH)
                dve.tensor_tensor(g3, g3, cc.unsqueeze(2).to_broadcast([P, CH, CD]), MUL).then_inc(o_rows, 1)

            new_values(0)
            for s in range(OD_OUT, OD_OUT + 2):
                lo(dve, s)
            next_state(0)
            new_values(1)
            lo(dve, OD_OUT + 2)
            next_state(1)
            out_state_part(0)
            new_values(2)
            lo(dve, OD_OUT + 3)
            next_state(2)
            out_sum(0)
            new_values(3)
            out_norm(0)
            out_gate(0)
            out_state_part(1)
            out_sum(1)
            xt_lower(dve, XT_GDN, 0, (2, 3))
            out_norm(1)
            out_gate(1)
            xt_lower(dve, XT_GDN + 2, 1, (4, 5))
            for s in range(OD_OUT + 4, OD_OUT + 8):
                lo(dve, s)
            norm_dve(dve, 2, XT_LN2, chain)
            mlp(MLP_B, 1)
            for m in range(TM):
                ln_stats(dve, 3, m, chain)
                ln_apply(dve, 3, m, chain)

        @block.tensor
        def _(pe):
            left_x, left_f = (xh, xl), (fh, fl)

            def project(g, ks=range(4)):
                if g >= 1 and ks[0] == 0:
                    pe.wait_ge(g_row, TM * g)
                for k in ks:
                    slab_product(pe, EV_IN + 4 * g + k, (4, 5), left_x, 2 * k, k == 0, k == 3)

            def transpose_rows(g):
                pe.wait_ge(g_row, TM * (g + 1))
                if g >= 1:
                    pe.wait_ge(t_sb, g)
                for c in range(4):
                    for m in range(TM):
                        ins = pe.transpose(ps[:, 2 + c // 2, (c % 2) * SEQ + m * P:(c % 2) * SEQ + m * P + P],
                                           stage[:, g % 2, m, c * P:c * P + P], ident)
                ins.then_inc(t_ps, 1)

            pe.wait_ge(s_ident, 16)
            for m in range(TM):
                pe.wait_ge(s_x[m], 16)
                xt_transposes(pe, m, (4 + 2 * m, 5 + 2 * m), xrow)
            pe.wait_ge(xt_lo, 4)
            project(0)
            pe.wait_ge(s_prow, 48)
            pe.transpose(ps[:, 0, 128:232], prow, ident[0:104, 0:104]).then_inc(prow_ps, 1)
            pe.wait_ge(s_tab, 32)
            pe.wait_ge(pool_ch, 1)
            pe.matmul(ps[0:AH, 1, 0:GW], tab33, hot, start=True, stop=True).then_inc(bias_ps, 1)
            project(1, (0, 1))
            transpose_rows(0)
            pe.wait_ge(s5_par, 1)
            for k in range(5):
                ins = pe.transpose(ps[:, 0, NJ * k:NJ * k + NJ], par16[:, k, :], ident[0:NJ, 0:NJ])
            ins.then_inc(par_ps, 1)
            project(1, (2, 3))
            pe.wait_ge(b_padded, 1)
            pe.wait_ge(t_sb, 1)
            for r in range(2):
                for c in range(4):
                    ins = pe.transpose(ps[:, 2 + r, c * P:c * P + P],
                                       bpad[:, r, 4 * c:4 * c + 4, :].rearrange("p a b -> p (a b)"), ident)
            ins.then_inc(b_ps, 1)
            pe.wait_ge(c_padded, 1)
            pe.wait_ge(bias_row_sb, 1)
            pe.wait_ge(params_sb, 1)
            for r in range(2):
                for c in range(4):
                    ins = pe.transpose(ps[:, r, c * P:c * P + P], cpad[:, r, c, :], ident)
            ins.then_inc(c_ps, 1)

            def inputs(q):
                if q == 0:
                    pe.wait_ge(t_sb, 1)
                    pe.wait_ge(cT_sb, 1)
                else:
                    pe.wait_ge(rot_ready, q)
                if q == FIRST_SPLIT:
                    pe.wait_ge(ub_lo, 1)
                c = q // 2
                for jj in range(2):
                    i = 2 * (q % 2) + jj
                    rows = slice(32 * i, 32 * i + 32)
                    for r in range(2):
                        o = ps[:, x_bank(q) + jj, r * SEQ:r * SEQ + SEQ]
                        if q < FIRST_SPLIT:
                            ins = pe.matmul(o, bT[rows, r, c, :], uT[rows, c, :], start=True, stop=True)
                        else:
                            pe.matmul(o, bTh[rows, r, c, :], uTh[rows, c, :], start=True, stop=False)
                            pe.matmul(o, bTh[rows, r, c, :], uTl[rows, c, :], start=False, stop=False)
                            ins = pe.matmul(o, bTl[rows, r, c, :], uTh[rows, c, :], start=False, stop=True)
                ins.then_inc(x_ps, 1)

            def outputs(q):
                c = q // 2
                pe.wait_ge(states_ready, q + 1)
                if c >= 2:
                    pe.wait_ge(y_sum, c - 1)
                for jj in range(2):
                    i = 2 * (q % 2) + jj
                    o = ps[32 * i:32 * i + 32, 6 + c % 2, 0:SEQ]
                    pe.matmul(o, cT[:, 0, c, 32 * i:32 * i + 32], hre[:, jj, :], start=True, stop=False)
                    ins = pe.matmul(o, cT[:, 1, c, 32 * i:32 * i + 32], him[:, jj, :], start=False, stop=True)
                ins.then_inc(y_done, 1)

            project(2, (0, 1))
            inputs(0)
            project(2, (2, 3))
            inputs(1)
            transpose_rows(1)
            project(3, (0, 1))
            outputs(0)
            project(3, (2, 3))
            inputs(2)
            transpose_rows(2)
            pe.wait_ge(g_row, TM * 4)
            pe.wait_ge(t_sb, 3)
            pe.wait_ge(s_bias_out, 32)

            def scores(h):
                if h >= 1:
                    pe.wait_ge(att_exp, h)
                c, r = h // 2, slice(AD * (h % 2), AD * (h % 2) + AD)
                for m, (k0, keys) in enumerate(((0, P), (P, SEQ))):
                    o, rows = ps[:, 4, k0:k0 + keys], slice(m * P, m * P + P)
                    pe.matmul(o, cst[:, C_FLIP:C_FLIP + P], bias[:, h, k0:k0 + keys], start=True, stop=False)
                    ins = pe.matmul(o, qT[r, c, rows], kT[r, c, 0:keys], start=False, stop=True)
                ins.then_inc(att_sc, 1)

            def weighted(h):
                pe.wait_ge(att_exp, h + 1)
                if h >= 1:
                    pe.wait_ge(att_pt_sb, h)
                for b in range(3):
                    ins = pe.transpose(ps[:, 5, b * P:b * P + P], att_p[:, b * P:b * P + P], ident)
                ins.then_inc(att_pt_ps, 1)
                pe.wait_ge(att_pt_sb, h + 1)
                v = slice(h * AD, h * AD + AD)
                pe.matmul(ps[:, 2, v], att_pt[:, 0:P], vrow[:, 0, v], start=True, stop=True)
                pe.matmul(ps[:, 3, v], att_pt[:, P:2 * P], vrow[:, 0, v], start=True, stop=False)
                pe.matmul(ps[:, 3, v], att_pt[:, 2 * P:GW], vrow[:, 1, v], start=False, stop=True).then_inc(att_o, 1)

            def att_slabs(n):
                for k in range(2):
                    slab_product(pe, EV_OUT + 2 * n + k, (n, 2 + n), left_x, 2 * k, k == 0, False)

            scores(0)
            for q in range(1, 5):
                h = 2 * q - 2
                scores(h + 1)
                weighted(h)
                outputs(q)
                inputs(q + 2)
                if h + 2 < AH:
                    scores(h + 2)
                weighted(h + 1)
            for m in range(TM):
                pe.wait_ge(att_rows, m + 1)
                xt_transposes(pe, m, (4 + m,), stage[:, 1])
            outputs(5)
            pe.wait_ge(xt_lo, XT_LN0)
            inputs(7)
            att_slabs(0)
            outputs(6)
            att_slabs(1)
            outputs(7)
            pe.wait_ge(gelu_lo, 4)
            pe.wait_ge(lo_ready, GLU + 2)
            for c in range(4):
                o = ps[:, 6 + c // 2, (c % 2) * SEQ:(c % 2) * SEQ + SEQ]
                cols = slice(c * P, c * P + P)
                for k in range(4):
                    q, kk = (GLU + k // 2) % SPL, k % 2
                    pe.matmul(o, whi[:, q, kk, cols], fh[:, k, :], start=k == 0, stop=False)
                    pe.matmul(o, whi[:, q, kk, cols], fl[:, k, :], start=False, stop=False)
                    ins = pe.matmul(o, wlo[:, q, kk, cols], fh[:, k, :], start=False, stop=k == 3)
            ins.then_inc(slab_used, 2)

            pe.wait_ge(ssm_lo, 4)
            for m in range(TM):
                four_slabs(pe, GLU + 2, m, [(2 * m + n, 4 + 2 * k, False, k == 1) for n in range(2) for k in range(2)],
                           left_x, acc_ready)

            def hidden_slabs(base, ks, i=0):
                for k in ks:
                    slab_product(pe, base + k, (4, 5), left_x, 2 * (k % 4), k % 4 == 0, k % 4 == 3, i)

            def hidden_transposes(layer, i=0, j0=0):
                b = FB * layer + j0
                pe.wait_ge(h_row, TM * (b + 1) + TM * i)
                if layer or j0:
                    pe.wait_ge(ht_lo, 2 * b + 2 * i)
                for c in range(4):
                    for m in range(TM):
                        ins = pe.transpose(ps[:, 6 + c // 2, (c % 2) * SEQ + m * P:(c % 2) * SEQ + m * P + P],
                                           stage[:, 0, m, c * P:c * P + P], ident)
                    if c % 2:
                        ins.then_inc(ht_ps, 1)

            def down(base, layer, i=0, j0=0, first=False, last=False):
                pe.wait_ge(ht_lo, 2 * (FB * layer + j0 + 1) + 2 * i)
                if last:
                    for m in range(TM):
                        four_slabs(pe, base + 8 * FB - 4, m,
                                   [(2 * m + n, 2 * k, False, k == 1) for n in range(2) for k in range(2)],
                                   left_f, acc_ready)
                    return
                for n in range(2):
                    for k in range(2):
                        slab_product(pe, base + 8 * j0 + 8 + 2 * n + k,
                                     (n, 2 + n), left_f, 2 * k, first and k == 0, False, i)

            def first_four(r, at, s0):
                norm_pe(pe, r, at, 0)
                for m in range(TM):
                    pe.wait_ge(xt_lo, at + 2 * m + 2)
                    four_slabs(pe, s0, m, [(4 + m, 2 * k, k == 0, k == 3) for k in range(4)], left_x,
                               halfway=None if m else lambda: norm_pe(pe, r, at, 1))

            def mlp(base, layer):
                first_four(2 * layer, (XT_LN0, XT_LN2)[layer], base)

                def step(i, j0, first):
                    pe.wait_ge(h_relu, TM * (FB * layer + j0 + 1) + TM * i)
                    hidden_slabs(base + 8 * j0 + 4, (0, 1), i)
                    hidden_transposes(layer, i, j0)
                    hidden_slabs(base + 8 * j0 + 4, (2, 3), i)
                    down(base, layer, i, j0, first=first)

                step(0, 0, True)
                with pe.Fori(0, FB - 2) as j:
                    step(j, 1, False)
                hidden_transposes(layer, 0, FB - 1)
                down(base, layer, 0, FB - 1, last=True)

            mlp(MLP_A, 0)

            first_four(1, XT_LN1, OD_IN)
            pe.wait_ge(wb_split, 2)
            for k in range(KC):
                o = ps[0:16, 0, 0:SEQ]
                pe.matmul(o, wbh[:, k, :], xh[:, k, :], start=k == 0, stop=False)
                pe.matmul(o, wbl[:, k, :], xh[:, k, :], start=False, stop=False)
                ins = pe.matmul(o, wbh[:, k, :], xl[:, k, :], start=False, stop=k == KC - 1)
            ins.then_inc(baT_ps, 1)

            def gate_rows():
                pe.wait_ge(baT_sb, 1)
                for m in range(TM):
                    ins = pe.transpose(ps[:, 1, 16 * m:16 * m + 16], baT[:, m * P:m * P + P], ident[0:16, 0:16])
                ins.then_inc(ba_ps, 1)

            def od_project(g, ks):
                b = 4 + 2 * (g % 2)
                if g >= 2 and ks[0] == 0:
                    pe.wait_ge(g1_row, TM * (g - 1))
                for k in ks if g else ():
                    slab_product(pe, OD_IN + 4 * g + k, (b, b + 1), left_x, 2 * k, k == 0, k == 3)

            def od_transposes(g):
                pe.wait_ge(g1_row, TM * (g + 1))
                if g:
                    pe.wait_ge(conv_done, g)
                for c in range(4):
                    for m in range(TM):
                        ins = pe.transpose(ps[:, 2 + c // 2, (c % 2) * SEQ + m * P:(c % 2) * SEQ + m * P + P],
                                           stage[:, g % 2, m, c * P:c * P + P], ident)
                ins.then_inc(t1_ps, 1)

            one = cst[:, C_ONE:C_ONE + 1]

            def lengths(g):
                pe.wait_ge(sq_done, g + 1)
                for c in range(4):
                    for m in range(TM):
                        i = 2 * (4 * g + c) + m
                        ins = pe.matmul(ps[:, 0, i:i + 1], sqT[:, c, m * P:m * P + P], one, start=True, stop=True)
                ins.then_inc(ss_ps, 1)

            up, same = cst[:, C_UP:C_UP + P], cst[:, C_SAME:C_SAME + P]

            def sums_of_g():
                pe.wait_ge(s_cst, 32)
                pe.wait_ge(g_ready, 1)
                for m in range(TM):
                    gr = sm[GR][:, m, :]
                    pe.matmul(ps[:, 1, 32 + 8 * m:40 + 8 * m], up, gr, start=True, stop=True)
                    pe.matmul(ps[:, 1, 48 + 8 * m:56 + 8 * m], same, gr, start=True, stop=True)
                    for c in range(2):
                        n = 2 * m + c
                        ins = pe.matmul(ps[:, 1, 64 + 8 * n:72 + 8 * n], cst[:, C_CH + c * P:C_CH + c * P + P], gr,
                                        start=True, stop=True)
                ins.then_inc(cum_ps, 1)

            for g in range(7):
                od_project(g, (0,))
                if g == 1:
                    gate_rows()
                od_project(g, (1,))
                if g >= 1:
                    od_transposes(g - 1)
                if g == 1:
                    sums_of_g()
                od_project(g, (2, 3))
                if 2 <= g <= 5:
                    lengths(g - 2)

            def kk_products(b):
                m, h0, base = b // 2, 4 * (b % 2), 3 * (b % 2)
                rows = slice(m * P, m * P + P)
                if b == 0:
                    pe.wait_ge(conv_done, 6)
                    pe.wait_ge(norm_in, 1)
                    pe.wait_ge(cum_exp, 3)
                if b == 1:
                    pe.wait_ge(g1_row, TM * 7)
                if b >= 2:
                    pe.wait_ge(nt_ready, b - 1)
                for h in range(4):
                    c = slice(h * P, h * P + P)
                    pe.matmul(ps[:, base, c], sm[GR][:, m, h0 + h:h0 + h + 1].to_broadcast([P, P]), up,
                              start=True, stop=True)
                    pe.matmul(ps[:, base + 1, c], kTd[:, h0 + h, rows], kTd[:, h0 + h, rows], start=True, stop=True)
                    ins = pe.matmul(ps[:, base + 2, c], kTd[:, h0 + h, rows], qTd[:, h0 + h, rows],
                                    start=True, stop=True)
                ins.then_inc(kk_ps, 1)

            def rows_of(src, m, bank):
                for h in range(CH):
                    ins = pe.transpose(ps[:, bank + h // 4, (h % 4) * P:(h % 4) * P + P],
                                       src[:, h, m * P:m * P + P], ident)
                ins.then_inc(rows_ps, 1)

            od_project(7, (0,))
            kk_products(0)
            kk_products(1)
            od_project(7, (1,))
            kk_products(2)
            kk_products(3)
            od_project(7, (2,))
            pe.wait_ge(nt_ready, 4)
            pe.wait_ge(v_silu, 2)
            rows_of(vTd, 0, 0)
            rows_of(kTd, 0, 2)
            pe.wait_ge(rows_sb, 1)
            rows_of(vTd, 1, 0)
            rows_of(kTd, 1, 4)
            od_project(7, (3,))

            def transposed(src, b):
                for h in range(4):
                    ins = pe.transpose(ps[:, 4 + b, h * P:h * P + P], tile4(src, b)[:, h, :], ident)
                ins.then_inc(tt_ps, 1)

            def level_first(lev, b):
                if lev == 1:
                    pe.wait_ge(t_first, b + 1)
                    pe.wait_ge(rows_sb, 4)
                for h in range(4):
                    o = half_bank(b, 0, lev)[:, h]
                    ins = pe.matmul(o, tile4(NT, b)[:, h, :], left(tile4(T, b), lev)[:, h], start=True, stop=True)
                ins.then_inc(nt_ps, 1)

            def level_second(lev, b):
                pe.wait_ge(xx_ready, 4 * lev + b - 3)
                if lev > 1:
                    pe.wait_ge(tt_sb, 4 * lev + b - 7)
                for h in range(4):
                    ins = pe.matmul(ps[:, b, SEQ + h * HP:SEQ + h * HP + HP], tile4(TT, b)[:, h, :], XX[:, b, h, :],
                                    start=True, stop=True)
                ins.then_inc(tx_ps, 1)

            for b in range(4):
                pe.wait_ge(t_init, b + 1)
                if b == 0:
                    pe.wait_ge(rows_sb, 4)
                if b == 2:
                    pe.wait_ge(g1_row, TM * 8)
                transposed(TT, b)
            for b in range(4):
                level_first(1, b)
            for lev in range(1, LEVELS + 1):
                for b in range(4):
                    level_second(lev, b)
                for b in range(4):
                    pe.wait_ge(t_done, 4 * lev + b - 3)
                    if lev > 1:
                        pe.wait_ge(tt_sb, 4 * lev + b - 7)
                    transposed(T, b)
                    if lev < LEVELS:
                        level_first(lev + 1, b)
            def values_inside(n, hh):
                m, rows = n // 2, slice(CK * (n % 2), CK * (n % 2) + CK)
                if n:
                    pe.wait_ge(vnew_done, 2 * n + hh - 1)
                for k in range(4):
                    h = 4 * hh + k
                    ins = pe.matmul(ps[rows, hh, k * P:k * P + P], TT[:, m, h, rows], dv[:, m, h, :],
                                    start=k == 0 or n == 0, stop=n == 0)
                if n == 0:
                    ins.then_inc(v_ps, 1)

            def values_state(n, hh):
                m, rows = n // 2, slice(CK * (n % 2), CK * (n % 2) + CK)
                pe.wait_ge(s_ready, 2 * n + hh - 1)
                for k in range(4):
                    h = 4 * hh + k
                    ins = pe.matmul(ps[rows, hh, k * P:k * P + P], WT[:, m, h, rows], S[n][:, h, :],
                                    start=False, stop=k == 3)
                ins.then_inc(v_ps, 1)

            def query_state(n, hh):
                rows = slice(CK * (n % 2), CK * (n % 2) + CK)
                for h in range(4 * hh, 4 * hh + 4):
                    pe.matmul(ps[rows, 4 + hh, (h % 4) * P:(h % 4) * P + P],
                              qTd[:, h, CK * n:CK * n + CK], S[n][:, h, :], start=True, stop=True)

            def key_values(n, hh):
                m, rows = n // 2, slice(CK * (n % 2), CK * (n % 2) + CK)
                pe.wait_ge(vnew_done, 2 * n + hh + 1)
                for h in range(4 * hh, 4 * hh + 4):
                    ins = pe.matmul(ps[:, 2 + hh, (h % 4) * P:(h % 4) * P + P], kdec[rows, m, h, :],
                                    vnew[rows, m, h, :], start=True, stop=True)
                ins.then_inc(kv_ps, 1)

            def intra_values(m):
                if m:
                    pe.wait_ge(o2_sb, m)
                for h in range(CH):
                    ins = pe.matmul(ps[:, 6 + h // 4, (h % 4) * P:(h % 4) * P + P], intraT[:, m, h, :],
                                    vnew[:, m, h, :], start=True, stop=True)
                ins.then_inc(o2_ps, 1)

            pe.wait_ge(tt_sb, 4 * LEVELS)
            for hh in range(2):
                values_inside(0, hh)
            for b in range(4):
                for h in range(4):
                    ins = pe.matmul(ps[:, 4 + b, h * P:h * P + P], tile4(kw, b)[:, h, :], tile4(TT, b)[:, h, :],
                                    start=True, stop=True)
                ins.then_inc(wt_ps, 1)
            pe.wait_ge(wt_sb, 4)
            for hh in range(2):
                key_values(0, hh)
            for n in range(1, 4):
                for hh in range(2):
                    values_inside(n, hh)
                for hh in range(2):
                    values_state(n, hh)
                if n == 2:
                    pe.wait_ge(o_state, 1)
                for hh in range(2):
                    query_state(n, hh)
                if n < 3:
                    for hh in range(2):
                        key_values(n, hh)
                if n == 3:
                    pe.wait_ge(vnew_done, 8)
                if n % 2:
                    intra_values(n // 2)
            pe.wait_ge(o_rows, 1)
            xt_transposes(pe, 0, (2, 3), gate)
            pe.wait_ge(xt_lo, XT_GDN + 2)

            def out_slabs(n, m):
                four_slabs(pe, OD_OUT + 4 * n, m, [(2 * m + n, 2 * k, k == 0, k == 3) for k in range(4)],
                           left_x, acc_ready)

            out_slabs(0, 0)
            pe.wait_ge(o_rows, TM)
            xt_transposes(pe, 1, (4, 5), gate)
            pe.wait_ge(xt_lo, XT_GDN + 4)
            out_slabs(0, 1)
            out_slabs(1, 0)
            out_slabs(1, 1)
            mlp(MLP_B, 1)



def constant_tile():
    import numpy as np
    c = np.zeros((P, C_W), np.float32)
    i, j = np.arange(P)[:, None], np.arange(P)[None, :]
    same = i // CK == j // CK
    c[:, C_ID:C_ID + P] = i == j
    c[:, C_UP:C_UP + P] = same & (i <= j)
    c[:, C_SAME:C_SAME + P] = same
    c[:, C_NEG:C_NEG + P] = np.where(same & (i <= j), 0.0, NEG)
    c[:, C_PAIR:C_PAIR + P] = np.where((i // 2 == j // 2) & (i < j), -1.0, 0.0)
    for lev in range(1, LEVELS + 1):
        b = 2 ** lev
        left = np.arange(P)[np.arange(P) // b % 2 == 0][None, :]
        c[:, C_LVL + (lev - 1) * HP:C_LVL + lev * HP] = (i // (2 * b) == left // (2 * b)) & (i // b % 2 == 1)
    for n in range(2):
        c[:, C_CH + n * P:C_CH + n * P + P] = i // CK == n
    c[:, C_T:C_T + 16] = np.arange(16)
    c[:, C_T + 16:C_T + 32] = 16 * np.arange(16)
    c[:, C_ONE:C_ONE + 2] = 1.0
    c[:, C_FLIP:C_FLIP + P] = i + j == P - 1
    for n in range(2):
        c[:, C_PAR + n:C_PAR + n + 1] = i // SH % 2 == n
    return c


def bucket_rows():
    import numpy as np
    d = 255 - np.arange(GW)
    n = np.maximum(d, 0)
    exact = BUCKETS // 2
    nf = np.maximum(n, 1).astype(np.float32)
    large = exact + (np.log(nf / np.float32(exact)) / np.float32(math.log(128 / exact)) * (BUCKETS - exact)).astype(np.int32)
    bucket = np.where(n < exact, n, np.minimum(large, BUCKETS - 1))
    h = np.zeros((BUCKETS + 1, GW), np.float32)
    h[np.where(d >= 0, bucket, BUCKETS), np.arange(GW)] = 1.0
    return h


_INS = ['x', 'rel_table', 'ev_w_in', 'ev_w_out', 's5_lambda_re', 's5_lambda_im', 's5_b_re', 's5_b_im',
        's5_c_re', 's5_c_im', 's5_d', 's5_log_dt', 's5_w_glu', 's5_b_glu', 'od_w_in', 'od_conv_w',
        'od_a_log', 'od_dt_bias', 'od_norm_w', 'od_w_out', 'ln_mix_g', 'ln_mix_b', 'mlp_w1', 'mlp_w2',
        'ln_ffn_g', 'ln_ffn_b']
_OUTS = [((1, SEQ, DM), 'float32')]


def kernel(**inputs):
    import numpy as _np
    import concourse.bacc as _bacc
    from concourse import mybir as _mybir
    from concourse.bass_utils import run_bass_kernel_spmd as _run

    nc = _bacc.Bacc("TRN2", target_bir_lowering=False, num_devices=1)
    arrays, args = {}, []
    given = {n: inputs[n] for n in _INS} | {"consts": constant_tile(), "onehot": bucket_rows()}
    for name, a in given.items():
        a = _np.ascontiguousarray(a)
        arrays[f"in_{name}_dram"] = a
        args.append(nc.dram_tensor(f"in_{name}_dram", a.shape, _mybir.dt.from_np(a.dtype), kind="ExternalInput").ap())
    for i, (shape, dtype) in enumerate(_OUTS):
        dt = _mybir.dt.from_np(_np.dtype(dtype))
        args.append(nc.dram_tensor(f"out_{i}_dram", shape, dt, kind="ExternalOutput").ap())
    build(nc, *args)
    r = _run(nc, [arrays], core_ids=[0])
    return r.results[0]["out_0_dram"]
```
